# Optimizing a Trainium2 kernel written in Bass

```python
import math
import jax, jax.numpy as jnp
from jax import lax
import numpy as np

D_MODEL = 2048
BATCH = 1
SEQ = 256
DEPTH = 2

DIFF_HEADS = 8
DIFF_QK_DIM = 64
DIFF_V_DIM = 128
DIFF_WIDTH = DIFF_HEADS * DIFF_V_DIM
MLA_HEADS = 8
MLA_Q_RANK = 512
MLA_KV_RANK = 512
MLA_NOPE_DIM = 128
MLA_ROPE_DIM = 64
MLA_V_DIM = 128
MLA_WIDTH = MLA_HEADS * MLA_V_DIM
MIX_WIDTH = DIFF_WIDTH + MLA_WIDTH
IN_SIZES = (
    DIFF_HEADS * 2 * DIFF_QK_DIM,
    DIFF_HEADS * 2 * DIFF_QK_DIM,
    DIFF_WIDTH,
    DIFF_WIDTH,
    MLA_Q_RANK,
    MLA_KV_RANK,
    MLA_ROPE_DIM,
    MLA_WIDTH,
)
IN_WIDTH = sum(IN_SIZES)
ROPE_THETA = 10000.0
NUM_BUCKETS = 32
MAX_DISTANCE = 128
BLOCK_Q = 128
EPS = 1e-6
NEG_INF = -1e30


def _rms_norm(x, g):
    xf = x.astype(jnp.float32)
    y = xf * lax.rsqrt(jnp.mean(xf * xf, axis=-1, keepdims=True) + EPS)
    return (y * g.astype(jnp.float32)).astype(x.dtype)

def _rope_tables(seq):
    pos = jnp.arange(seq, dtype=jnp.float32)
    inv = 1.0 / (ROPE_THETA ** (jnp.arange(0, MLA_ROPE_DIM, 2, dtype=jnp.float32) / MLA_ROPE_DIM))
    ang = pos[:, None] * inv[None, :]
    ang = jnp.concatenate([ang, ang], axis=-1)
    return jnp.cos(ang), jnp.sin(ang)

def _apply_rope(x, cos, sin):
    half = x.shape[-1] // 2
    x1, x2 = x[..., :half], x[..., half:]
    rot = jnp.concatenate([-x2, x1], axis=-1)
    return x * cos.astype(x.dtype) + rot * sin.astype(x.dtype)

def _t5_bucket(dist):
    n = jnp.maximum(dist, 0)
    max_exact = NUM_BUCKETS // 2
    nf = jnp.maximum(n, 1).astype(jnp.float32)
    large = max_exact + (jnp.log(nf / max_exact) / math.log(MAX_DISTANCE / max_exact)
                         * (NUM_BUCKETS - max_exact)).astype(jnp.int32)
    large = jnp.minimum(large, NUM_BUCKETS - 1)
    return jnp.where(n < max_exact, n, large)

def _block_sweep(one_block, seq):
    starts = jnp.arange(seq // BLOCK_Q, dtype=jnp.int32) * BLOCK_Q
    out = lax.map(one_block, starts)
    out = jnp.moveaxis(out, 0, 1)
    b, nb, q, h, dv = out.shape
    return out.reshape(b, nb * q, h, dv)

def _diff_attention(q, k, v, lam, bias_table):
    seq = q.shape[1]
    kpos = jnp.arange(seq, dtype=jnp.int32)
    scale = DIFF_QK_DIM ** -0.5
    table = bias_table.astype(jnp.float32)

    def one_block(start):
        qb = lax.dynamic_slice_in_dim(q, start, BLOCK_Q, axis=1)
        s = jnp.einsum('bqhmd,bkhmd->bmhqk', qb, k).astype(jnp.float32) * scale
        dist = (start + jnp.arange(BLOCK_Q, dtype=jnp.int32))[:, None] - kpos[None, :]
        bias = jnp.transpose(table[_t5_bucket(dist)], (2, 0, 1))
        s = jnp.where((dist >= 0)[None, None, None], s + bias[None, None], NEG_INF)
        p = jax.nn.softmax(s, axis=-1)
        w = p[:, 0] - lam * p[:, 1]
        return jnp.einsum('bhqk,bkhd->bqhd', w.astype(v.dtype), v)

    return _block_sweep(one_block, seq)

def _mla_attention(q_nope, q_rope, k_nope, k_rope, v):
    seq = q_nope.shape[1]
    kpos = jnp.arange(seq, dtype=jnp.int32)
    scale = (MLA_NOPE_DIM + MLA_ROPE_DIM) ** -0.5

    def one_block(start):
        qn = lax.dynamic_slice_in_dim(q_nope, start, BLOCK_Q, axis=1)
        qr = lax.dynamic_slice_in_dim(q_rope, start, BLOCK_Q, axis=1)
        s = (jnp.einsum('bqhd,bkhd->bhqk', qn, k_nope)
             + jnp.einsum('bqhr,bkr->bhqk', qr, k_rope)).astype(jnp.float32) * scale
        dist = (start + jnp.arange(BLOCK_Q, dtype=jnp.int32))[:, None] - kpos[None, :]
        s = jnp.where((dist >= 0)[None, None], s, NEG_INF)
        p = jax.nn.softmax(s, axis=-1)
        return jnp.einsum('bhqk,bkhd->bqhd', p.astype(v.dtype), v)

    return _block_sweep(one_block, seq)

def first_inputs(seed: int = 0) -> dict:
    key = jax.random.key(seed)
    ks = jax.random.split(key, 12)
    f32 = jnp.float32
    x = jax.random.normal(ks[0], (BATCH, SEQ, D_MODEL), f32)
    norm_g = 1.0 + 0.02 * jax.random.normal(ks[1], (DEPTH, D_MODEL), f32)
    w_in = jax.random.normal(ks[2], (DEPTH, D_MODEL, IN_WIDTH), f32) * D_MODEL ** -0.5
    diff_lambda = 0.1 * jax.random.normal(ks[3], (DEPTH, 4, DIFF_QK_DIM), f32)
    diff_subln_g = 1.0 + 0.02 * jax.random.normal(ks[4], (DEPTH, DIFF_V_DIM), f32)
    rel_bias_table = 0.2 * jax.random.normal(ks[5], (NUM_BUCKETS, DIFF_HEADS), f32)
    mla_q_norm_g = 1.0 + 0.02 * jax.random.normal(ks[6], (DEPTH, MLA_Q_RANK), f32)
    w_uq = jax.random.normal(ks[7], (DEPTH, MLA_Q_RANK, MLA_HEADS * (MLA_NOPE_DIM + MLA_ROPE_DIM)), f32) * MLA_Q_RANK ** -0.5
    mla_kv_norm_g = 1.0 + 0.02 * jax.random.normal(ks[8], (DEPTH, MLA_KV_RANK), f32)
    w_ukv = jax.random.normal(ks[9], (DEPTH, MLA_KV_RANK, MLA_HEADS * (MLA_NOPE_DIM + MLA_V_DIM)), f32) * MLA_KV_RANK ** -0.5
    w_out = jax.random.normal(ks[10], (DEPTH, MIX_WIDTH, D_MODEL), f32) * MIX_WIDTH ** -0.5
    final_norm_g = 1.0 + 0.02 * jax.random.normal(ks[11], (D_MODEL,), f32)
    return {"x": x, "norm_g": norm_g, "w_in": w_in, "diff_lambda": diff_lambda,
            "diff_subln_g": diff_subln_g, "rel_bias_table": rel_bias_table,
            "mla_q_norm_g": mla_q_norm_g, "w_uq": w_uq, "mla_kv_norm_g": mla_kv_norm_g,
            "w_ukv": w_ukv, "w_out": w_out, "final_norm_g": final_norm_g}

def first_block(x, norm_g, w_in, diff_lambda, diff_subln_g, rel_bias_table,
              mla_q_norm_g, w_uq, mla_kv_norm_g, w_ukv, w_out, final_norm_g):
    b, seq, _ = x.shape
    cos, sin = _rope_tables(seq)
    split_points = [int(v) for v in np.cumsum(IN_SIZES)[:-1]]
    for l in range(DEPTH):
        h = _rms_norm(x, norm_g[l])
        proj = jnp.einsum('bsd,de->bse', h, w_in[l])
        q_a, k_a, v_a, z_a, c_q, c_kv, k_r, z_b = jnp.split(proj, split_points, axis=-1)

        lambda_init = 0.8 - 0.6 * math.exp(-0.3 * l)
        lp = diff_lambda[l].astype(jnp.float32)
        lam = (jnp.exp(jnp.sum(lp[0] * lp[1])) - jnp.exp(jnp.sum(lp[2] * lp[3])) + lambda_init)
        qa = q_a.reshape(b, seq, DIFF_HEADS, 2, DIFF_QK_DIM)
        ka = k_a.reshape(b, seq, DIFF_HEADS, 2, DIFF_QK_DIM)
        va = v_a.reshape(b, seq, DIFF_HEADS, DIFF_V_DIM)
        o_a = _diff_attention(qa, ka, va, lam, rel_bias_table)
        o_a = _rms_norm(o_a, diff_subln_g[l]) * (1.0 - lambda_init)
        o_a = o_a.reshape(b, seq, DIFF_WIDTH) * jax.nn.silu(z_a)

        q_b = jnp.einsum('bsr,re->bse', _rms_norm(c_q, mla_q_norm_g[l]), w_uq[l])
        q_b = q_b.reshape(b, seq, MLA_HEADS, MLA_NOPE_DIM + MLA_ROPE_DIM)
        q_nope, q_rope = q_b[..., :MLA_NOPE_DIM], q_b[..., MLA_NOPE_DIM:]
        q_rope = _apply_rope(q_rope, cos[:, None, :], sin[:, None, :])
        kv = jnp.einsum('bsr,re->bse', _rms_norm(c_kv, mla_kv_norm_g[l]), w_ukv[l])
        kv = kv.reshape(b, seq, MLA_HEADS, MLA_NOPE_DIM + MLA_V_DIM)
        k_nope, v_b = kv[..., :MLA_NOPE_DIM], kv[..., MLA_NOPE_DIM:]
        k_rope = _apply_rope(k_r, cos, sin)
        o_b = _mla_attention(q_nope, q_rope, k_nope, k_rope, v_b)
        o_b = o_b.reshape(b, seq, MLA_WIDTH) * jax.nn.silu(z_b)

        mixed = jnp.concatenate([o_a, o_b], axis=-1)
        x = x + jnp.einsum('bse,ed->bsd', mixed, w_out[l])
    return _rms_norm(x, final_norm_g)


DEPTH_2 = 1

SSM_HEAD_DIM = 64
SSM_HEADS = D_MODEL // SSM_HEAD_DIM
D_SSM = SSM_HEADS * SSM_HEAD_DIM
SSM_GROUPS = 8
HEADS_PER_GROUP = SSM_HEADS // SSM_GROUPS
D_STATE = 128
CONV_WIDTH = 4
SSD_CHUNK = 128
D_XBC = D_SSM + 2 * SSM_GROUPS * D_STATE

ATT_HEAD_DIM = 128
ATT_HEADS = D_MODEL // ATT_HEAD_DIM
D_ATT = ATT_HEADS * ATT_HEAD_DIM
DILATION_PAIRS = ((128, 1), (512, 4), (2048, 16))
ATT_BLOCK = 128

D_MIX = D_SSM + D_ATT
IN_SPLITS = (D_SSM,
             D_SSM + D_XBC,
             D_SSM + D_XBC + SSM_HEADS,
             D_SSM + D_XBC + SSM_HEADS + D_ATT,
             D_SSM + D_XBC + SSM_HEADS + 2 * D_ATT)
D_IN_PROJ = D_SSM + D_XBC + SSM_HEADS + 3 * D_ATT
D_FF = 4 * D_MODEL


def rmsnorm(x, w):
    xf = x.astype(jnp.float32)
    xf = xf * lax.rsqrt(jnp.mean(xf * xf, axis=-1, keepdims=True) + EPS)
    return (xf * w.astype(jnp.float32)).astype(x.dtype)

def causal_depthwise_conv(u, w, b):
    out = lax.conv_general_dilated(
        u, w[:, None, :].astype(u.dtype), window_strides=(1,),
        padding=[(CONV_WIDTH - 1, 0)],
        dimension_numbers=('NWC', 'WIO', 'NWC'),
        feature_group_count=u.shape[-1])
    return out + b.astype(u.dtype)

def ssd_chunked(xh, dt, a, bm, cm):
    b_, s_ = xh.shape[:2]
    nc = s_ // SSD_CHUNK

    def chunk(t):
        return t.reshape((b_, nc, SSD_CHUNK) + t.shape[2:])

    xc, dtc, bc, cc = chunk(xh), chunk(dt), chunk(bm), chunk(cm)
    a_cs = jnp.cumsum(dtc * a, axis=2).transpose(0, 1, 3, 4, 2)
    causal = jnp.tril(jnp.ones((SSD_CHUNK, SSD_CHUNK), dtype=bool))
    decay_in = jnp.exp(jnp.where(causal, a_cs[..., :, None] - a_cs[..., None, :], -jnp.inf))
    cb = jnp.einsum('bcign,bcjgn->bcgij', cc, bc)
    xdt = xc * dtc[..., None]
    y_diag = jnp.einsum('bcgrij,bcjgrp->bcigrp', cb[:, :, :, None] * decay_in, xdt)

    decay_to_end = jnp.exp(a_cs[..., -1:] - a_cs)
    states = jnp.einsum('bcjgn,bcgrj,bcjgrp->bcgrpn', bc, decay_to_end, xdt)
    chunk_decay = jnp.exp(a_cs[..., -1])

    def step(h, inp):
        st, dec = inp
        return h * dec[..., None, None] + st, h

    h0 = jnp.zeros(states.shape[:1] + states.shape[2:], jnp.float32)
    _, prev = lax.scan(step, h0, (jnp.swapaxes(states, 0, 1), jnp.swapaxes(chunk_decay, 0, 1)))
    prev = jnp.swapaxes(prev, 0, 1)
    y_off = jnp.einsum('bcign,bcgrpn,bcgri->bcigrp', cc, prev, jnp.exp(a_cs))
    return (y_diag + y_off).reshape(xh.shape)

def dilated_window_attention(q, k, v, window, dilation):
    b_, s_, h_, d_ = q.shape
    sd = s_ // dilation
    reach = window // dilation
    nb = -(-sd // ATT_BLOCK)
    lp = nb * ATT_BLOCK
    bd = b_ * dilation

    def decimate(t):
        t = t.reshape(b_, sd, dilation, h_, d_).transpose(0, 2, 1, 3, 4)
        t = t.reshape(bd, sd, h_, d_)
        return jnp.pad(t, ((0, 0), (0, lp - sd), (0, 0), (0, 0)))

    def with_prev(t):
        t = jnp.pad(t, ((0, 0), (ATT_BLOCK, 0), (0, 0), (0, 0)))
        t = t.reshape(bd, nb + 1, ATT_BLOCK, h_, d_)
        return jnp.concatenate([t[:, :-1], t[:, 1:]], axis=2)

    qb = decimate(q).reshape(bd, nb, ATT_BLOCK, h_, d_)
    kb = with_prev(decimate(k))
    vb = with_prev(decimate(v))
    s = jnp.einsum('bnqhd,bnkhd->bnhqk', qb, kb)
    qi = jnp.arange(ATT_BLOCK)[:, None]
    kj = jnp.arange(2 * ATT_BLOCK)[None, :]
    dist = ATT_BLOCK + qi - kj
    key_pos = (jnp.arange(nb)[:, None, None] - 1) * ATT_BLOCK + kj[None]
    mask = (dist >= 0) & (dist <= reach) & (key_pos >= 0)
    s = jnp.where(mask[None, :, None], s, -jnp.inf)
    m = jnp.max(s, axis=-1, keepdims=True)
    p = jnp.exp(s - m)
    den = jnp.sum(p, axis=-1)
    o = jnp.einsum('bnhqk,bnkhd->bnqhd', p, vb) / jnp.swapaxes(den, 2, 3)[..., None]
    lse = jnp.swapaxes(m[..., 0] + jnp.log(den), 2, 3)

    def undecimate(t):
        t = t.reshape((bd, lp) + t.shape[3:])[:, :sd]
        t = t.reshape((b_, dilation, sd) + t.shape[2:])
        return jnp.moveaxis(t, 1, 2).reshape((b_, s_) + t.shape[3:])

    return undecimate(o), undecimate(lse)

def hybrid_mixer(u, w_in, conv_w, conv_b, dt_bias, a_log, d_skip, ssm_norm_w, w_out):
    b_, s_, _ = u.shape
    f32 = jnp.float32
    proj = jnp.einsum('bsd,de->bse', u, w_in)
    z, xbc, dt_raw, q, k, v = jnp.split(proj, IN_SPLITS, axis=-1)

    xbc = jax.nn.silu(causal_depthwise_conv(xbc, conv_w, conv_b))
    xs, bm, cm = jnp.split(xbc, (D_SSM, D_SSM + SSM_GROUPS * D_STATE), axis=-1)
    xh = xs.astype(f32).reshape(b_, s_, SSM_GROUPS, HEADS_PER_GROUP, SSM_HEAD_DIM)
    dt = jax.nn.softplus(dt_raw.astype(f32) + dt_bias.astype(f32))
    dt = dt.reshape(b_, s_, SSM_GROUPS, HEADS_PER_GROUP)
    a = -jnp.exp(a_log.astype(f32)).reshape(SSM_GROUPS, HEADS_PER_GROUP)
    bm = bm.astype(f32).reshape(b_, s_, SSM_GROUPS, D_STATE)
    cm = cm.astype(f32).reshape(b_, s_, SSM_GROUPS, D_STATE)
    y = ssd_chunked(xh, dt, a, bm, cm)
    y = y + d_skip.astype(f32).reshape(SSM_GROUPS, HEADS_PER_GROUP)[:, :, None] * xh
    yg = y.reshape(b_, s_, SSM_GROUPS, -1) * jax.nn.silu(z.astype(f32)).reshape(b_, s_, SSM_GROUPS, -1)
    yg = yg * lax.rsqrt(jnp.mean(yg * yg, axis=-1, keepdims=True) + EPS)
    y_ssm = (yg.reshape(b_, s_, D_SSM) * ssm_norm_w.astype(f32)).astype(u.dtype)

    qh = q.astype(f32).reshape(b_, s_, ATT_HEADS, ATT_HEAD_DIM) * (ATT_HEAD_DIM ** -0.5)
    kh = k.astype(f32).reshape(b_, s_, ATT_HEADS, ATT_HEAD_DIM)
    vh = v.astype(f32).reshape(b_, s_, ATT_HEADS, ATT_HEAD_DIM)
    outs, lses = [], []
    for window, dilation in DILATION_PAIRS:
        o, l = dilated_window_attention(qh, kh, vh, window, dilation)
        outs.append(o)
        lses.append(l)
    wts = jax.nn.softmax(jnp.stack(lses, axis=0), axis=0)
    y_att = jnp.einsum('ibsh,ibshd->bshd', wts, jnp.stack(outs, axis=0))
    y_att = y_att.reshape(b_, s_, D_ATT).astype(u.dtype)

    y_mix = jnp.concatenate([y_ssm, y_att], axis=-1)
    return jnp.einsum('bse,ed->bsd', y_mix, w_out)

def squared_relu_mlp(u, w_up, w_down):
    hdn = jax.nn.relu(jnp.einsum('bsd,df->bsf', u, w_up))
    return jnp.einsum('bsf,fd->bsd', hdn * hdn, w_down)

def second_inputs(seed: int = 0) -> dict:
    key = jax.random.key(seed)
    ks = jax.random.split(key, 16)
    L = DEPTH_2

    def gain(k, n):
        return 1.0 + 0.1 * jax.random.normal(k, (L, n), jnp.float32)

    dt0 = jnp.exp(jax.random.uniform(ks[5], (L, SSM_HEADS), jnp.float32,
                                     math.log(1e-3), math.log(1e-1)))
    dt_bias = dt0 + jnp.log(-jnp.expm1(-dt0))
    return {
        "x": jax.random.normal(ks[0], (BATCH, SEQ, D_MODEL), jnp.float32),
        "norm_mix_pre": gain(ks[1], D_MODEL),
        "w_in": jax.random.normal(ks[2], (L, D_MODEL, D_IN_PROJ), jnp.float32) * D_MODEL ** -0.5,
        "conv_w": jax.random.normal(ks[3], (L, CONV_WIDTH, D_XBC), jnp.float32) * CONV_WIDTH ** -0.5,
        "conv_b": 0.01 * jax.random.normal(ks[4], (L, D_XBC), jnp.float32),
        "dt_bias": dt_bias,
        "a_log": jnp.log(jax.random.uniform(ks[6], (L, SSM_HEADS), jnp.float32, 1.0, 16.0)),
        "d_skip": gain(ks[7], SSM_HEADS),
        "ssm_norm_w": gain(ks[8], D_SSM),
        "w_out": jax.random.normal(ks[9], (L, D_MIX, D_MODEL), jnp.float32) * D_MIX ** -0.5,
        "norm_mix_post": gain(ks[10], D_MODEL),
        "norm_mlp_pre": gain(ks[11], D_MODEL),
        "w_up": jax.random.normal(ks[12], (L, D_MODEL, D_FF), jnp.float32) * D_MODEL ** -0.5,
        "w_down": jax.random.normal(ks[13], (L, D_FF, D_MODEL), jnp.float32) * D_FF ** -0.5,
        "norm_mlp_post": gain(ks[14], D_MODEL),
    }

def second_block(x, norm_mix_pre, w_in, conv_w, conv_b, dt_bias, a_log, d_skip, ssm_norm_w,
              w_out, norm_mix_post, norm_mlp_pre, w_up, w_down, norm_mlp_post):
    h = x
    for i in range(DEPTH_2):
        mix = hybrid_mixer(rmsnorm(h, norm_mix_pre[i]), w_in[i], conv_w[i], conv_b[i],
                           dt_bias[i], a_log[i], d_skip[i], ssm_norm_w[i], w_out[i])
        h = h + rmsnorm(mix, norm_mix_post[i])
        ff = squared_relu_mlp(rmsnorm(h, norm_mlp_pre[i]), w_up[i], w_down[i])
        h = h + rmsnorm(ff, norm_mlp_post[i])
    return h


def setup_inputs(seed=0):
    out = dict(first_inputs(seed))
    for name, value in second_inputs(seed + 1).items():
        if name != "x":
            out[name + "_2"] = value
    return out


def reference(
    x, norm_g, w_in, diff_lambda, diff_subln_g, rel_bias_table, mla_q_norm_g, w_uq,
    mla_kv_norm_g, w_ukv, w_out, final_norm_g, norm_mix_pre_2, w_in_2, conv_w_2, conv_b_2,
    dt_bias_2, a_log_2, d_skip_2, ssm_norm_w_2, w_out_2, norm_mix_post_2, norm_mlp_pre_2,
    w_up_2, w_down_2, norm_mlp_post_2,
):
    x = first_block(
        x, norm_g, w_in, diff_lambda, diff_subln_g, rel_bias_table, mla_q_norm_g, w_uq,
        mla_kv_norm_g, w_ukv, w_out, final_norm_g,
    )
    return second_block(
        x, norm_mix_pre_2, w_in_2, conv_w_2, conv_b_2, dt_bias_2, a_log_2, d_skip_2,
        ssm_norm_w_2, w_out_2, norm_mix_post_2, norm_mlp_pre_2, w_up_2, w_down_2,
        norm_mlp_post_2,
    )


_drawn_inputs = setup_inputs


def setup_inputs(seed=0):
    import zlib

    import numpy as np

    out = dict(_drawn_inputs(seed))
    spreads = {}
    factors = {'diff_subln_g': 5.012, 'mla_q_norm_g': 8.0, 'mla_kv_norm_g': 8.0, 'conv_b_2': 5.491}
    for name, (base, spread) in spreads.items():
        noise = np.random.default_rng([zlib.crc32(name.encode()), seed]).standard_normal(out[name].shape)
        drawn = base * np.exp(spread * noise) if base else spread * noise
        out[name] = __import__('jax').numpy.asarray(drawn.astype(out[name].dtype))
    for name, factor in factors.items():
        out[name] = (out[name] * factor).astype(out[name].dtype)
    return out
```

```python
import math
from contextlib import ExitStack, contextmanager

import concourse.bass as bass
from concourse import mybir

F32 = mybir.dt.float32
F32R = mybir.dt.float32r
ALU = mybir.AluOpType
ACT = mybir.ActivationFunctionType
ET = mybir.EngineType
AX = mybir.AxisListType

P = 128
D = 2048
S = 256
T = S // P
DEPTH = 2
UNIT = 512
KC = 2
CHUNK = KC * UNIT
RING = 4
KT = D // P
UC = KT // KC
EPS = 1e-6
NEG = -1e30
CREDIT = 512

DH, DQK, DV = 8, 64, 128
MH, NOPE, ROPE, MV = 8, 128, 64, 128
QR = KVR = 512
W_IN = 6208
SH, SG, HPG, SN = 32, 8, 4, 128
HD = 64
AH, AD = 16, 128
W_IN2 = 12320
XBC = 4096
FF = 8192
LAYER_CHUNKS = 12 * UC + 2 + 7 * 2 + 4 * UC

C_G, C_QG, C_KVG, C_SUB, C_LAM, C_INIT = 0, 16, 20, 24, 152, 408
C_N = 410
B_PRE, B_MLP, B_SSM, B_CW, B_CB, B_DTB, B_AL, B_DS = 0, 16, 32, 48, 176, 208, 240, 272
B_N = 304


class Mark:

    def __init__(self, sem, n, frames):
        self.sem, self.n, self.frames = sem, n, frames


class Marks:

    def __init__(self, nc, plan):
        self.nc, self.plan, self.stack = nc, plan, []
        self.count, self.named = {}, {}
        self.eng = {"pe": nc.tensor, "act": nc.scalar, "dve": nc.vector, "pool": nc.gpsimd,
                    "sp": nc.sync}
        self.handle = {}

    def add(self, name, handle, start=0):
        self.handle[name], self.count[name] = handle, start

    def stride(self, frame, sem):
        return self.plan.get((frame, sem), 0)

    @contextmanager
    def loop(self, name, n, carry=()):
        for eng, names in carry:
            for m in names:
                if m in self.named:
                    self.wait(eng, self.named[m])
        start = dict(self.count)
        with self.nc.Fori(0, n, engines=(ET.PE, ET.Activation, ET.DVE, ET.Pool)) as i:
            frame = {"name": name, "var": i, "n": n, "live": True, "marks": {}}
            self.stack.append(frame)
            yield i
            self.stack.pop()
            frame["live"] = False
        for s in self.count:
            self.plan[(name, s)] = self.count[s] - start[s]
            self.count[s] = start[s] + n * (self.count[s] - start[s])
        for k, m in frame["marks"].items():
            self.plan[(name, "last", k)] = (m.sem, m.n)

    def done(self, ins, sem, name=None, by=1):
        ins.then_inc(self.handle[sem], by)
        self.count[sem] += by
        return self.keep(name, Mark(sem, self.count[sem], list(self.stack)))

    def keep(self, name, m):
        if name:
            self.named[name] = m
            for f in self.stack:
                f["marks"][name] = m
        return m

    def value(self, sem, n, frames, back=None):
        v = n
        for f in frames:
            st = self.stride(f["name"], sem)
            if f["live"]:
                k = f["var"]
                v = v + (k * st if st else 0)
                if f is back:
                    assert not self.plan.get("real") or n - st > 0, (sem, n, st)
                    v = v - st
            else:
                v = v + (f["n"] - 1) * st
        return v

    def wait_value(self, eng, sem, v, alone=True):
        self.eng[eng].wait_ge(self.handle[sem], v)
        if alone and not isinstance(v, int):
            self.eng[eng].sem_inc(self.handle["holder_" + eng])

    def wait(self, eng, m):
        if m is not None:
            self.wait_value(eng, m.sem, self.value(m.sem, m.n, m.frames))

    def wait_last(self, eng, name):
        if not self.stack:
            return self.wait(eng, self.named.get(name))
        f = self.stack[-1]
        if name in f["marks"]:
            return self.wait(eng, f["marks"][name])
        last = self.plan.get((f["name"], "last", name))
        if last is None:
            return self.wait(eng, self.named.get(name))
        sem, n = last
        self.wait_value(eng, sem, self.value(sem, n, list(self.stack), back=f))


def build(nc, plan, x, layer_c, w_in, w_uq, w_ukv, w_out, rel_table, block_c, rows_c, w_in_2,
          w_out_2, w_up, w_down, c_ident, c_tri, c_mask, c_bucket, c_rope, out):
    with ExitStack() as ctx:
        def sb(name, shape, dt=F32):
            return ctx.enter_context(nc.sbuf_tensor(name, shape, dt))

        def sem(name):
            return ctx.enter_context(nc.semaphore(name))

        M = Marks(nc, plan)
        pe, act, dve, pool, sp = nc.tensor, nc.scalar, nc.vector, nc.gpsimd, nc.sync
        wait, done, last, keep = M.wait, M.done, M.wait_last, M.keep

        raw = sb("raw", [P, RING, CHUNK])
        w_hi = sb("w_hi", [P, RING, CHUNK], F32R)
        w_lo = sb("w_lo", [P, RING, CHUNK], F32R)
        a_hi = sb("a_hi", [P, KT, S], F32R)
        a_lo = sb("a_lo", [P, KT, S], F32R)
        HT = 8
        hid_hi = sb("hid_hi", [P, HT, S], F32R)
        hid_lo = sb("hid_lo", [P, HT, S], F32R)
        xres = sb("xres", [P, T, D])
        ident = sb("ident", [P, P])
        tri = sb("tri", [P, P])
        ones = sb("ones", [P, P])
        masks = sb("masks", [P, 2, S])
        cvals = sb("cvals", [P, 2])
        lc = sb("lc", [P, C_N])
        bc = sb("bc", [P, B_N])
        ARENA = 21 * 1024
        arena = sb("arena", [P, ARENA])
        stat = sb("stat", [P, 64])

        def cut(at, *shape):
            n = 1
            for v in shape:
                n *= v
            assert at + n <= ARENA, (at, n)
            ap = arena[:, at:at + n]
            if len(shape) == 2:
                return ap.rearrange("p (a b) -> p a b", b=shape[1])
            if len(shape) == 3:
                return ap.rearrange("p (a b c) -> p a b c", b=shape[1], c=shape[2])
            return ap

        pg = ctx.enter_context(nc.psum_tensor("pg", [P, 2, 2, 512], F32))
        pa = ctx.enter_context(nc.psum_tensor("pa", [P, 4, 512], F32))
        bias_dram = nc.dram_tensor("bias_scratch", (P, DH, 512), F32, kind="Internal").ap()

        for e in ("pe", "act", "dve", "pool"):
            M.add(e, sem(f"progress_{e}"), CREDIT)
            M.eng[e].sem_inc(M.handle[e], CREDIT)
        for e in ("pe", "act", "dve", "pool", "sp"):
            M.handle["holder_" + e] = sem(f"holder_{e}")
        landed = [sem(f"landed{s}") for s in range(RING)]
        M.add("rounded", sem("rounded"))
        M.add("split", sem("split"), RING)
        dve.sem_inc(M.handle["split"], RING)
        M.add("used", sem("used"))
        M.count["unit"] = 0
        M.add("out_a", sem("out_a"), 2)
        M.add("out_v", sem("out_v"), 2)
        act.sem_inc(M.handle["out_a"], 2)
        dve.sem_inc(M.handle["out_v"], 2)
        for n in ("ld_const", "ld_layer", "ld_bias"):
            M.add(n, sem(n))
        stored = sem("stored")

        def here(name):
            return M.value(name, M.count[name], M.stack)

        def stream():
            c = [0]

            def load(src, n, k, base=None):
                s = c[0] % RING
                num = c[0] if base is None else base + c[0]
                M.wait_value("sp", "split", num + 1)
                dst = raw[:, s, 0:k * n].rearrange("p (k n) -> p k n", k=k)
                sp.dma_start(dst, src.rearrange("(k p) n -> p k n", p=P)).then_inc(landed[s], 32)
                c[0] += 1

            def units(w, col, n, row=0, base=None):
                c0 = c[0]
                with sp.Fori(0, n) as u:
                    off = u * (UC * 1) if base is None else base + u * UC
                    for j in range(UC):
                        load(w[bass.ds(row + j * KC * P, KC * P), bass.ds(col + u * UNIT, UNIT)],
                             UNIT, KC, off)
                assert (c[0] - c0) % RING == 0
                c[0] = c0 + n * UC

            with sp.Fori(0, DEPTH) as l:
                lb = l * LAYER_CHUNKS
                win = w_in[bass.ds(l * D, D), :]
                units(win, 0, 10, base=lb)
                units(win, W_IN - MH * MV, 2, base=lb)
                for j in range(2):
                    load(win[j * D // 2:(j + 1) * D // 2, W_IN - MH * MV - ROPE:W_IN - MH * MV],
                         ROPE, KT // 2, lb)
                uq = w_uq[bass.ds(l * QR, QR), :].rearrange("k (h c) -> k h c", h=MH)
                ukv = w_ukv[bass.ds(l * KVR, KVR), :].rearrange("k (h c) -> k h c", h=MH)

                def low_rank(w, c0, cn, h0, hn):
                    for j in range(2):
                        s = c[0] % RING
                        M.wait_value("sp", "split", lb + c[0] + 1)
                        for k in range(KC):
                            dst = raw[:, s, k * UNIT:(k + 1) * UNIT].rearrange("p (h c) -> p h c", h=hn)
                            r0 = (j * KC + k) * P
                            sp.dma_start(dst, w[r0:r0 + P, h0:h0 + hn, c0:c0 + cn]).then_inc(
                                landed[s], 16)
                        c[0] += 1

                for h0 in (0, 4):
                    low_rank(uq, 0, NOPE, h0, 4)
                for h0 in (0, 4):
                    low_rank(ukv, 0, NOPE, h0, 4)
                low_rank(uq, NOPE, ROPE, 0, 8)
                for h0 in (0, 4):
                    low_rank(ukv, NOPE, MV, h0, 4)
                units(w_out[bass.ds(l * D, D), :], 0, 4, base=lb)
                assert c[0] == LAYER_CHUNKS, c[0]
            c[0] = DEPTH * LAYER_CHUNKS
            base = [c[0]]

            def units2(w, col, n, row=0):
                with sp.Fori(0, n) as u:
                    for j in range(UC):
                        s = (base[0] + j) % RING
                        M.wait_value("sp", "split", u * UC + (base[0] + j + 1))
                        dst = raw[:, s, :].rearrange("p (k n) -> p k n", k=KC)
                        src = w[row + j * KC * P:row + (j + 1) * KC * P, bass.ds(u * UNIT + col, UNIT)]
                        sp.dma_start(dst, src.rearrange("(k p) n -> p k n", p=P)).then_inc(landed[s], 32)
                base[0] += n * UC

            units2(w_in_2, D, 8)
            units2(w_in_2, 0, 4)
            c[0] = base[0]
            load(w_in_2[:, D + XBC:D + XBC + SH], SH, KT)
            base[0] = c[0]
            units2(w_in_2, D + XBC + SH, 12)
            units2(w_out_2, 0, 4)
            units2(w_out_2, 0, 4, row=D)
            hc = HT // KC
            with sp.Fori(0, FF // (HT * P)) as q:
                for uu in range(2):
                    for j in range(UC):
                        s = (base[0] + j) % RING
                        M.wait_value("sp", "split", q * (4 * UC) + (base[0] + j + 1))
                        dst = raw[:, s, :].rearrange("p (k n) -> p k n", k=KC)
                        src = w_up[j * KC * P:(j + 1) * KC * P, bass.ds(q * (HT * P) + uu * UNIT, UNIT)]
                        sp.dma_start(dst, src.rearrange("(k p) n -> p k n", p=P)).then_inc(landed[s], 32)
                    base[0] += UC
                with sp.Fori(0, 4) as u:
                    for j in range(hc):
                        s = (base[0] + j) % RING
                        M.wait_value("sp", "split", q * (4 * UC) + u * hc + (base[0] + j + 1))
                        dst = raw[:, s, :].rearrange("p (k n) -> p k n", k=KC)
                        src = w_down[bass.ds(q * (HT * P) + j * KC * P, KC * P), bass.ds(u * UNIT, UNIT)]
                        sp.dma_start(dst, src.rearrange("(k p) n -> p k n", p=P)).then_inc(landed[s], 32)
                base[0] += 4 * hc
            base[0] += (FF // (HT * P) - 1) * 4 * UC
            for j in range(RING):
                s = (base[0] + j) % RING
                M.wait_value("sp", "split", base[0] + j + 1)
                sp.dma_start(raw[:, s, :].rearrange("p (k n) -> p k n", k=KC),
                             w_down[0:KC * P, 0:UNIT].rearrange("(k p) n -> p k n", p=P)).then_inc(
                    landed[s], 32)

        for s in range(RING):
            M.handle[f"landed{s}"], M.count[f"landed{s}"] = landed[s], 0

        chunk_no = [0]

        def split_next():
            s = M.count["rounded"] % RING
            M.count[f"landed{s}"] += 32
            M.wait_value("act", f"landed{s}", here(f"landed{s}"), alone=False)
            if chunk_no[0]:
                M.wait_value("act", "used", here("used"), alone=False)
            done(act.copy(w_hi[:, s, :], raw[:, s, :]), "rounded")
            M.wait_value("dve", "rounded", here("rounded"), alone=False)
            done(dve.tensor_tensor(w_lo[:, s, :], raw[:, s, :], w_hi[:, s, :].bitcast(F32),
                                   ALU.subtract), "split")

        def multiply(emit):
            s = M.count["used"] % RING
            M.wait_value("pe", "split", here("used") + RING + 1, alone=False)
            done(emit(s), "used")
            chunk_no[0] += 1
            split_next()

        def column_chunk(s, k0, par, first, final, a0):
            ins = None
            for kk in range(KC):
                for f in range(4):
                    wh = w_hi[:, s, kk * UNIT + f * P:kk * UNIT + (f + 1) * P]
                    wl = w_lo[:, s, kk * UNIT + f * P:kk * UNIT + (f + 1) * P]
                    o = pg[:, par, f // 2, (f % 2) * S:(f % 2 + 1) * S]
                    ah, al = a_hi[:, a0 + k0 + kk, :], a_lo[:, a0 + k0 + kk, :]
                    for n, (l, r) in enumerate(((wh, ah), (wh, al), (wl, ah))):
                        ins = pe.matmul(o, l, r, start=(first and kk == 0 and f % 2 == 0 and n == 0),
                                        stop=(final and kk == KC - 1 and n == 2),
                                        skip_group_check=True)
            return ins

        def row_chunk(s, k0, par, first, final, a0, act_hi=None, act_lo=None, n=UNIT, kc=KC):
            ins = None
            for kk in range(kc):
                wh, wl = w_hi[:, s, kk * n:(kk + 1) * n], w_lo[:, s, kk * n:(kk + 1) * n]
                for t in range(T):
                    ah = (act_hi or a_hi)[:, a0 + k0 + kk, t * P:(t + 1) * P]
                    al = (act_lo or a_lo)[:, a0 + k0 + kk, t * P:(t + 1) * P]
                    for m, (l, r) in enumerate(((ah, wh), (ah, wl), (al, wh))):
                        ins = pe.matmul(pg[:, par, t, 0:n], l, r,
                                        start=(first and kk == 0 and m == 0),
                                        stop=(final and kk == kc - 1 and m == 2))
            return ins

        def unit(kind, evac, chunks=UC, a0=0, n=UNIT, kc=KC, hi=None, lo=None):
            par = M.count["unit"] % 2
            M.wait_value("pe", "out_a", here("unit") + 1)
            M.wait_value("pe", "out_v", here("unit") + 1)
            for j in range(chunks):
                if kind == "col":
                    def emit(s):
                        return column_chunk(s, j * kc, par, j == 0, j == chunks - 1, a0)
                else:
                    def emit(s):
                        return row_chunk(s, j * kc, par, j == 0, j == chunks - 1, a0, hi, lo, n, kc)
                multiply(emit)
            M.count["unit"] += 1
            complete = Mark("used", M.count["used"], list(M.stack))
            wait("act", complete)
            wait("dve", complete)
            a, v = evac(par)
            done(a, "out_a")
            done(v, "out_v")

        def copy_rows(dst):
            def evac(par):
                return (act.copy(dst(0), pg[:, par, 0, :]), dve.tensor_copy(dst(1), pg[:, par, 1, :]))
            return evac

        def copy_cols(dst):
            def evac(par):
                return (act.copy(dst(0), pg[:, par, 0, :].rearrange("p (f s) -> p f s", f=2)),
                        dve.tensor_copy(dst(1), pg[:, par, 1, :].rearrange("p (f s) -> p f s", f=2)))
            return evac

        def all_wait(engines=("pe", "act", "dve", "pool"), on=("pe", "act", "dve", "pool")):
            for e in engines:
                for o in on:
                    M.wait_value(e, o, here(o))
                M.wait_value(e, "out_a", here("out_a"))
                M.wait_value(e, "out_v", here("out_v"))
                M.wait_value(e, "used", here("used"))

        def rstd(ss, dst, width):
            n = ss.shape[1]
            m = done(dve.tensor_scalar(ss, ss, 1.0 / width, EPS, ALU.mult, ALU.add), "dve")
            wait("pool", m)
            return done(pool.tensor_tensor(dst, ss, cvals[:, 1:2].to_broadcast([P, n]), ALU.pow), "pool")

        def transpose_split(src, ntiles, a0, gain=None, ready=None):
            for kp in range(ntiles // 2):
                b = kp % 2
                if ready:
                    wait("pe", ready)
                last("pe", f"xp_lo{b}")
                for kk in range(2):
                    for t in range(T):
                        k = 2 * kp + kk
                        ins = pe.transpose(pa[:, b, kk * S + t * P:kk * S + (t + 1) * P],
                                           src(t)[:, k * P:(k + 1) * P], ident[:, :])
                m = done(ins, "pe")
                wait("act", m)
                wait("dve", m)
                if gain is None:
                    dst_h = a_hi[:, a0 + 2 * kp:a0 + 2 * kp + 2, :]
                    dst_l = a_lo[:, a0 + 2 * kp:a0 + 2 * kp + 2, :]
                    ps = pa[:, b, :].rearrange("p (k s) -> p k s", k=2)
                    h = done(act.copy(dst_h, ps), "act")
                    wait("dve", h)
                    done(dve.tensor_tensor(dst_l, ps, dst_h.bitcast(F32), ALU.subtract), "dve",
                         f"xp_lo{b}")
                else:
                    for kk in range(2):
                        k = 2 * kp + kk
                        h = done(act.activation(a_hi[:, a0 + k, :], pa[:, b, kk * S:(kk + 1) * S], ACT.Copy,
                                                scale=gain[:, k:k + 1]), "act")
                    wait("dve", h)
                    for kk in range(2):
                        k = 2 * kp + kk
                        done(dve.scalar_tensor_tensor(a_lo[:, a0 + k, :], pa[:, b, kk * S:(kk + 1) * S],
                                                      gain[:, k:k + 1], a_hi[:, a0 + k, :].bitcast(F32),
                                                      ALU.mult, ALU.subtract), "dve", f"xp_lo{b}")

        def norm(src, width, tmp, st):
            for t in range(T):
                m = done(act.activation(tmp(t), src(t), ACT.Square, accum_out=stat[:, st + t:st + t + 1]),
                         "act")
            wait("dve", m)
            r = rstd(stat[:, st:st + T], stat[:, st + 2:st + 2 + T], width)
            wait("dve", r)
            for t in range(T):
                m = done(dve.tensor_scalar(tmp(t), src(t), stat[:, st + 2 + t:st + 3 + t], None, ALU.mult),
                         "dve")
            return m

        def softmax(sc, ps, mask, scale, st, tiles):
            n = len(tiles)
            for i, (a, b, m0) in enumerate(tiles):
                m = done(dve.tensor_tensor_reduce(sc[:, a:b], ps[:, a:b], mask[:, m0:m0 + b - a], scale,
                                                  3.0 * NEG, ALU.add, ALU.max, stat[:, st + i:st + i + 1]),
                         "dve")
            wait("dve", m)
            m = done(dve.tensor_scalar(stat[:, st + n:st + 2 * n], stat[:, st:st + n], -1.0, None,
                                       ALU.mult), "dve")
            wait("act", m)
            for i, (a, b, _) in enumerate(tiles):
                m = done(act.activation(sc[:, a:b], sc[:, a:b], ACT.Exp,
                                        bias=stat[:, st + n + i:st + n + i + 1],
                                        accum_out=stat[:, st + 2 * n + i:st + 2 * n + i + 1]), "act")
            return m, stat[:, st + 2 * n:st + 3 * n]

        T0, T1 = (0, P, P), (P, 3 * P, 0)

        def weigh(probs, pt, vrhs, after, bank_t=2, bank_o=3):
            wait("pe", after)
            for b in range(3):
                ins = pe.transpose(pa[:, bank_t, b * P:(b + 1) * P], probs[:, b * P:(b + 1) * P],
                                   ident[:, :])
            m = done(ins, "pe")
            wait("act", m)
            m = done(act.copy(pt, pa[:, bank_t, 0:3 * P]), "act")
            wait("pe", m)
            o = pa[:, bank_o, 0:2 * P].rearrange("p (t v) -> p t v", t=2)
            pe.matmul(o[:, 0, :], pt[:, 0:P], vrhs(0), start=True, stop=True)
            pe.matmul(o[:, 1, :], pt[:, P:2 * P], vrhs(0), start=True, stop=False)
            return done(pe.matmul(o[:, 1, :], pt[:, 2 * P:3 * P], vrhs(1), start=False, stop=True),
                        "pe"), o

        sp.dma_start(xres[:, :, :], x.rearrange("(t p) d -> p t d", p=P)).then_inc(M.handle["ld_const"], 16)
        for dst, src in ((ident[:, :], c_ident), (tri[:, :], c_tri), (masks[:, :, :], c_mask)):
            sp.dma_start(dst, src).then_inc(M.handle["ld_const"], 16)
        sp.dma_start(bc[:, :], block_c).then_inc(M.handle["ld_const"], 16)
        bucket = cut(0, 512)
        table = cut(512, DH)
        rope = sb("rope", [P, T, 2, ROPE])
        sp.dma_start(bucket[0:33, :], c_bucket).then_inc(M.handle["ld_const"], 16)
        sp.dma_start(table[0:32, :], rel_table).then_inc(M.handle["ld_const"], 16)
        sp.dma_start(rope[:, :, :, :], c_rope).then_inc(M.handle["ld_const"], 16)
        M.count["ld_const"] = 8 * 16
        stream()
        done(dve.memset(ones[:, :], 1.0), "dve")
        done(dve.memset(cvals[:, 0:1], EPS), "dve")
        done(dve.memset(cvals[:, 1:2], -0.5), "dve")
        m_tab = done(dve.memset(table[32:33, :], 1.0), "dve")
        for e in ("pe", "act", "dve", "pool"):
            M.eng[e].wait_ge(M.handle["ld_const"], M.count["ld_const"])
            wait(e, m_tab)
        for _ in range(RING):
            split_next()

        bias = cut(19 * 1024, DH, S)
        vec = cut(1024, DH, 512)
        vmarks = {}
        for h in range(DH):
            if h >= 2:
                wait("pe", vmarks[h - 2])
            m = done(pe.matmul(pa[:, h % 2, :], table[0:33, h:h + 1].to_broadcast([33, P]),
                               bucket[0:33, :], start=True, stop=True), "pe")
            wait("act", m)
            vmarks[h] = done(act.copy(vec[:, h, :], pa[:, h % 2, :]), "act")
        wait("pool", vmarks[DH - 1])
        pool.dma_start(bias_dram, vec[:, :, :]).then_inc(M.handle["ld_bias"], 16)
        M.wait_value("pool", "ld_bias", 16)
        flat = bias_dram.rearrange("p h j -> (p h j)")
        skew = bass.AP(tensor=flat.tensor, offset=flat.offset + P - 1,
                       ap=[[DH * 512 - 1, P], [512, DH], [1, S]])
        pool.dma_start(bias[:, :, :], skew).then_inc(M.handle["ld_bias"], 16)
        M.count["ld_bias"] = 32
        for e in ("pe", "act", "dve", "pool"):
            M.eng[e].wait_ge(M.handle["ld_bias"], 32)
        all_wait()

        tok = cut(0, T, 8 * UNIT)
        qkT = cut(8 * 1024, 16, S)
        qrT = cut(12 * 1024, 4, S)
        krT = cut(13 * 1024, S)
        kr = cut(13 * 1024 + 256, T, ROPE)
        krd = cut(13 * 1024 + 512, T, 2 * ROPE)
        tmp = cut(8 * 1024, T, D)
        rt = cut(14 * 1024, T, 1152)
        st_q = [cut(14 * 1024 + 512 * e, 2, S) for e in range(2)]
        st_r = cut(15 * 1024, S)
        b_st = cut(15 * 1024 + 256, S)
        sc = [cut(16896, 2, 3 * P)]
        w_s = [cut(17664, 3 * P)]
        pt_s = [cut(18048, 3 * P)]
        lamt = cut(18432, 2, 64)

        with M.loop("layer", DEPTH) as l:
            all_wait()
            pool.dma_start(lc[:, :], layer_c[bass.ds(l * P, P), :]).then_inc(M.handle["ld_layer"], 16)
            M.count["ld_layer"] += 16
            for e in ("act", "dve"):
                M.wait_value(e, "ld_layer", here("ld_layer"))
            for i in range(2):
                m = done(dve.tensor_tensor_reduce(lamt[:, i, :], lc[:, C_LAM + 128 * i:C_LAM + 128 * i + 64],
                                                  lc[:, C_LAM + 128 * i + 64:C_LAM + 128 * i + 128], 1.0,
                                                  0.0, ALU.mult, ALU.add, stat[:, 60 + i:61 + i]), "dve")
            wait("act", m)
            m = done(act.activation(stat[:, 60:62], stat[:, 60:62], ACT.Exp), "act")
            wait("dve", m)
            m = done(dve.tensor_tensor(stat[:, 62:63], stat[:, 61:62], stat[:, 60:61], ALU.subtract), "dve")
            wait("dve", m)
            done(dve.tensor_tensor(stat[:, 62:63], stat[:, 62:63], lc[:, C_INIT:C_INIT + 1],
                                   ALU.subtract), "dve", "neglam")

            m = norm(lambda t: xres[:, t, :], D, lambda t: tmp[:, t, :], 0)
            transpose_split(lambda t: tmp[:, t, :], KT, 0, lc[:, C_G:C_G + KT], m)
            all_wait()
            with M.loop("qk", 2) as u:
                for e in range(2):
                    unit("col", copy_cols(lambda half: qkT[:, bass.ds(u * 8 + (4 * e + 2 * half), 2), :]))
            with M.loop("rest", 4) as u:
                for e in range(2):
                    unit("row", copy_rows(lambda t: tok[:, t, bass.ds(u * (2 * UNIT) + e * UNIT, UNIT)]))
            unit("row", lambda par: (act.copy(kr[:, 0, :], pg[:, par, 0, 0:ROPE]),
                                     dve.tensor_copy(kr[:, 1, :], pg[:, par, 1, 0:ROPE])),
                 chunks=2, n=ROPE, kc=KT // 2)
            all_wait()
            for t in range(T):
                done(act.activation(tok[:, t, 1024:2048], tok[:, t, 1024:2048], ACT.Silu), "act")
                m = done(act.activation(tok[:, t, 3072:4096], tok[:, t, 3072:4096], ACT.Silu), "act")
            wait("dve", m)
            for t in range(T):
                za = tok[:, t, 1024:2048].rearrange("p (h v) -> p h v", h=DH)
                g = lc[:, C_SUB:C_SUB + DV].unsqueeze(1).to_broadcast([P, DH, DV])
                m = done(dve.scalar_tensor_tensor(za, za, lc[:, C_INIT + 1:C_INIT + 2], g,
                                                  ALU.mult, ALU.mult), "dve")
            all_wait()

            with M.loop("diff", DH) as h:
                all_wait()
                q_s, k_s = st_q[0][:, 0, :], st_q[0][:, 1, :]
                done(pool.tensor_copy(q_s, qkT[:, bass.ds(h, 1), :].rearrange("p a s -> p (a s)")), "pool")
                m = done(pool.tensor_copy(k_s, qkT[:, bass.ds(h + DH, 1), :].rearrange("p a s -> p (a s)")),
                         "pool")
                bh = b_st
                m_bias = done(pool.tensor_copy(bh, bias[:, bass.ds(h, 1), :].rearrange("p a s -> p (a s)")),
                              "pool")
                wait("pe", m)
                for mm in range(2):
                    r = slice(mm * DQK, (mm + 1) * DQK)
                    pe.matmul(pa[:, mm, 0:P], q_s[r, 0:P], k_s[r, 0:P], start=True, stop=True)
                    ins = pe.matmul(pa[:, mm, P:3 * P], q_s[r, P:S], k_s[r, 0:S], start=True, stop=True)
                m = done(ins, "pe")
                wait("dve", m)
                wait("dve", m_bias)
                dens = []
                for mm in range(2):
                    m, den = softmax(sc[0][:, mm, :], pa[:, mm, :], bh, DQK ** -0.5, 8 + 8 * mm, (T0, T1))
                    dens.append(den)
                wait("dve", m)
                done(dve.reciprocal(stat[:, 24:26], dens[0]), "dve")
                m = done(dve.reciprocal(stat[:, 26:28], dens[1]), "dve")
                wait("dve", m)
                m = done(dve.tensor_scalar(stat[:, 26:28], stat[:, 26:28], stat[:, 62:63], None, ALU.mult),
                         "dve")
                wait("dve", m)
                cols = ((0, P), (P, 3 * P))
                for t, (a, b) in enumerate(cols):
                    m = done(dve.tensor_scalar(sc[0][:, 0, a:b], sc[0][:, 0, a:b], stat[:, 24 + t:25 + t],
                                               None, ALU.mult), "dve")
                wait("dve", m)
                for t, (a, b) in enumerate(cols):
                    m = done(dve.scalar_tensor_tensor(w_s[0][:, a:b], sc[0][:, 1, a:b],
                                                      stat[:, 26 + t:27 + t], sc[0][:, 0, a:b],
                                                      ALU.mult, ALU.add), "dve")
                m, o = weigh(w_s[0], pt_s[0], lambda t: tok[:, t, bass.ds(h * DV, DV)], m)
                wait("act", m)
                wait("dve", m)
                for t in range(T):
                    m = done(act.activation(sc[0][:, 0, t * P:(t + 1) * P], o[:, t, :], ACT.Square,
                                            accum_out=stat[:, 28 + t:29 + t]), "act")
                wait("dve", m)
                m = rstd(stat[:, 28:30], stat[:, 30:32], DV)
                wait("dve", m)
                for t in range(T):
                    z = tok[:, t, bass.ds(h * DV + 1024, DV)]
                    done(dve.scalar_tensor_tensor(z, o[:, t, :], stat[:, 30 + t:31 + t], z,
                                                  ALU.mult, ALU.mult), "dve")
            all_wait()

            for i, gc in ((0, C_QG), (1, C_KVG)):
                m = norm(lambda t: tok[:, t, 2048 + UNIT * i:2048 + UNIT * (i + 1)], QR,
                         lambda t: tmp[:, t, UNIT * i:UNIT * (i + 1)], 32 + 4 * i)
                transpose_split(lambda t: tmp[:, t, UNIT * i:UNIT * (i + 1)], 4, 4 * i,
                                lc[:, gc:gc + 4], m)
            all_wait()
            for i in range(4):
                unit("col", copy_cols(lambda half: qkT[:, 4 * i + 2 * half:4 * i + 2 * half + 2, :]),
                     chunks=2, a0=4 * (i // 2))
            unit("row", copy_rows(lambda t: tok[:, t, 2048:2048 + UNIT]), chunks=2, a0=0)
            for i in range(2):
                unit("row", copy_rows(lambda t: tok[:, t, i * UNIT:(i + 1) * UNIT]), chunks=2, a0=4)
            all_wait()
            for t in range(T):
                cs = rope[:, t, 0, :]
                sn = rope[:, t, 1, :]
                half = ROPE // 2
                for src, dst, heads in ((tok[:, t, 2048:2560], rt[:, t, 0:512], MH),
                                        (kr[:, t, :], rt[:, t, 512:576], 1)):
                    s3 = src.rearrange("p (h c) -> p h c", h=heads)
                    d3 = dst.rearrange("p (h c) -> p h c", h=heads)
                    rot = rt[:, t, 576:576 + ROPE * heads].rearrange("p (h c) -> p h c", h=heads)

                    def bcast(v):
                        return v.unsqueeze(1).to_broadcast([P, heads, v.shape[-1]])
                    last("dve", "rope_add")
                    done(dve.tensor_tensor(rot[:, :, 0:half], s3[:, :, half:ROPE], bcast(sn[:, 0:half]),
                                           ALU.mult), "dve")
                    done(dve.tensor_tensor(rot[:, :, half:ROPE], s3[:, :, 0:half], bcast(sn[:, half:ROPE]),
                                           ALU.mult), "dve")
                    m = done(dve.tensor_tensor(d3, s3, bcast(cs), ALU.mult), "dve")
                    wait("dve", m)
                    m = done(dve.tensor_tensor(d3, d3, rot, ALU.add), "dve", "rope_add")
                wait("dve", m)
                for i in range(2):
                    m = done(dve.tensor_copy(krd[:, t, i * ROPE:(i + 1) * ROPE], rt[:, t, 512:576]), "dve")
            wait("pe", m)
            for i in range(4):
                for t in range(T):
                    ins = pe.transpose(pa[:, i // 2, (i % 2) * S + t * P:(i % 2) * S + (t + 1) * P],
                                       rt[:, t, i * P:(i + 1) * P], ident[:, :])
            for t in range(T):
                ins = pe.transpose(pa[:, 2, t * P:(t + 1) * P], krd[:, t, :], ident[:, :])
            m = done(ins, "pe")
            wait("act", m)
            wait("dve", m)
            done(act.copy(qrT[:, 0:2, :], pa[:, 0, :].rearrange("p (a s) -> p a s", a=2)), "act")
            done(dve.tensor_copy(qrT[:, 2:4, :], pa[:, 1, :].rearrange("p (a s) -> p a s", a=2)), "dve")
            done(act.copy(krT, pa[:, 2, 0:S]), "act")
            all_wait()

            with M.loop("mla", MH // 2) as hp:
                for e in range(2):
                    all_wait()
                    r = slice(e * ROPE, (e + 1) * ROPE)
                    if e == 0:
                        m = done(pool.tensor_copy(st_r, qrT[:, bass.ds(hp, 1), :].rearrange(
                            "p a s -> p (a s)")), "pool")
                    q_s = st_q[e][:, 0, :]
                    m = done(pool.tensor_copy(q_s, qkT[:, bass.ds(hp * 2 + e, 1), :].rearrange(
                        "p a s -> p (a s)")), "pool")
                    wait("pe", m)
                    k_h = qkT[:, bass.ds(hp * 2 + (MH + e), 1), :].rearrange("p a s -> p (a s)")
                    for (a, b), qc, nk in (((0, P), slice(0, P), P), ((P, 3 * P), slice(P, S), S)):
                        pe.matmul(pa[:, 0, a:b], q_s[:, qc], k_h[:, 0:nk], start=True, stop=False)
                        ins = pe.matmul(pa[:, 0, a:b], st_r[r, qc], krT[r, 0:nk], start=False, stop=True)
                    m = done(ins, "pe")
                    wait("dve", m)
                    m, den = softmax(sc[0][:, 0, :], pa[:, 0, :], masks[:, 0, :], (NOPE + ROPE) ** -0.5, 8,
                                     (T0, T1))
                    wait("dve", m)
                    rd = done(dve.reciprocal(stat[:, 24:26], den), "dve")
                    m, o = weigh(sc[0][:, 0, :], pt_s[0],
                                 lambda t: tok[:, t, bass.ds(hp * (2 * MV) + e * MV, MV)], m)
                    wait("dve", m)
                    wait("dve", rd)
                    for t in range(T):
                        z = tok[:, t, bass.ds(hp * (2 * MV) + (e * MV + 3072), MV)]
                        done(dve.scalar_tensor_tensor(z, o[:, t, :], stat[:, 24 + t:25 + t], z,
                                                      ALU.mult, ALU.mult), "dve")
            all_wait()
            transpose_split(lambda t: tok[:, t, 1024:2048], 8, 0)
            transpose_split(lambda t: tok[:, t, 3072:4096], 8, 8)
            all_wait()

            def add_x(u, e):
                def evac(par):
                    xs = [xres[:, t, bass.ds(u * (2 * UNIT) + e * UNIT, UNIT)] for t in range(T)]
                    done(dve.tensor_tensor(xs[0], xs[0], pg[:, par, 0, :], ALU.add), "dve")
                    return act.nop(), dve.tensor_tensor(xs[1], xs[1], pg[:, par, 1, :], ALU.add)
                return evac
            with M.loop("w_out", 2) as u:
                for e in range(2):
                    unit("row", add_x(u, e))

        all_wait()
        rows = cut(18 * 1024, D)

        def load_row(i):
            M.wait_value("pool", "dve", here("dve"))
            pool.dma_start(rows, rows_c[i * P:(i + 1) * P, :]).then_inc(M.handle["ld_layer"], 16)
            M.count["ld_layer"] += 16
            M.wait_value("dve", "ld_layer", here("ld_layer"))

        load_row(0)
        tmp2 = cut(8 * 1024, T, D)
        m = norm(lambda t: xres[:, t, :], D, lambda t: tmp2[:, t, :], 0)
        wait("dve", m)
        for t in range(T):
            m = done(dve.tensor_tensor(xres[:, t, :], tmp2[:, t, :], rows, ALU.mult), "dve")
        all_wait()

        z = cut(0, T, D)
        xbc = cut(4 * 1024, 32, S)
        xs = cut(12 * 1024, T, D)
        m = norm(lambda t: xres[:, t, :], D, lambda t: tmp2[:, t, :], 0)
        transpose_split(lambda t: tmp2[:, t, :], KT, 0, bc[:, B_PRE:B_PRE + KT], m)
        all_wait()

        def conv(u, e):
            def evac(par):
                def tap(f, j):
                    return bc[:, bass.ds(u * 32 + (B_CW + (4 * e + f) * 4 + j), 1)]
                def dst(f, a=0, b=S):
                    return xbc[:, bass.ds(u * 8 + (4 * e + f), 1), a:b].rearrange("p a s -> p (a s)")
                ps = [pg[:, par, f // 2, (f % 2) * S:(f % 2 + 1) * S] for f in range(4)]
                for f in range(4):
                    cb = bc[:, bass.ds(u * 8 + (B_CB + 4 * e + f), 1)]
                    m = done(dve.tensor_scalar(dst(f), ps[f], tap(f, 3), cb, ALU.mult, ALU.add), "dve")
                for j in (1, 2, 3):
                    wait("dve", m)
                    for f in range(4):
                        v = dve.scalar_tensor_tensor(dst(f, j), ps[f][:, 0:S - j], tap(f, 3 - j),
                                                     dst(f, j), ALU.mult, ALU.add)
                        if not (j == 3 and f == 3):
                            m = done(v, "dve")
                return act.nop(), v
            return evac

        with M.loop("xbc", 4) as u:
            for e in range(2):
                unit("col", conv(u, e))
        with M.loop("z", 2) as u:
            for e in range(2):
                unit("row", copy_rows(lambda t: z[:, t, bass.ds(u * (2 * UNIT) + e * UNIT, UNIT)]))
        dt = cut(16 * 1024, T, SH)
        unit("row", lambda par: (act.copy(dt[:, 0, :], pg[:, par, 0, 0:SH]),
                                 dve.tensor_copy(dt[:, 1, :], pg[:, par, 1, 0:SH])),
             chunks=1, n=SH, kc=KT)
        all_wait()
        for t in range(T):
            done(act.activation(z[:, t, :], z[:, t, :], ACT.Silu), "act")
        for i in range(4):
            done(act.activation(xbc[:, 8 * i:8 * i + 8, :], xbc[:, 8 * i:8 * i + 8, :], ACT.Silu), "act")

        A = 16 * 1024 + 64
        n2 = T * SH
        v1, v2, s1, s2 = (cut(A + n2 * i, n2) for i in range(4))
        dtf = dt.rearrange("p t h -> p (t h)")
        dA = cut(A + 4 * n2, T, SH)
        acs = cut(A + 5 * n2, 3, SH)
        aneg = cut(A + 7 * n2, SH)

        def chain(ins):
            m = done(ins, "dve")
            wait("dve", m)
            return m

        chain(dve.tensor_tensor(dt, dt, bc[:, B_DTB:B_DTB + SH].unsqueeze(1).to_broadcast([P, T, SH]),
                                ALU.add))
        chain(dve.tensor_scalar(v1, dtf, -1.0, None, ALU.mult))
        m = chain(dve.tensor_tensor(v1, v1, dtf, ALU.min))
        wait("act", m)
        done(act.activation(aneg, bc[:, B_AL:B_AL + SH], ACT.Exp), "act")
        m = done(act.activation(v1, v1, ACT.Exp), "act")
        wait("dve", m)
        chain(dve.tensor_scalar(v2, v1, 2.0, None, ALU.add))
        chain(dve.reciprocal(v2, v2))
        chain(dve.tensor_tensor(s1, v1, v2, ALU.mult))
        chain(dve.tensor_tensor(s2, s1, s1, ALU.mult))
        chain(dve.tensor_scalar(v1, s2, 1.0 / 17, 1.0 / 15, ALU.mult, ALU.add))
        for k in (13, 11, 9, 7, 5, 3, 1):
            chain(dve.tensor_tensor(v1, v1, s2, ALU.mult))
            chain(dve.tensor_scalar(v1, v1, 1.0 / k, None, ALU.add))
        chain(dve.tensor_tensor(v1, v1, s1, ALU.mult))
        chain(dve.tensor_scalar(dtf, dtf, 0.0, None, ALU.max))
        chain(dve.scalar_tensor_tensor(dtf, v1, 2.0, dtf, ALU.mult, ALU.add))
        m = chain(dve.scalar_tensor_tensor(dA, dt, -1.0, aneg.unsqueeze(1).to_broadcast([P, T, SH]),
                                           ALU.mult, ALU.mult))
        wait("pe", m)
        pe.matmul(pa[:, 0, 0:SH], tri[:, :], dA[:, 0, :], start=True, stop=True)
        pe.matmul(pa[:, 0, SH:2 * SH], tri[:, :], dA[:, 1, :], start=True, stop=True)
        m = done(pe.matmul(pa[:, 0, 2 * SH:3 * SH], ones[:, :], dA[:, 0, :], start=True, stop=True), "pe")
        wait("dve", m)
        done(dve.tensor_copy(acs[:, 0, :], pa[:, 0, 0:SH]), "dve")
        m = chain(dve.tensor_copy(acs[:, 2, :], pa[:, 0, SH:2 * SH]))
        done(dve.tensor_tensor(acs[:, 1, :], acs[:, 0, :], pa[:, 0, 2 * SH:3 * SH], ALU.subtract), "dve")
        all_wait()
        for i in range(8):
            b = i % 4
            last("pe", f"xs_out{b}")
            for kk in range(2):
                for t in range(T):
                    ins = pe.transpose(pa[:, b, (t * 2 + kk) * P:(t * 2 + kk + 1) * P],
                                       xbc[:, 2 * i + kk, t * P:(t + 1) * P], ident[:, :])
            m = done(ins, "pe")
            e, fn = (("act", act.copy), ("dve", dve.tensor_copy))[i % 2]
            wait(e, m)
            done(fn(xs[:, :, 2 * P * i:2 * P * (i + 1)], pa[:, b, :].rearrange("p (t c) -> p t c", t=T)), e,
                 f"xs_out{b}")
        all_wait()

        G = 17 * 1024
        b_s = cut(G, S)
        c_m = cut(G + 256, 3 * P)
        da_s = cut(G + 640, T, HPG)
        ac_s = cut(G + 656, 3, HPG)
        dec = cut(G + 1024, HPG, 3 * P)
        xdt = cut(G + 2560, T, HPG, HD)
        yb = cut(G + 3072, T, HPG * HD)
        ysq = cut(G + 3584, HPG * HD)
        with M.loop("scan", SG) as g:
            all_wait()
            done(pool.tensor_copy(b_s, xbc[:, bass.ds(g + 16, 1), :].rearrange("p a s -> p (a s)")), "pool")
            done(pool.tensor_copy(da_s, dA[:, :, bass.ds(g * HPG, HPG)]), "pool")
            m_st = done(pool.tensor_copy(ac_s, acs[:, :, bass.ds(g * HPG, HPG)]), "pool")
            wait("pe", m_st)
            c_g = xbc[:, bass.ds(g + 24, 1), :].rearrange("p a s -> p (a s)")
            pe.matmul(pa[:, 0, 0:S], b_s[:, 0:P], c_g[:, 0:S], start=True, stop=True)
            m = done(pe.matmul(pa[:, 0, S:S + P], b_s[:, P:S], c_g[:, P:S], start=True, stop=True), "pe")
            wait("dve", m)
            done(dve.tensor_tensor(c_m[:, 0:P], pa[:, 0, 0:P], tri[:, :], ALU.mult), "dve")
            done(dve.tensor_copy(c_m[:, P:S], pa[:, 0, P:S]), "dve")
            done(dve.tensor_tensor(c_m[:, S:S + P], pa[:, 0, S:S + P], tri[:, :], ALU.mult), "dve")
            for r in range(HPG):
                for t in range(T):
                    ins = pe.matmul(pa[:, 1 + r // 2, (r % 2) * S + t * P:(r % 2) * S + (t + 1) * P],
                                    da_s[:, t, r:r + 1].to_broadcast([P, P]), tri[:, :],
                                    start=True, stop=True)
            m = done(ins, "pe")
            wait("dve", m)
            wait("dve", m_st)
            for r in range(HPG):
                for blk, t in ((0, 0), (1, 1), (2, 1)):
                    m = done(dve.tensor_scalar(dec[:, r, blk * P:(blk + 1) * P],
                                               pa[:, 1 + r // 2, (r % 2) * S + t * P:(r % 2) * S + (t + 1) * P],
                                               ac_s[:, blk, r:r + 1], 0.0, ALU.subtract, ALU.min), "dve")
            wait("act", m)
            m = done(act.activation(dec, dec, ACT.Exp), "act")
            wait("dve", m)
            m = done(dve.tensor_tensor(dec, dec, c_m.unsqueeze(1).to_broadcast([P, HPG, 3 * P]), ALU.mult),
                     "dve")
            x_g = xs[:, :, bass.ds(g * (HPG * HD), HPG * HD)].rearrange("p t (r c) -> p t r c", r=HPG)
            for t in range(T):
                dt_g = dt[:, t, bass.ds(g * HPG, HPG)].unsqueeze(2).to_broadcast([P, HPG, HD])
                m = done(dve.tensor_tensor(xdt[:, t, :, :], x_g[:, t, :, :], dt_g, ALU.mult), "dve")
            wait("pe", m)
            for r in range(HPG):
                o = [pa[:, 3, t * S + r * HD:t * S + (r + 1) * HD] for t in range(T)]
                pe.matmul(o[0], dec[:, r, 0:P], xdt[:, 0, r, :], start=True, stop=True)
                pe.matmul(o[1], dec[:, r, P:2 * P], xdt[:, 0, r, :], start=True, stop=False)
                ins = pe.matmul(o[1], dec[:, r, 2 * P:3 * P], xdt[:, 1, r, :], start=False, stop=True)
            m = done(ins, "pe")
            for t in range(T):
                ds_g = bc[:, bass.ds(g * HPG + B_DS, HPG)].unsqueeze(2).to_broadcast([P, HPG, HD])
                yt = yb[:, t, :].rearrange("p (r c) -> p r c", r=HPG)
                d = done(dve.tensor_tensor(yt, x_g[:, t, :, :], ds_g, ALU.mult), "dve")
            wait("dve", m)
            wait("dve", d)
            m = chain(dve.tensor_tensor(yb, yb, pa[:, 3, :].rearrange("p (t c) -> p t c", t=T), ALU.add))
            zg = z[:, :, bass.ds(g * (HPG * HD), HPG * HD)]
            m = chain(dve.tensor_tensor(yb, yb, zg, ALU.mult))
            wait("act", m)
            for t in range(T):
                if t:
                    wait("act", m)
                m = done(act.activation(ysq, yb[:, t, :], ACT.Square, accum_out=stat[:, 28 + t:29 + t]),
                         "act")
            wait("dve", m)
            m = rstd(stat[:, 28:30], stat[:, 30:32], HPG * HD)
            wait("dve", m)
            for t in range(T):
                done(dve.tensor_scalar(zg[:, t, :], yb[:, t, :], stat[:, 30 + t:31 + t], None, ALU.mult),
                     "dve")
        all_wait()

        qkT2 = cut(4 * 1024, 32, S)
        v2t = cut(12 * 1024, T, D)
        with M.loop("qk2", 4) as u:
            for e in range(2):
                unit("col", copy_cols(lambda half: qkT2[:, bass.ds(u * 8 + (4 * e + 2 * half), 2), :]))
        with M.loop("v2", 2) as u:
            for e in range(2):
                unit("row", copy_rows(lambda t: v2t[:, t, bass.ds(u * (2 * UNIT) + e * UNIT, UNIT)]))
        all_wait()
        sc2 = cut(17 * 1024, 3 * P)
        pt2 = cut(17 * 1024 + 384, 3 * P)
        q2 = cut(18 * 1024, S)
        with M.loop("dilated", AH) as h:
            all_wait()
            m = done(pool.tensor_copy(q2, qkT2[:, bass.ds(h, 1), :].rearrange("p a s -> p (a s)")), "pool")
            wait("pe", m)
            k_h = qkT2[:, bass.ds(h + AH, 1), :].rearrange("p a s -> p (a s)")
            pe.matmul(pa[:, 0, 0:P], q2[:, 0:P], k_h[:, 0:P], start=True, stop=True)
            m = done(pe.matmul(pa[:, 0, P:3 * P], q2[:, P:S], k_h[:, 0:S], start=True, stop=True), "pe")
            wait("dve", m)
            m, den = softmax(sc2, pa[:, 0, :], masks[:, 1, :], AD ** -0.5, 8, (T0, T1))
            wait("dve", m)
            rd = done(dve.reciprocal(stat[:, 24:26], den), "dve")
            m, o = weigh(sc2, pt2, lambda t: v2t[:, t, bass.ds(h * AD, AD)], m)
            wait("dve", m)
            wait("dve", rd)
            for t in range(T):
                done(dve.tensor_scalar(v2t[:, t, bass.ds(h * AD, AD)], o[:, t, :], stat[:, 24 + t:25 + t],
                                       None, ALU.mult), "dve")
        all_wait()

        mix = cut(4 * 1024, T, D)

        def put(dst, u, e, add):
            def evac(par):
                d = [dst[:, t, bass.ds(u * (2 * UNIT) + e * UNIT, UNIT)] for t in range(T)]
                if not add:
                    return act.copy(d[0], pg[:, par, 0, :]), dve.tensor_copy(d[1], pg[:, par, 1, :])
                done(dve.tensor_tensor(d[0], d[0], pg[:, par, 0, :], ALU.add), "dve")
                return act.nop(), dve.tensor_tensor(d[1], d[1], pg[:, par, 1, :], ALU.add)
            return evac

        for half, src in enumerate((z, v2t)):
            transpose_split(lambda t: src[:, t, :], KT, 0,
                            bc[:, B_SSM:B_SSM + KT] if half == 0 else None)
            all_wait()
            with M.loop(f"w_out2_{half}", 2) as u:
                for e in range(2):
                    unit("row", put(mix, u, e, half == 1))
            all_wait()

        def add_normed(src, i):
            load_row(i)
            m = norm(lambda t: src[:, t, :], D, lambda t: tmp2[:, t, :], 0)
            for t in range(T):
                wait("dve", m)
                m = done(dve.tensor_tensor(tmp2[:, t, :], tmp2[:, t, :], rows, ALU.mult), "dve")
            for t in range(T):
                wait("dve", m)
                m = done(dve.tensor_tensor(xres[:, t, :], xres[:, t, :], tmp2[:, t, :], ALU.add), "dve")
            all_wait()

        add_normed(mix, 1)

        m = norm(lambda t: xres[:, t, :], D, lambda t: tmp2[:, t, :], 0)
        transpose_split(lambda t: tmp2[:, t, :], KT, 0, bc[:, B_MLP:B_MLP + KT], m)
        done(dve.memset(mix, 0.0), "dve")
        all_wait()
        h_t = cut(0, 4, UNIT)

        def relu2(uu):
            def evac(par):
                for b in range(2):
                    r = h_t[:, 2 * par + b, :]
                    last("act", f"hid_lo{par}{b}")
                    m = done(act.activation(r, pg[:, par, b, :], ACT.Relu), "act")
                    wait("act", m)
                    m = done(act.activation(r, r, ACT.Square), "act")
                    wait("act", m)
                    r3 = r.rearrange("p (f s) -> p f s", f=2)
                    hh = hid_hi[:, 4 * uu + 2 * b:4 * uu + 2 * b + 2, :]
                    hl = hid_lo[:, 4 * uu + 2 * b:4 * uu + 2 * b + 2, :]
                    a = act.copy(hh, r3)
                    m = done(a, "act")
                    wait("dve", m)
                    done(dve.tensor_tensor(hl, r3, hh.bitcast(F32), ALU.subtract), "dve",
                         f"hid_lo{par}{b}")
                return act.nop(), dve.nop()
            return evac

        with M.loop("slice", FF // (HT * P)) as q:
            all_wait()
            for uu in range(2):
                unit("col", relu2(uu))
            all_wait()
            with M.loop("down", 2) as u:
                for e in range(2):
                    unit("row", put(mix, u, e, True), chunks=HT // KC, hi=hid_hi, lo=hid_lo)
            all_wait()

        add_normed(mix, 2)
        M.wait_value("act", "dve", here("dve"))
        act.dma_start(out.rearrange("(t p) d -> p t d", p=P), xres[:, :, :]).then_inc(stored, 16)
        act.wait_ge(stored, 16)
    return M.plan


def _rope_consts(np):
    pos = np.arange(S, dtype=np.float32)
    inv = (1.0 / (10000.0 ** (np.arange(0, ROPE, 2, dtype=np.float32) / ROPE))).astype(np.float32)
    ang = (pos[:, None] * inv[None, :]).astype(np.float32)
    ang = np.concatenate([ang, ang], axis=-1)
    sin = np.sin(ang)
    sin[:, :ROPE // 2] *= -1
    t = np.stack([np.cos(ang), sin], axis=1).astype(np.float32)
    return np.ascontiguousarray(t.reshape(T, P, 2, ROPE).transpose(1, 0, 2, 3))


def _bucket_const(np):
    dist = 255 - np.arange(512)
    n = np.maximum(dist, 0)
    nf = np.maximum(n, 1).astype(np.float32)
    large = 16 + (np.log(nf / np.float32(16)) / np.float32(math.log(128 / 16)) * 16).astype(np.int32)
    b = np.where(n < 16, n, np.minimum(large, 31))
    c = np.zeros((33, 512), np.float32)
    c[b, np.arange(512)] = 8.0
    c[:32, dist < 0] = 0.0
    c[32, dist < 0] = NEG
    return c


def _mask_const(np):
    dist = 128 + np.arange(P)[:, None] - np.arange(S)[None, :]
    causal = np.where(dist >= 0, 0.0, NEG)
    n = sum(((dist >= 0) & (dist % d == 0) & (dist <= w)).astype(np.int64)
            for w, d in ((128, 1), (512, 4), (2048, 16)))
    dil = np.where(n > 0, np.log(np.maximum(n, 1)) * AD ** 0.5, NEG)
    return np.stack([causal, dil], axis=1).astype(np.float32)


def kernel(**inputs):
    import numpy as np
    import concourse.bacc as bacc
    from concourse.bass_utils import run_bass_kernel_spmd as run

    g = {k: np.ascontiguousarray(v) for k, v in inputs.items()}

    def cols(v):
        return v.reshape(-1, P).T

    def rows(v):
        return np.broadcast_to(v.reshape(1, -1), (P, v.size))

    layer_c = []
    for l in range(DEPTH):
        li = 0.8 - 0.6 * math.exp(-0.3 * l)
        layer_c.append(np.concatenate([
            cols(g["norm_g"][l]), cols(g["mla_q_norm_g"][l]), cols(g["mla_kv_norm_g"][l]),
            rows(g["diff_subln_g"][l]), rows(g["diff_lambda"][l]),
            rows(np.array([li, 1.0 - li], np.float32))], axis=1))
    conv = g["conv_w_2"][0].reshape(4, 32, P).transpose(2, 1, 0).reshape(P, 128)
    block_c = np.concatenate([
        cols(g["norm_mix_pre_2"][0]), cols(g["norm_mlp_pre_2"][0]), cols(g["ssm_norm_w_2"][0]), conv,
        cols(g["conv_b_2"][0]), rows(g["dt_bias_2"][0]), rows(g["a_log_2"][0]), rows(g["d_skip_2"][0])],
        axis=1)
    arrays = {
        "x": g["x"][0], "layer_c": np.concatenate(layer_c, axis=0),
        "w_in": g["w_in"].reshape(DEPTH * D, W_IN), "w_uq": g["w_uq"].reshape(DEPTH * QR, -1),
        "w_ukv": g["w_ukv"].reshape(DEPTH * KVR, -1), "w_out": g["w_out"].reshape(DEPTH * D, D),
        "rel_table": g["rel_bias_table"], "block_c": block_c,
        "rows_c": np.concatenate([rows(g["final_norm_g"]), rows(g["norm_mix_post_2"][0]),
                                  rows(g["norm_mlp_post_2"][0])], axis=0),
        "w_in_2": g["w_in_2"][0], "w_out_2": g["w_out_2"][0], "w_up": g["w_up_2"][0],
        "w_down": g["w_down_2"][0], "c_ident": np.eye(P, dtype=np.float32),
        "c_tri": np.triu(np.ones((P, P), np.float32)), "c_mask": _mask_const(np),
        "c_bucket": _bucket_const(np), "c_rope": _rope_consts(np),
    }
    arrays = {k: np.ascontiguousarray(v) for k, v in arrays.items()}
    plan = {}
    for real in (False, True):
        plan["real"] = real
        nc = bacc.Bacc("TRN2", target_bir_lowering=False, num_devices=1)
        args = {k: nc.dram_tensor(f"in_{k}", v.shape, mybir.dt.from_np(v.dtype),
                                  kind="ExternalInput").ap() for k, v in arrays.items()}
        out = nc.dram_tensor("out_x", (S, D), F32, kind="ExternalOutput").ap()
        build(nc, plan, out=out, **args)
    r = run(nc, [{f"in_{k}": v for k, v in arrays.items()}], core_ids=[0])
    return r.results[0]["out_x"].reshape(1, S, D)
```

```python
import math
from contextlib import ExitStack, contextmanager

import concourse.bass as bass
from concourse import mybir

F32 = mybir.dt.float32
F32R = mybir.dt.float32r
ALU = mybir.AluOpType
ACT = mybir.ActivationFunctionType
ET = mybir.EngineType
AX = mybir.AxisListType

P = 128
D = 2048
S = 256
T = S // P
DEPTH = 2
UNIT = 512
KC = 2
CHUNK = KC * UNIT
RING = 4
KT = D // P
UC = KT // KC
EPS = 1e-6
NEG = -1e30
CREDIT = 512

DH, DQK, DV = 8, 64, 128
MH, NOPE, ROPE, MV = 8, 128, 64, 128
QR = KVR = 512
W_IN = 6208
SH, SG, HPG, SN = 32, 8, 4, 128
HD = 64
AH, AD = 16, 128
W_IN2 = 12320
XBC = 4096
FF = 8192
LAYER_CHUNKS = 12 * UC + 2 + 7 * 2 + 4 * UC
GT = UNIT // P
GROUPS = FF // UNIT
GROUP2_CHUNKS = 2 * (UC + D // UNIT * (GT // KC))

C_G, C_QG, C_KVG, C_SUB, C_LAM, C_INIT = 0, 16, 20, 24, 152, 408
C_N = 410
B_PRE, B_MLP, B_SSM, B_CW, B_CB, B_DTB, B_AL, B_DS = 0, 16, 32, 48, 176, 208, 240, 272
B_N = 304


class Mark:

    def __init__(self, sem, n, frames):
        self.sem, self.n, self.frames = sem, n, frames


class Marks:

    def __init__(self, nc, plan):
        self.nc, self.plan, self.stack = nc, plan, []
        self.count, self.named = {}, {}
        self.eng = {"pe": nc.tensor, "act": nc.scalar, "dve": nc.vector, "pool": nc.gpsimd,
                    "sp": nc.sync}
        self.handle = {}

    def add(self, name, handle, start=0):
        self.handle[name], self.count[name] = handle, start

    def stride(self, frame, sem):
        return self.plan.get((frame, sem), 0)

    @contextmanager
    def loop(self, name, n, carry=()):
        for eng, names in carry:
            for m in names:
                if m in self.named:
                    self.wait(eng, self.named[m])
        start = dict(self.count)
        with self.nc.Fori(0, n, engines=(ET.PE, ET.Activation, ET.DVE, ET.Pool)) as i:
            frame = {"name": name, "var": i, "n": n, "live": True, "marks": {}}
            self.stack.append(frame)
            yield i
            self.stack.pop()
            frame["live"] = False
        for s in self.count:
            self.plan[(name, s)] = self.count[s] - start[s]
            self.count[s] = start[s] + n * (self.count[s] - start[s])
        for k, m in frame["marks"].items():
            self.plan[(name, "last", k)] = (m.sem, m.n)

    def done(self, ins, sem, name=None, by=1):
        ins.then_inc(self.handle[sem], by)
        self.count[sem] += by
        return self.keep(name, Mark(sem, self.count[sem], list(self.stack)))

    def keep(self, name, m):
        if name:
            self.named[name] = m
            for f in self.stack:
                f["marks"][name] = m
        return m

    def value(self, sem, n, frames, back=None):
        v = n
        for f in frames:
            st = self.stride(f["name"], sem)
            if f["live"]:
                k = f["var"]
                v = v + (k * st if st else 0)
                if f is back:
                    assert not self.plan.get("real") or n - st > 0, (sem, n, st)
                    v = v - st
            else:
                v = v + (f["n"] - 1) * st
        return v

    def wait_value(self, eng, sem, v, alone=True):
        self.eng[eng].wait_ge(self.handle[sem], v)
        if alone and not isinstance(v, int):
            self.eng[eng].sem_inc(self.handle["holder_" + eng])

    def wait(self, eng, m):
        if m is not None:
            self.wait_value(eng, m.sem, self.value(m.sem, m.n, m.frames))

    def wait_last(self, eng, name):
        if not self.stack:
            return self.wait(eng, self.named.get(name))
        f = self.stack[-1]
        if name in f["marks"]:
            return self.wait(eng, f["marks"][name])
        last = self.plan.get((f["name"], "last", name))
        if last is None:
            return self.wait(eng, self.named.get(name))
        sem, n = last
        self.wait_value(eng, sem, self.value(sem, n, list(self.stack), back=f))


def build(nc, plan, x, layer_c, w_in, w_uq, w_ukv, w_out, rel_table, block_c, rows_c, w_in_2,
          w_out_2, w_up, w_down, c_ident, c_tri, c_mask, c_bucket, c_rope, out):
    with ExitStack() as ctx:
        def sb(name, shape, dt=F32):
            return ctx.enter_context(nc.sbuf_tensor(name, shape, dt))

        def sem(name):
            return ctx.enter_context(nc.semaphore(name))

        M = Marks(nc, plan)
        pe, act, dve, pool, sp = nc.tensor, nc.scalar, nc.vector, nc.gpsimd, nc.sync
        wait, done, last, keep = M.wait, M.done, M.wait_last, M.keep

        raw = sb("raw", [P, RING, CHUNK])
        w_hi = sb("w_hi", [P, RING, CHUNK], F32R)
        w_lo = sb("w_lo", [P, RING, CHUNK], F32R)
        a_hi = sb("a_hi", [P, KT, S], F32R)
        a_lo = sb("a_lo", [P, KT, S], F32R)
        b_hi = sb("b_hi", [P, 2 * GT, S], F32R)
        b_lo = sb("b_lo", [P, 2 * GT, S], F32R)
        xres = sb("xres", [P, T, D])
        ident = sb("ident", [P, P])
        tri = sb("tri", [P, P])
        ones = sb("ones", [P, P])
        masks = sb("masks", [P, 2, S])
        cvals = sb("cvals", [P, 2])
        lc = sb("lc", [P, C_N])
        bc = sb("bc", [P, B_N])
        ARENA = 21 * 1024
        arena = sb("arena", [P, ARENA])
        stat = sb("stat", [P, 128])

        def cut(at, *shape):
            n = 1
            for v in shape:
                n *= v
            assert at + n <= ARENA, (at, n)
            ap = arena[:, at:at + n]
            if len(shape) == 2:
                return ap.rearrange("p (a b) -> p a b", b=shape[1])
            if len(shape) == 3:
                return ap.rearrange("p (a b c) -> p a b c", b=shape[1], c=shape[2])
            return ap

        pg = ctx.enter_context(nc.psum_tensor("pg", [P, 2, 2, 512], F32))
        pa = ctx.enter_context(nc.psum_tensor("pa", [P, 4, 512], F32))
        bias_dram = nc.dram_tensor("bias_scratch", (P, DH, 512), F32, kind="Internal").ap()

        for e in ("pe", "act", "dve", "pool"):
            M.add(e, sem(f"progress_{e}"), CREDIT)
            M.eng[e].sem_inc(M.handle[e], CREDIT)
        for e in ("pe", "act", "dve", "pool", "sp"):
            M.handle["holder_" + e] = sem(f"holder_{e}")
        landed = [sem(f"landed{s}") for s in range(RING)]
        M.add("rounded", sem("rounded"))
        M.add("split", sem("split"), RING)
        dve.sem_inc(M.handle["split"], RING)
        M.add("used", sem("used"))
        M.count["unit"] = 0
        M.add("out_a", sem("out_a"), 2)
        M.add("out_v", sem("out_v"), 2)
        act.sem_inc(M.handle["out_a"], 2)
        dve.sem_inc(M.handle["out_v"], 2)
        for n in ("ld_const", "ld_layer", "ld_bias"):
            M.add(n, sem(n))
        stored = sem("stored")

        def here(name):
            return M.value(name, M.count[name], M.stack)

        def stream():
            c = [0]

            def load(src, n, k, base):
                s = c[0] % RING
                num = base + c[0]
                M.wait_value("sp", "split", num + 1)
                dst = raw[:, s, 0:k * n].rearrange("p (k n) -> p k n", k=k)
                sp.dma_start(dst, src.rearrange("(k p) n -> p k n", p=P)).then_inc(landed[s], 32)
                c[0] += 1

            def units(w, col, n, base, chunks=UC):
                c0 = c[0]
                with sp.Fori(0, n) as u:
                    for j in range(chunks):
                        load(w[j * KC * P:(j + 1) * KC * P, bass.ds(u * UNIT + col, UNIT)], UNIT, KC,
                             base + u * chunks)
                assert chunks % RING == 0
                c[0] = c0 + n * chunks

            with sp.Fori(0, DEPTH) as l:
                lb = l * LAYER_CHUNKS
                win = w_in[bass.ds(l * D, D), :]
                units(win, 0, 8, lb)
                for j in range(2):
                    load(win[j * D // 2:(j + 1) * D // 2, W_IN - MH * MV - ROPE:W_IN - MH * MV],
                         ROPE, KT // 2, lb)
                units(win, 8 * UNIT, 2, lb)
                units(win, W_IN - MH * MV, 2, lb)
                uq = w_uq[bass.ds(l * QR, QR), :].rearrange("k (h c) -> k h c", h=MH)
                ukv = w_ukv[bass.ds(l * KVR, KVR), :].rearrange("k (h c) -> k h c", h=MH)

                def low_rank(w, c0, cn, h0, hn):
                    for j in range(2):
                        s = c[0] % RING
                        M.wait_value("sp", "split", lb + c[0] + 1)
                        for k in range(KC):
                            dst = raw[:, s, k * UNIT:(k + 1) * UNIT].rearrange("p (h c) -> p h c", h=hn)
                            r0 = (j * KC + k) * P
                            sp.dma_start(dst, w[r0:r0 + P, h0:h0 + hn, c0:c0 + cn]).then_inc(
                                landed[s], 16)
                        c[0] += 1

                low_rank(uq, NOPE, ROPE, 0, 8)
                for h0 in (0, 4):
                    low_rank(uq, 0, NOPE, h0, 4)
                for h0 in (0, 4):
                    low_rank(ukv, 0, NOPE, h0, 4)
                for h0 in (0, 4):
                    low_rank(ukv, NOPE, MV, h0, 4)
                for half in range(2):
                    units(w_out[bass.ds(l * D + half * (D // 2), D // 2), :], 0, 4, lb, UC // 2)
                assert c[0] == LAYER_CHUNKS, c[0]
            c[0] = DEPTH * LAYER_CHUNKS
            units(w_in_2[:, :], D + XBC + SH, 12, 0)
            units(w_in_2[:, :], 0, 12, 0)
            load(w_in_2[:, D + XBC:D + XBC + SH], SH, KT, 0)
            units(w_out_2[D:2 * D, :], 0, 4, 0)
            units(w_out_2[0:D, :], 0, 4, 0)

            def up(g, base):
                for j in range(UC):
                    load(w_up[j * KC * P:(j + 1) * KC * P, bass.ds(g, UNIT)], UNIT, KC, base)

            def down(g, base):
                c0 = c[0]
                with sp.Fori(0, D // UNIT // 2) as u:
                    for j in range(RING):
                        e, k = j // (GT // KC), j % (GT // KC)
                        load(w_down[bass.ds(g + k * KC * P, KC * P),
                                    bass.ds(u * (2 * UNIT) + e * UNIT, UNIT)], UNIT, KC, base + u * RING)
                c[0] = c0 + D // UNIT * (GT // KC)

            up(0, 0)
            c0 = c[0]
            with sp.Fori(0, GROUPS // 2 - 1) as i:
                f = i * (2 * UNIT)
                for b in range(2):
                    up(f + (b + 1) * UNIT, i * GROUP2_CHUNKS)
                    down(f + b * UNIT, i * GROUP2_CHUNKS)
            assert c[0] - c0 == GROUP2_CHUNKS
            c[0] = c0 + (GROUPS // 2 - 1) * GROUP2_CHUNKS
            up(FF - UNIT, 0)
            down(FF - 2 * UNIT, 0)
            down(FF - UNIT, 0)
            for j in range(RING):
                s = (c[0] + j) % RING
                M.wait_value("sp", "split", c[0] + j + 1)
                sp.dma_start(raw[:, s, :].rearrange("p (k n) -> p k n", k=KC),
                             w_down[0:KC * P, 0:UNIT].rearrange("(k p) n -> p k n", p=P)).then_inc(
                    landed[s], 32)

        for s in range(RING):
            M.handle[f"landed{s}"], M.count[f"landed{s}"] = landed[s], 0

        chunk_no = [0]

        def split_next():
            s = M.count["rounded"] % RING
            M.count[f"landed{s}"] += 32
            M.wait_value("act", f"landed{s}", here(f"landed{s}"), alone=False)
            if chunk_no[0]:
                M.wait_value("act", "used", here("used"), alone=False)
            done(act.copy(w_hi[:, s, :], raw[:, s, :]), "rounded")
            M.wait_value("dve", "rounded", here("rounded"), alone=False)
            done(dve.tensor_tensor(w_lo[:, s, :], raw[:, s, :], w_hi[:, s, :].bitcast(F32),
                                   ALU.subtract), "split")

        hosted = {"at": 0, "steps": {}}

        def host(steps):
            hosted["at"], hosted["steps"] = 0, steps
            for f in steps.get(-1, ()):
                f()

        def multiply(emit):
            s = M.count["used"] % RING
            M.wait_value("pe", "split", here("used") + RING + 1, alone=False)
            done(emit(s), "used")
            chunk_no[0] += 1
            split_next()
            for f in hosted["steps"].get(hosted["at"], ()):
                f()
            hosted["at"] += 1

        def column_chunk(s, k0, par, first, final, a0):
            ins = None
            for kk in range(KC):
                for f in range(4):
                    wh = w_hi[:, s, kk * UNIT + f * P:kk * UNIT + (f + 1) * P]
                    wl = w_lo[:, s, kk * UNIT + f * P:kk * UNIT + (f + 1) * P]
                    o = pg[:, par, f // 2, (f % 2) * S:(f % 2 + 1) * S]
                    ah, al = a_hi[:, a0 + k0 + kk, :], a_lo[:, a0 + k0 + kk, :]
                    for n, (l, r) in enumerate(((wh, ah), (wh, al), (wl, ah))):
                        ins = pe.matmul(o, l, r, start=(first and kk == 0 and f % 2 == 0 and n == 0),
                                        stop=(final and kk == KC - 1 and n == 2),
                                        skip_group_check=True)
            return ins

        def row_chunk(s, k0, par, first, final, a0, act_hi=None, act_lo=None, n=UNIT, kc=KC):
            ins = None
            for kk in range(kc):
                wh, wl = w_hi[:, s, kk * n:(kk + 1) * n], w_lo[:, s, kk * n:(kk + 1) * n]
                for t in range(T):
                    ah = (act_hi or a_hi)[:, a0 + k0 + kk, t * P:(t + 1) * P]
                    al = (act_lo or a_lo)[:, a0 + k0 + kk, t * P:(t + 1) * P]
                    for m, (l, r) in enumerate(((ah, wh), (ah, wl), (al, wh))):
                        ins = pe.matmul(pg[:, par, t, 0:n], l, r,
                                        start=(first and kk == 0 and m == 0),
                                        stop=(final and kk == kc - 1 and m == 2))
            return ins

        def unit(kind, evac, chunks=UC, a0=0, n=UNIT, kc=KC, hi=None, lo=None, after=None):
            par = M.count["unit"] % 2
            M.wait_value("pe", "out_a", here("unit") + 1)
            M.wait_value("pe", "out_v", here("unit") + 1)
            for j in range(chunks):
                if kind == "col":
                    def emit(s):
                        return column_chunk(s, j * kc, par, j == 0, j == chunks - 1, a0)
                else:
                    def emit(s):
                        return row_chunk(s, j * kc, par, j == 0, j == chunks - 1, a0, hi, lo, n, kc)
                multiply(emit)
            M.count["unit"] += 1
            complete = Mark("used", M.count["used"], list(M.stack))
            wait("act", complete)
            wait("dve", complete)
            a, v = evac(par)
            done(v, "out_v")
            done(a or after(), "out_a")

        def copy_rows(dst):
            def evac(par):
                return (act.copy(dst(0), pg[:, par, 0, :]), dve.tensor_copy(dst(1), pg[:, par, 1, :]))
            return evac

        def copy_cols(dst):
            def evac(par):
                return (act.copy(dst(0), pg[:, par, 0, :].rearrange("p (f s) -> p f s", f=2)),
                        dve.tensor_copy(dst(1), pg[:, par, 1, :].rearrange("p (f s) -> p f s", f=2)))
            return evac

        def fence(engines=("pe", "act", "dve", "pool"), on=("pe", "act", "dve", "pool"), gemm=True):
            for e in engines:
                for o in on + (("used", "out_a", "out_v") if gemm else ()):
                    M.wait_value(e, o, here(o))

        def all_wait():
            fence()

        def rstd(ss, dst, width):
            n = ss.shape[1]
            m = done(dve.tensor_scalar(ss, ss, 1.0 / width, EPS, ALU.mult, ALU.add), "dve")
            wait("pool", m)
            return done(pool.tensor_tensor(dst, ss, cvals[:, 1:2].to_broadcast([P, n]), ALU.pow), "pool")

        def transpose_split(src, ntiles, a0, gain=None, ready=None):
            for kp in range(ntiles // 2):
                b = kp % 2
                if ready:
                    wait("pe", ready)
                last("pe", f"xp_lo{b}")
                for kk in range(2):
                    for t in range(T):
                        k = 2 * kp + kk
                        ins = pe.transpose(pa[:, b, kk * S + t * P:kk * S + (t + 1) * P],
                                           src(t)[:, k * P:(k + 1) * P], ident[:, :])
                m = done(ins, "pe")
                wait("act", m)
                wait("dve", m)
                if gain is None:
                    dst_h = a_hi[:, a0 + 2 * kp:a0 + 2 * kp + 2, :]
                    dst_l = a_lo[:, a0 + 2 * kp:a0 + 2 * kp + 2, :]
                    ps = pa[:, b, :].rearrange("p (k s) -> p k s", k=2)
                    h = done(act.copy(dst_h, ps), "act")
                    wait("dve", h)
                    done(dve.tensor_tensor(dst_l, ps, dst_h.bitcast(F32), ALU.subtract), "dve",
                         f"xp_lo{b}")
                else:
                    for kk in range(2):
                        k = 2 * kp + kk
                        h = done(act.activation(a_hi[:, a0 + k, :], pa[:, b, kk * S:(kk + 1) * S], ACT.Copy,
                                                scale=gain[:, k:k + 1]), "act")
                    wait("dve", h)
                    for kk in range(2):
                        k = 2 * kp + kk
                        done(dve.scalar_tensor_tensor(a_lo[:, a0 + k, :], pa[:, b, kk * S:(kk + 1) * S],
                                                      gain[:, k:k + 1], a_hi[:, a0 + k, :].bitcast(F32),
                                                      ALU.mult, ALU.subtract), "dve", f"xp_lo{b}")

        def norm(src, width, tmp, st):
            for t in range(T):
                m = done(act.activation(tmp(t), src(t), ACT.Square, accum_out=stat[:, st + t:st + t + 1]),
                         "act")
            wait("dve", m)
            r = rstd(stat[:, st:st + T], stat[:, st + 2:st + 2 + T], width)
            wait("dve", r)
            for t in range(T):
                m = done(dve.tensor_scalar(tmp(t), src(t), stat[:, st + 2 + t:st + 3 + t], None, ALU.mult),
                         "dve")
            return m

        ROWS = ((0, P, P), (P, 3 * P, 0))

        def head(e, stage, score, maps, mask, scale, weights, pt, v, finish, turned=None, dest=None):
            base = 64 + 32 * e
            n = 2 * maps
            mx, neg, den, rec = (stat[:, base + n * i:base + n * (i + 1)] for i in range(4))
            box = {}

            def stage_step():
                last("pool", "scored")
                last("pool", "maxed")
                box["staged"] = stage()

            def score_step():
                wait("pe", box["staged"])
                last("pe", "maxed")
                m = done(score(), "pe", "scored")
                wait("dve", m)
                last("dve", f"turned{e}")
                for mm in range(maps):
                    for i, (a, b, m0) in enumerate(ROWS):
                        k = 2 * mm + i
                        m = done(dve.tensor_tensor_reduce(
                            sc[e][:, mm, a:b], pa[:, mm, a:b], mask[:, m0:m0 + b - a], scale, 3.0 * NEG,
                            ALU.add, ALU.max, mx[:, k:k + 1]), "dve", "maxed")
                wait("dve", m)
                m = done(dve.tensor_scalar(neg, mx, -1.0, None, ALU.mult), "dve")
                wait("act", m)
                for mm in range(maps):
                    for i, (a, b, _) in enumerate(ROWS):
                        k = 2 * mm + i
                        m = done(act.activation(sc[e][:, mm, a:b], sc[e][:, mm, a:b], ACT.Exp,
                                                bias=neg[:, k:k + 1], accum_out=den[:, k:k + 1]), "act")
                wait("dve", m)
                box["rec"] = done(dve.reciprocal(rec, den), "dve")
                box["tile"], box["weighed"] = weights(e, m, rec, box["rec"])

            def turn_step():
                wait("pe", box["weighed"])
                last("pe", "pt_copied")
                for b in range(3):
                    ins = pe.transpose(pa[:, 2, b * P:(b + 1) * P], box["tile"][:, b * P:(b + 1) * P],
                                       ident[:, :])
                m = done(ins, "pe", f"turned{e}")
                wait("act", m)
                last("act", "applied")
                box["pt"] = done(act.copy(pt, pa[:, 2, 0:3 * P]), "act", "pt_copied")

            def apply_step():
                wait("pe", box["pt"])
                last("pe", "finished")
                last("pe", "moved")
                o = pa[:, 3, 0:2 * P].rearrange("p (t v) -> p t v", t=2)
                pe.matmul(o[:, 0, :], pt[:, 0:P], v(0), start=True, stop=True)
                pe.matmul(o[:, 1, :], pt[:, P:2 * P], v(0), start=True, stop=False)
                m = done(pe.matmul(o[:, 1, :], pt[:, 2 * P:3 * P], v(1), start=False, stop=True), "pe",
                         "applied")
                if turned is not None:
                    last("dve", "out_turned")
                box["finished"] = keep("finished", finish(e, o, rec, m, box["rec"]))

            def move_step():
                wait("pe", box["finished"])
                for t in range(T):
                    ins = pe.transpose(pa[:, 3, S + t * P:S + (t + 1) * P], turned[:, t, :], ident[:, :])
                m = done(ins, "pe", "out_turned")
                wait("act", m)
                m = done(act.copy(dest[0], pa[:, 3, S:2 * S]), "act")
                wait("dve", m)
                done(dve.tensor_tensor(dest[1], pa[:, 3, S:2 * S], dest[0].bitcast(F32), ALU.subtract),
                     "dve", "moved")

            return stage_step, score_step, turn_step, apply_step, move_step

        def schedule(heads, at):
            steps = {-1: [heads[0][0]]}
            for i, (h, when) in enumerate(zip(heads, at)):
                for rank, slot in enumerate(when, 1):
                    fs = steps.setdefault(slot, [])
                    fs.append(h[rank])
                    if rank == 1 and i + 1 < len(heads):
                        fs.append(heads[i + 1][0])
            return steps

        def flat(ap):
            return ap.rearrange("p a s -> p (a s)")

        sp.dma_start(xres[:, :, :], x.rearrange("(t p) d -> p t d", p=P)).then_inc(M.handle["ld_const"], 16)
        for dst, src in ((ident[:, :], c_ident), (tri[:, :], c_tri), (masks[:, :, :], c_mask)):
            sp.dma_start(dst, src).then_inc(M.handle["ld_const"], 16)
        sp.dma_start(bc[:, :], block_c).then_inc(M.handle["ld_const"], 16)
        bucket = cut(0, 512)
        table = cut(512, DH)
        rope = sb("rope", [P, T, 2, ROPE])
        sp.dma_start(bucket[0:33, :], c_bucket).then_inc(M.handle["ld_const"], 16)
        sp.dma_start(table[0:32, :], rel_table).then_inc(M.handle["ld_const"], 16)
        sp.dma_start(rope[:, :, :, :], c_rope).then_inc(M.handle["ld_const"], 16)
        M.count["ld_const"] = 8 * 16
        stream()
        done(dve.memset(ones[:, :], 1.0), "dve")
        done(dve.memset(cvals[:, 0:1], EPS), "dve")
        done(dve.memset(cvals[:, 1:2], -0.5), "dve")
        m_tab = done(dve.memset(table[32:33, :], 1.0), "dve")
        for e in ("pe", "act", "dve", "pool"):
            M.eng[e].wait_ge(M.handle["ld_const"], M.count["ld_const"])
            wait(e, m_tab)
        for _ in range(RING):
            split_next()

        bias = cut(19456, DH, S)
        vec = cut(1024, DH, 512)
        vmarks = {}
        for h in range(DH):
            if h >= 2:
                wait("pe", vmarks[h - 2])
            m = done(pe.matmul(pa[:, h % 2, :], table[0:33, h:h + 1].to_broadcast([33, P]),
                               bucket[0:33, :], start=True, stop=True), "pe")
            wait("act", m)
            vmarks[h] = done(act.copy(vec[:, h, :], pa[:, h % 2, :]), "act")
        wait("pool", vmarks[DH - 1])
        pool.dma_start(bias_dram, vec[:, :, :]).then_inc(M.handle["ld_bias"], 16)
        M.wait_value("pool", "ld_bias", 16)
        vecs = bias_dram.rearrange("p h j -> (p h j)")
        skew = bass.AP(tensor=vecs.tensor, offset=vecs.offset + P - 1,
                       ap=[[DH * 512 - 1, P], [512, DH], [1, S]])
        pool.dma_start(bias[:, :, :], skew).then_inc(M.handle["ld_bias"], 16)
        M.count["ld_bias"] = 32
        for e in ("pe", "act", "dve", "pool"):
            M.eng[e].wait_ge(M.handle["ld_bias"], 32)
        all_wait()

        tok = cut(0, T, 8 * UNIT)
        qkT = cut(8 * 1024, 16, S)
        qrT = cut(12 * 1024, 4, S)
        krT = cut(13 * 1024, S)
        kr = cut(13 * 1024 + 256, T, ROPE)
        krd = cut(13 * 1024 + 512, T, 2 * ROPE)
        tmp = cut(8 * 1024, T, D)
        rt = cut(14 * 1024, T, 1152)
        q_s, k_s, b_st = (cut(16640 + S * i, S) for i in range(3))
        sc = [cut(17408, 2, 3 * P), cut(14 * 1024, 2, 3 * P)]
        w_s = cut(18176, 3 * P)
        pt_s = cut(18560, 3 * P)
        og = cut(18944, T, P)
        junk = cut(19200, P)
        lamt = cut(19200, 2, 64)
        with M.loop("layer", DEPTH) as l:
            all_wait()
            pool.dma_start(lc[:, :], layer_c[bass.ds(l * P, P), :]).then_inc(M.handle["ld_layer"], 16)
            M.count["ld_layer"] += 16
            for e in ("act", "dve"):
                M.wait_value(e, "ld_layer", here("ld_layer"))
            for i in range(2):
                m = done(dve.tensor_tensor_reduce(lamt[:, i, :], lc[:, C_LAM + 128 * i:C_LAM + 128 * i + 64],
                                                  lc[:, C_LAM + 128 * i + 64:C_LAM + 128 * i + 128], 1.0,
                                                  0.0, ALU.mult, ALU.add, stat[:, 60 + i:61 + i]), "dve")
            wait("act", m)
            m = done(act.activation(stat[:, 60:62], stat[:, 60:62], ACT.Exp), "act")
            wait("dve", m)
            m = done(dve.tensor_tensor(stat[:, 62:63], stat[:, 61:62], stat[:, 60:61], ALU.subtract), "dve")
            wait("dve", m)
            done(dve.tensor_tensor(stat[:, 62:63], stat[:, 62:63], lc[:, C_INIT:C_INIT + 1],
                                   ALU.subtract), "dve", "neglam")

            m = norm(lambda t: xres[:, t, :], D, lambda t: tmp[:, t, :], 0)
            transpose_split(lambda t: tmp[:, t, :], KT, 0, lc[:, C_G:C_G + KT], m)
            all_wait()
            with M.loop("qk", 2) as u:
                for e in range(2):
                    unit("col", copy_cols(lambda half: qkT[:, bass.ds(u * 8 + (4 * e + 2 * half), 2), :]))
            with M.loop("v_za", 2) as u:
                for e in range(2):
                    unit("row", copy_rows(lambda t: tok[:, t, bass.ds(u * (2 * UNIT) + e * UNIT, UNIT)]))
            unit("row", lambda par: (act.copy(kr[:, 0, :], pg[:, par, 0, 0:ROPE]),
                                     dve.tensor_copy(kr[:, 1, :], pg[:, par, 1, 0:ROPE])),
                 chunks=2, n=ROPE, kc=KT // 2)
            fence(("act", "pool"))
            for t in range(T):
                m = done(act.activation(tok[:, t, 1024:2048], tok[:, t, 1024:2048], ACT.Silu), "act")
            fence(("dve",))
            for t in range(T):
                za = tok[:, t, 1024:2048].rearrange("p (h v) -> p h v", h=DH)
                g = lc[:, C_SUB:C_SUB + DV].unsqueeze(1).to_broadcast([P, DH, DV])
                m = done(dve.scalar_tensor_tensor(za, za, lc[:, C_INIT + 1:C_INIT + 2], g,
                                                  ALU.mult, ALU.mult), "dve")
            wait("dve", m)

            def diff_head(h, e):
                def stage():
                    done(pool.tensor_copy(q_s, flat(qkT[:, bass.ds(h, 1), :])), "pool")
                    done(pool.tensor_copy(k_s, flat(qkT[:, bass.ds(h + DH, 1), :])), "pool")
                    return done(pool.tensor_copy(b_st, flat(bias[:, bass.ds(h, 1), :])), "pool")

                def score():
                    for mm in range(2):
                        r = slice(mm * DQK, (mm + 1) * DQK)
                        pe.matmul(pa[:, mm, 0:P], q_s[r, 0:P], k_s[r, 0:P], start=True, stop=True)
                        ins = pe.matmul(pa[:, mm, P:3 * P], q_s[r, P:S], k_s[r, 0:S], start=True,
                                        stop=True)
                    return ins

                def weights(_, m, rec, rm):
                    wait("dve", rm)
                    m = done(dve.tensor_scalar(rec[:, 2:4], rec[:, 2:4], stat[:, 62:63], None, ALU.mult),
                             "dve")
                    for t, (a, b, _) in enumerate(ROWS):
                        m2 = done(dve.tensor_scalar(sc[0][:, 0, a:b], sc[0][:, 0, a:b], rec[:, t:t + 1],
                                                    None, ALU.mult), "dve")
                    wait("dve", m2)
                    last("dve", "turned0")
                    for t, (a, b, _) in enumerate(ROWS):
                        m = done(dve.scalar_tensor_tensor(w_s[:, a:b], sc[0][:, 1, a:b],
                                                          rec[:, 2 + t:3 + t], sc[0][:, 0, a:b],
                                                          ALU.mult, ALU.add), "dve")
                    return w_s, m

                def finish(_, o, rec, m, rm):
                    ss, rs = stat[:, 80:82], stat[:, 82:84]
                    wait("act", m)
                    for t in range(T):
                        last("act", "junk")
                        m = done(act.activation(junk, o[:, t, :], ACT.Square, accum_out=ss[:, t:t + 1]),
                                 "act", "junk")
                    wait("dve", m)
                    m = rstd(ss, rs, DV)
                    wait("dve", m)
                    for t in range(T):
                        m = done(dve.scalar_tensor_tensor(og[:, t, :], o[:, t, :], rs[:, t:t + 1],
                                                          tok[:, t, bass.ds(h * DV + 1024, DV)],
                                                          ALU.mult, ALU.mult), "dve")
                    return m

                return head(0, stage, score, 2, b_st, DQK ** -0.5, weights, pt_s,
                            lambda t: tok[:, t, bass.ds(h * DV, DV)], finish, og,
                            (flat(b_hi[:, bass.ds(h, 1), :]), flat(b_lo[:, bass.ds(h, 1), :])))

            fence(("pe",), gemm=False)
            with M.loop("c_zb", 2) as u:
                host(schedule([diff_head(u * 4 + e, e) for e in range(4)],
                              [(0, 3, 4, 6), (4, 7, 8, 10), (7, 10, 11, 13), (11, 14, 15, 15)]))
                for e in range(2):
                    unit("row", copy_rows(lambda t: tok[:, t, bass.ds(u * (2 * UNIT) + (2048 + e * UNIT),
                                                                      UNIT)]))
            host({})
            fence()

            for i in range(2):
                m = norm(lambda t: tok[:, t, 2048 + UNIT * i:2048 + UNIT * (i + 1)], QR,
                         lambda t: tmp[:, t, UNIT * i:UNIT * (i + 1)], 32 + 4 * i)
            for i, gc in ((0, C_QG), (1, C_KVG)):
                transpose_split(lambda t: tmp[:, t, UNIT * i:UNIT * (i + 1)], 4, 4 * i,
                                lc[:, gc:gc + 4], m)
            fence()
            unit("row", copy_rows(lambda t: tok[:, t, 2048:2048 + UNIT]), chunks=2, a0=0)
            for i in range(4):
                unit("col", copy_cols(lambda half: qkT[:, 4 * i + 2 * half:4 * i + 2 * half + 2, :]),
                     chunks=2, a0=4 * (i // 2))
            unit("row", copy_rows(lambda t: tok[:, t, 0:UNIT]), chunks=2, a0=4)
            fence(("act", "dve"))
            for t in range(T):
                cs = rope[:, t, 0, :]
                sn = rope[:, t, 1, :]
                half = ROPE // 2
                for src, dst, heads in ((tok[:, t, 2048:2560], rt[:, t, 0:512], MH),
                                        (kr[:, t, :], rt[:, t, 512:576], 1)):
                    s3 = src.rearrange("p (h c) -> p h c", h=heads)
                    d3 = dst.rearrange("p (h c) -> p h c", h=heads)
                    rot = rt[:, t, 576:576 + ROPE * heads].rearrange("p (h c) -> p h c", h=heads)

                    def bcast(v):
                        return v.unsqueeze(1).to_broadcast([P, heads, v.shape[-1]])
                    last("dve", "rope_add")
                    done(dve.tensor_tensor(rot[:, :, 0:half], s3[:, :, half:ROPE], bcast(sn[:, 0:half]),
                                           ALU.mult), "dve")
                    done(dve.tensor_tensor(rot[:, :, half:ROPE], s3[:, :, 0:half], bcast(sn[:, half:ROPE]),
                                           ALU.mult), "dve")
                    m = done(dve.tensor_tensor(d3, s3, bcast(cs), ALU.mult), "dve")
                    wait("dve", m)
                    m = done(dve.tensor_tensor(d3, d3, rot, ALU.add), "dve", "rope_add")
                wait("dve", m)
                for i in range(2):
                    m = done(dve.tensor_copy(krd[:, t, i * ROPE:(i + 1) * ROPE], rt[:, t, 512:576]), "dve")
            unit("row", copy_rows(lambda t: tok[:, t, UNIT:2 * UNIT]), chunks=2, a0=4)
            wait("pe", m)
            for i in range(4):
                for t in range(T):
                    ins = pe.transpose(pa[:, i // 2, (i % 2) * S + t * P:(i % 2) * S + (t + 1) * P],
                                       rt[:, t, i * P:(i + 1) * P], ident[:, :])
            for t in range(T):
                ins = pe.transpose(pa[:, 2, t * P:(t + 1) * P], krd[:, t, :], ident[:, :])
            m = done(ins, "pe")
            wait("act", m)
            wait("dve", m)
            done(act.copy(qrT[:, 0:2, :], pa[:, 0, :].rearrange("p (a s) -> p a s", a=2)), "act")
            done(dve.tensor_copy(qrT[:, 2:4, :], pa[:, 1, :].rearrange("p (a s) -> p a s", a=2)), "dve")
            done(act.copy(krT, pa[:, 2, 0:S]), "act")
            all_wait()

            for t in range(T):
                done(act.activation(tok[:, t, 3072:4096], tok[:, t, 3072:4096], ACT.Silu), "act")

            def latent_head(hp, e):
                r = slice((e % 2) * ROPE, (e % 2 + 1) * ROPE)

                def stage():
                    if e % 2 == 0:
                        done(pool.tensor_copy(b_st, flat(qrT[:, bass.ds(hp * 2 + e // 2, 1), :])), "pool")
                    return done(pool.tensor_copy(q_s, flat(qkT[:, bass.ds(hp * 4 + e, 1), :])), "pool")

                def score():
                    k_h = flat(qkT[:, bass.ds(hp * 4 + (MH + e), 1), :])
                    for (a, b, _), qc, nk in zip(ROWS, (slice(0, P), slice(P, S)), (P, S)):
                        pe.matmul(pa[:, 0, a:b], q_s[:, qc], k_h[:, 0:nk], start=True, stop=False)
                        ins = pe.matmul(pa[:, 0, a:b], b_st[r, qc], krT[r, 0:nk], start=False, stop=True)
                    return ins

                def finish(_, o, rec, m, rm):
                    wait("dve", m)
                    for t in range(T):
                        m = done(dve.scalar_tensor_tensor(
                            og[:, t, :], o[:, t, :], rec[:, t:t + 1],
                            tok[:, t, bass.ds(hp * (4 * MV) + (e * MV + 3072), MV)], ALU.mult, ALU.mult),
                            "dve")
                    return m

                return head(e % 2, stage, score, 1, masks[:, 0, :], (NOPE + ROPE) ** -0.5,
                            lambda _, m, rec, rm: (sc[e % 2][:, 0, :], m), pt_s,
                            lambda t: tok[:, t, bass.ds(hp * (4 * MV) + e * MV, MV)], finish, og,
                            (flat(a_hi[:, bass.ds(hp * 4 + (8 + e), 1), :]),
                             flat(a_lo[:, bass.ds(hp * 4 + (8 + e), 1), :])))

            def add_x(u, e):
                def evac(par):
                    xs = [xres[:, t, bass.ds(u * (2 * UNIT) + e * UNIT, UNIT)] for t in range(T)]
                    done(dve.tensor_tensor(xs[0], xs[0], pg[:, par, 0, :], ALU.add), "dve")
                    return act.nop(), dve.tensor_tensor(xs[1], xs[1], pg[:, par, 1, :], ALU.add)
                return evac

            fence()
            with M.loop("out_diff", 2) as u:
                host(schedule([latent_head(u, e) for e in range(4)],
                              [(0, 2, 3, 4), (1, 3, 4, 5), (3, 5, 6, 7), (4, 6, 7, 7)]))
                for e in range(2):
                    unit("row", add_x(u, e), chunks=UC // 2, hi=b_hi, lo=b_lo)
            host({})
            fence(("pe",), gemm=False)
            with M.loop("out_latent", 2) as u:
                for e in range(2):
                    unit("row", add_x(u, e), chunks=UC // 2, a0=8)

        all_wait()
        rows = cut(18 * 1024, D)

        def load_row(i):
            M.wait_value("pool", "dve", here("dve"))
            pool.dma_start(rows, rows_c[i * P:(i + 1) * P, :]).then_inc(M.handle["ld_layer"], 16)
            M.count["ld_layer"] += 16
            M.wait_value("dve", "ld_layer", here("ld_layer"))

        load_row(0)
        tmp2 = cut(8 * 1024, T, D)
        m = norm(lambda t: xres[:, t, :], D, lambda t: tmp2[:, t, :], 0)
        wait("dve", m)
        for t in range(T):
            m = done(dve.tensor_tensor(xres[:, t, :], tmp2[:, t, :], rows, ALU.mult), "dve")
        all_wait()

        z = cut(0, T, D)
        qkT2 = cut(4 * 1024, 32, S)
        v2t = cut(12 * 1024, T, D)
        m = norm(lambda t: xres[:, t, :], D, lambda t: tmp2[:, t, :], 0)
        transpose_split(lambda t: tmp2[:, t, :], KT, 0, bc[:, B_PRE:B_PRE + KT], m)
        all_wait()
        with M.loop("qk2", 4) as u:
            for e in range(2):
                unit("col", copy_cols(lambda half: qkT2[:, bass.ds(u * 8 + (4 * e + 2 * half), 2), :]))
        with M.loop("v2", 2) as u:
            for e in range(2):
                unit("row", copy_rows(lambda t: v2t[:, t, bass.ds(u * (2 * UNIT) + e * UNIT, UNIT)]))
        sc[0], sc[1] = cut(17408, 1, 3 * P), cut(17408 + 384, 1, 3 * P)

        def dilated_head(hp, e):
            def stage():
                return done(pool.tensor_copy(q_s, flat(qkT2[:, bass.ds(hp * 8 + e, 1), :])), "pool")

            def score():
                k_h = flat(qkT2[:, bass.ds(hp * 8 + (AH + e), 1), :])
                pe.matmul(pa[:, 0, 0:P], q_s[:, 0:P], k_h[:, 0:P], start=True, stop=True)
                return pe.matmul(pa[:, 0, P:3 * P], q_s[:, P:S], k_h[:, 0:S], start=True, stop=True)

            def finish(_, o, rec, m, rm):
                wait("dve", m)
                for t in range(T):
                    m = done(dve.tensor_scalar(v2t[:, t, bass.ds(hp * (8 * AD) + e * AD, AD)], o[:, t, :],
                                               rec[:, t:t + 1], None, ALU.mult), "dve")
                return m

            return head(e % 2, stage, score, 1, masks[:, 1, :], AD ** -0.5,
                        lambda _, m, rec, rm: (sc[e % 2][:, 0, :], m), pt_s,
                        lambda t: v2t[:, t, bass.ds(hp * (8 * AD) + e * AD, AD)], finish)

        fence(("act", "dve", "pool"))
        fence(("pe",), gemm=False)
        with M.loop("z", 2) as u:
            host(schedule([dilated_head(u, e) for e in range(8)],
                          [(k, min(k + 2, 15), min(k + 3, 15)) for k in (0, 2, 4, 6, 8, 10, 11, 13)]))
            for e in range(2):
                unit("row", copy_rows(lambda t: z[:, t, bass.ds(u * (2 * UNIT) + e * UNIT, UNIT)]))
        host({})
        fence(("act", "dve", "pool"))
        for t in range(T):
            done(act.activation(z[:, t, :], z[:, t, :], ACT.Silu), "act")

        xbc = cut(4 * 1024, 32, S)

        def conv(u, e):
            def evac(par):
                def tap(f, j):
                    return bc[:, bass.ds(u * 32 + (B_CW + (4 * e + f) * 4 + j), 1)]

                def dst(f, a=0, b=S):
                    return flat(xbc[:, bass.ds(u * 8 + (4 * e + f), 1), a:b])
                ps = [pg[:, par, f // 2, (f % 2) * S:(f % 2 + 1) * S] for f in range(4)]
                for f in range(4):
                    cb = bc[:, bass.ds(u * 8 + (B_CB + 4 * e + f), 1)]
                    m = done(dve.tensor_scalar(dst(f), ps[f], tap(f, 3), cb, ALU.mult, ALU.add), "dve")
                for j in (1, 2, 3):
                    wait("dve", m)
                    for f in range(4):
                        v = dve.scalar_tensor_tensor(dst(f, j), ps[f][:, 0:S - j], tap(f, 3 - j),
                                                     dst(f, j), ALU.mult, ALU.add)
                        if not (j == 3 and f == 3):
                            m = done(v, "dve")
                return None, v
            return evac

        def silu_tiles(u, e):
            wait("act", Mark("out_v", M.count["out_v"], list(M.stack)))
            t4 = xbc[:, bass.ds(u * 8 + 4 * e, 4), :]
            return act.activation(t4, t4, ACT.Silu)

        with M.loop("xbc", 4) as u:
            for e in range(2):
                unit("col", conv(u, e), after=lambda: silu_tiles(u, e))
        dt = cut(16 * 1024, T, SH)
        unit("row", lambda par: (act.copy(dt[:, 0, :], pg[:, par, 0, 0:SH]),
                                 dve.tensor_copy(dt[:, 1, :], pg[:, par, 1, 0:SH])),
             chunks=1, n=SH, kc=KT)
        fence()

        A = 16 * 1024 + 64
        n2 = T * SH
        v1, v2, s1, s2 = (cut(A + n2 * i, n2) for i in range(4))
        dtf = dt.rearrange("p t h -> p (t h)")
        dA = cut(A + 4 * n2, T, SH)
        acs = cut(A + 5 * n2, 3, SH)
        aneg = cut(A + 7 * n2, SH)

        def chain(ins):
            m = done(ins, "dve")
            wait("dve", m)
            return m

        chain(dve.tensor_tensor(dt, dt, bc[:, B_DTB:B_DTB + SH].unsqueeze(1).to_broadcast([P, T, SH]),
                                ALU.add))
        chain(dve.tensor_scalar(v1, dtf, -1.0, None, ALU.mult))
        m = chain(dve.tensor_tensor(v1, v1, dtf, ALU.min))
        wait("act", m)
        done(act.activation(aneg, bc[:, B_AL:B_AL + SH], ACT.Exp), "act")
        m = done(act.activation(v1, v1, ACT.Exp), "act")
        wait("dve", m)
        chain(dve.tensor_scalar(v2, v1, 2.0, None, ALU.add))
        chain(dve.reciprocal(v2, v2))
        chain(dve.tensor_tensor(s1, v1, v2, ALU.mult))
        chain(dve.tensor_tensor(s2, s1, s1, ALU.mult))
        chain(dve.tensor_scalar(v1, s2, 1.0 / 17, 1.0 / 15, ALU.mult, ALU.add))
        for k in (13, 11, 9, 7, 5, 3, 1):
            chain(dve.tensor_tensor(v1, v1, s2, ALU.mult))
            chain(dve.tensor_scalar(v1, v1, 1.0 / k, None, ALU.add))
        chain(dve.tensor_tensor(v1, v1, s1, ALU.mult))
        chain(dve.tensor_scalar(dtf, dtf, 0.0, None, ALU.max))
        chain(dve.scalar_tensor_tensor(dtf, v1, 2.0, dtf, ALU.mult, ALU.add))
        m = chain(dve.scalar_tensor_tensor(dA, dt, -1.0, aneg.unsqueeze(1).to_broadcast([P, T, SH]),
                                           ALU.mult, ALU.mult))
        wait("pe", m)
        pe.matmul(pa[:, 3, 0:SH], tri[:, :], dA[:, 0, :], start=True, stop=True)
        pe.matmul(pa[:, 3, SH:2 * SH], tri[:, :], dA[:, 1, :], start=True, stop=True)
        m = done(pe.matmul(pa[:, 3, 2 * SH:3 * SH], ones[:, :], dA[:, 0, :], start=True, stop=True), "pe")
        wait("dve", m)
        done(dve.tensor_copy(acs[:, 0, :], pa[:, 3, 0:SH]), "dve")
        m = chain(dve.tensor_copy(acs[:, 2, :], pa[:, 3, SH:2 * SH]))
        done(dve.tensor_tensor(acs[:, 1, :], acs[:, 0, :], pa[:, 3, 2 * SH:3 * SH], ALU.subtract), "dve")
        transpose_split(lambda t: v2t[:, t, :], KT, 0)
        fence()
        xs = cut(12 * 1024, T, D)
        for i in range(8):
            b = i % 4
            last("pe", f"xs_out{b}")
            for kk in range(2):
                for t in range(T):
                    ins = pe.transpose(pa[:, b, (t * 2 + kk) * P:(t * 2 + kk + 1) * P],
                                       xbc[:, 2 * i + kk, t * P:(t + 1) * P], ident[:, :])
            m = done(ins, "pe")
            e, fn = (("act", act.copy), ("dve", dve.tensor_copy))[i % 2]
            wait(e, m)
            done(fn(xs[:, :, 2 * P * i:2 * P * (i + 1)], pa[:, b, :].rearrange("p (t c) -> p t c", t=T)), e,
                 f"xs_out{b}")
        all_wait()

        G = 17 * 1024
        b_s = cut(G, S)
        c_m = cut(G + 256, 3 * P)
        da_s = cut(G + 640, T, HPG)
        ac_s = cut(G + 656, 3, HPG)
        dec = cut(G + 1024, HPG, 3 * P)
        xdt = cut(G + 2560, T, HPG, HD)
        yb = cut(G + 3072, T, HPG * HD)
        ysq = cut(G + 3584, HPG * HD)
        mix = cut(4 * 1024, T, D)

        def scan_group(g):
            x_g = xs[:, :, bass.ds(g * (HPG * HD), HPG * HD)].rearrange("p t (r c) -> p t r c", r=HPG)
            box = {}

            def stage():
                last("pool", "scored")
                last("pool", "decayed")
                done(pool.tensor_copy(b_s, flat(xbc[:, bass.ds(g + 16, 1), :])), "pool")
                done(pool.tensor_copy(da_s, dA[:, :, bass.ds(g * HPG, HPG)]), "pool")
                box["staged"] = done(pool.tensor_copy(ac_s, acs[:, :, bass.ds(g * HPG, HPG)]), "pool")

            def score():
                wait("pe", box["staged"])
                last("pe", "decayed")
                c_g = flat(xbc[:, bass.ds(g + 24, 1), :])
                pe.matmul(pa[:, 0, 0:S], b_s[:, 0:P], c_g[:, 0:S], start=True, stop=True)
                m = done(pe.matmul(pa[:, 0, S:S + P], b_s[:, P:S], c_g[:, P:S], start=True, stop=True),
                         "pe")
                wait("dve", m)
                last("dve", "multiplied")
                done(dve.tensor_tensor(c_m[:, 0:P], pa[:, 0, 0:P], tri[:, :], ALU.mult), "dve")
                done(dve.tensor_copy(c_m[:, P:S], pa[:, 0, P:S]), "dve")
                done(dve.tensor_tensor(c_m[:, S:S + P], pa[:, 0, S:S + P], tri[:, :], ALU.mult), "dve")
                for r in range(HPG):
                    for t in range(T):
                        ins = pe.matmul(pa[:, 1 + r // 2, (r % 2) * S + t * P:(r % 2) * S + (t + 1) * P],
                                        da_s[:, t, r:r + 1].to_broadcast([P, P]), tri[:, :],
                                        start=True, stop=True)
                m = done(ins, "pe", "scored")
                wait("dve", m)
                last("dve", "applied")
                for r in range(HPG):
                    for blk, t in ((0, 0), (1, 1), (2, 1)):
                        m = done(dve.tensor_scalar(
                            dec[:, r, blk * P:(blk + 1) * P],
                            pa[:, 1 + r // 2, (r % 2) * S + t * P:(r % 2) * S + (t + 1) * P],
                            ac_s[:, blk, r:r + 1], 0.0, ALU.subtract, ALU.min), "dve", "decayed")
                wait("act", m)
                m = done(act.activation(dec, dec, ACT.Exp), "act")
                wait("dve", m)
                box["m"] = done(dve.tensor_tensor(dec, dec, c_m.unsqueeze(1).to_broadcast([P, HPG, 3 * P]),
                                                  ALU.mult), "dve", "multiplied")
                last("pool", "applied")
                last("pool", "gated")
                for t in range(T):
                    dt_g = dt[:, t, bass.ds(g * HPG, HPG)].unsqueeze(2).to_broadcast([P, HPG, HD])
                    done(pool.tensor_tensor(xdt[:, t, :, :], x_g[:, t, :, :], dt_g, ALU.mult), "pool")
                for t in range(T):
                    ds_g = bc[:, bass.ds(g * HPG + B_DS, HPG)].unsqueeze(2).to_broadcast([P, HPG, HD])
                    yt = yb[:, t, :].rearrange("p (r c) -> p r c", r=HPG)
                    box["x"] = done(pool.tensor_tensor(yt, x_g[:, t, :, :], ds_g, ALU.mult), "pool")

            def apply():
                wait("pe", box["m"])
                wait("pe", box["x"])
                last("pe", "summed")
                for r in range(HPG):
                    o = [pa[:, 3, t * S + r * HD:t * S + (r + 1) * HD] for t in range(T)]
                    pe.matmul(o[0], dec[:, r, 0:P], xdt[:, 0, r, :], start=True, stop=True)
                    pe.matmul(o[1], dec[:, r, P:2 * P], xdt[:, 0, r, :], start=True, stop=False)
                    ins = pe.matmul(o[1], dec[:, r, 2 * P:3 * P], xdt[:, 1, r, :], start=False, stop=True)
                m = done(ins, "pe", "applied")
                wait("dve", m)
                m = done(dve.tensor_tensor(yb, yb, pa[:, 3, :].rearrange("p (t c) -> p t c", t=T),
                                           ALU.add), "dve", "summed")
                wait("dve", m)
                zg = z[:, :, bass.ds(g * (HPG * HD), HPG * HD)]
                m = done(dve.tensor_tensor(yb, yb, zg, ALU.mult), "dve")
                wait("act", m)
                for t in range(T):
                    last("act", "junk")
                    m = done(act.activation(ysq, yb[:, t, :], ACT.Square, accum_out=stat[:, 28 + t:29 + t]),
                             "act", "junk")
                wait("dve", m)
                m = rstd(stat[:, 28:30], stat[:, 30:32], HPG * HD)
                wait("dve", m)
                for t in range(T):
                    done(dve.tensor_scalar(zg[:, t, :], yb[:, t, :], stat[:, 30 + t:31 + t], None,
                                           ALU.mult), "dve", "gated")

            return stage, score, apply

        def put(dst, u, e, add):
            def evac(par):
                d = [dst[:, t, bass.ds(u * (2 * UNIT) + e * UNIT, UNIT)] for t in range(T)]
                if not add:
                    return act.copy(d[0], pg[:, par, 0, :]), dve.tensor_copy(d[1], pg[:, par, 1, :])
                done(dve.tensor_tensor(d[0], d[0], pg[:, par, 0, :], ALU.add), "dve")
                return act.nop(), dve.tensor_tensor(d[1], d[1], pg[:, par, 1, :], ALU.add)
            return evac

        fence()
        with M.loop("out_att", 2) as u:
            g4 = [scan_group(u * 4 + e) for e in range(4)]
            host({-1: [g4[0][0]], 0: [g4[0][1], g4[1][0]], 4: [g4[0][2], g4[1][1], g4[2][0]],
                  8: [g4[1][2], g4[2][1], g4[3][0]], 11: [g4[2][2]], 12: [g4[3][1]], 15: [g4[3][2]]})
            for e in range(2):
                unit("row", put(mix, u, e, False))
        host({})
        fence()
        transpose_split(lambda t: z[:, t, :], KT, 0, bc[:, B_SSM:B_SSM + KT])
        fence()
        with M.loop("out_ssm", 2) as u:
            for e in range(2):
                unit("row", put(mix, u, e, True))
        fence()

        def add_normed(src, i):
            load_row(i)
            m = norm(lambda t: src[:, t, :], D, lambda t: tmp2[:, t, :], 0)
            for t in range(T):
                wait("dve", m)
                m = done(dve.tensor_tensor(tmp2[:, t, :], tmp2[:, t, :], rows, ALU.mult), "dve")
            for t in range(T):
                wait("dve", m)
                m = done(dve.tensor_tensor(xres[:, t, :], xres[:, t, :], tmp2[:, t, :], ALU.add), "dve")
            all_wait()

        add_normed(mix, 1)

        m = norm(lambda t: xres[:, t, :], D, lambda t: tmp2[:, t, :], 0)
        done(dve.memset(mix, 0.0), "dve")
        transpose_split(lambda t: tmp2[:, t, :], KT, 0, bc[:, B_MLP:B_MLP + KT], m)
        all_wait()
        h_t = cut(0, 2, 2, UNIT)

        def up(b):
            def evac(par):
                for i in range(2):
                    r = h_t[:, b, i, :]
                    last("act", f"hidden{b}")
                    m = done(act.activation(r, pg[:, par, i, :], ACT.Relu), "act")
                    wait("act", m)
                    m = done(act.activation(r, r, ACT.Square), "act")
                    wait("act", m)
                    r3 = r.rearrange("p (f s) -> p f s", f=2)
                    hh = b_hi[:, 4 * b + 2 * i:4 * b + 2 * i + 2, :]
                    hl = b_lo[:, 4 * b + 2 * i:4 * b + 2 * i + 2, :]
                    a = act.copy(hh, r3)
                    m = done(a, "act")
                    wait("dve", m)
                    m = done(dve.tensor_tensor(hl, r3, hh.bitcast(F32), ALU.subtract), "dve")
                keep(f"hidden{b}", m)
                return act.nop(), dve.nop()
            unit("col", evac)

        def down(b, name):
            last("pe", f"hidden{b}")
            with M.loop(name, 2) as u:
                for e in range(2):
                    unit("row", put(mix, u, e, True), chunks=GT // KC, hi=b_hi[:, 4 * b:4 * b + 4, :],
                         lo=b_lo[:, 4 * b:4 * b + 4, :])

        up(0)
        fence(("pe",), gemm=False)
        with M.loop("groups", GROUPS // 2 - 1):
            for b in range(2):
                up(1 - b)
                down(b, f"down{b}")
        fence(("pe",), gemm=False)
        up(1)
        down(0, "down_last0")
        down(1, "down_last1")
        fence()

        add_normed(mix, 2)
        M.wait_value("act", "dve", here("dve"))
        act.dma_start(out.rearrange("(t p) d -> p t d", p=P), xres[:, :, :]).then_inc(stored, 16)
        act.wait_ge(stored, 16)
    return M.plan


def _rope_consts(np):
    pos = np.arange(S, dtype=np.float32)
    inv = (1.0 / (10000.0 ** (np.arange(0, ROPE, 2, dtype=np.float32) / ROPE))).astype(np.float32)
    ang = (pos[:, None] * inv[None, :]).astype(np.float32)
    ang = np.concatenate([ang, ang], axis=-1)
    sin = np.sin(ang)
    sin[:, :ROPE // 2] *= -1
    t = np.stack([np.cos(ang), sin], axis=1).astype(np.float32)
    return np.ascontiguousarray(t.reshape(T, P, 2, ROPE).transpose(1, 0, 2, 3))


def _bucket_const(np):
    dist = 255 - np.arange(512)
    n = np.maximum(dist, 0)
    nf = np.maximum(n, 1).astype(np.float32)
    large = 16 + (np.log(nf / np.float32(16)) / np.float32(math.log(128 / 16)) * 16).astype(np.int32)
    b = np.where(n < 16, n, np.minimum(large, 31))
    c = np.zeros((33, 512), np.float32)
    c[b, np.arange(512)] = 8.0
    c[:32, dist < 0] = 0.0
    c[32, dist < 0] = NEG
    return c


def _mask_const(np):
    dist = 128 + np.arange(P)[:, None] - np.arange(S)[None, :]
    causal = np.where(dist >= 0, 0.0, NEG)
    n = sum(((dist >= 0) & (dist % d == 0) & (dist <= w)).astype(np.int64)
            for w, d in ((128, 1), (512, 4), (2048, 16)))
    dil = np.where(n > 0, np.log(np.maximum(n, 1)) * AD ** 0.5, NEG)
    return np.stack([causal, dil], axis=1).astype(np.float32)


def kernel(**inputs):
    import numpy as np
    import concourse.bacc as bacc
    from concourse.bass_utils import run_bass_kernel_spmd as run

    g = {k: np.ascontiguousarray(v) for k, v in inputs.items()}

    def cols(v):
        return v.reshape(-1, P).T

    def rows(v):
        return np.broadcast_to(v.reshape(1, -1), (P, v.size))

    layer_c = []
    for l in range(DEPTH):
        li = 0.8 - 0.6 * math.exp(-0.3 * l)
        layer_c.append(np.concatenate([
            cols(g["norm_g"][l]), cols(g["mla_q_norm_g"][l]), cols(g["mla_kv_norm_g"][l]),
            rows(g["diff_subln_g"][l]), rows(g["diff_lambda"][l]),
            rows(np.array([li, 1.0 - li], np.float32))], axis=1))
    conv = g["conv_w_2"][0].reshape(4, 32, P).transpose(2, 1, 0).reshape(P, 128)
    block_c = np.concatenate([
        cols(g["norm_mix_pre_2"][0]), cols(g["norm_mlp_pre_2"][0]), cols(g["ssm_norm_w_2"][0]), conv,
        cols(g["conv_b_2"][0]), rows(g["dt_bias_2"][0]), rows(g["a_log_2"][0]), rows(g["d_skip_2"][0])],
        axis=1)
    arrays = {
        "x": g["x"][0], "layer_c": np.concatenate(layer_c, axis=0),
        "w_in": g["w_in"].reshape(DEPTH * D, W_IN), "w_uq": g["w_uq"].reshape(DEPTH * QR, -1),
        "w_ukv": g["w_ukv"].reshape(DEPTH * KVR, -1), "w_out": g["w_out"].reshape(DEPTH * D, D),
        "rel_table": g["rel_bias_table"], "block_c": block_c,
        "rows_c": np.concatenate([rows(g["final_norm_g"]), rows(g["norm_mix_post_2"][0]),
                                  rows(g["norm_mlp_post_2"][0])], axis=0),
        "w_in_2": g["w_in_2"][0], "w_out_2": g["w_out_2"][0], "w_up": g["w_up_2"][0],
        "w_down": g["w_down_2"][0], "c_ident": np.eye(P, dtype=np.float32),
        "c_tri": np.triu(np.ones((P, P), np.float32)), "c_mask": _mask_const(np),
        "c_bucket": _bucket_const(np), "c_rope": _rope_consts(np),
    }
    arrays = {k: np.ascontiguousarray(v) for k, v in arrays.items()}
    plan = {}
    for real in (False, True):
        plan["real"] = real
        nc = bacc.Bacc("TRN2", target_bir_lowering=False, num_devices=1)
        args = {k: nc.dram_tensor(f"in_{k}", v.shape, mybir.dt.from_np(v.dtype),
                                  kind="ExternalInput").ap() for k, v in arrays.items()}
        out = nc.dram_tensor("out_x", (S, D), F32, kind="ExternalOutput").ap()
        build(nc, plan, out=out, **args)
    r = run(nc, [{f"in_{k}": v for k, v in arrays.items()}], core_ids=[0])
    return r.results[0]["out_x"].reshape(1, S, D)
```

```python
import math
from contextlib import ExitStack, contextmanager

import concourse.bass as bass
from concourse import mybir

F32 = mybir.dt.float32
F32R = mybir.dt.float32r
ALU = mybir.AluOpType
ACT = mybir.ActivationFunctionType
ET = mybir.EngineType
AX = mybir.AxisListType

P = 128
D = 2048
S = 256
T = S // P
DEPTH = 2
UNIT = 512
KC = 2
CHUNK = KC * UNIT
RING = 4
KT = D // P
UC = KT // KC
EPS = 1e-6
NEG = -1e30
CREDIT = 512

DH, DQK, DV = 8, 64, 128
MH, NOPE, ROPE, MV = 8, 128, 64, 128
QR = KVR = 512
W_IN = 6208
SH, SG, HPG, SN = 32, 8, 4, 128
HD = 64
AH, AD = 16, 128
W_IN2 = 12320
XBC = 4096
FF = 8192
LAYER_CHUNKS = 12 * UC + 2 + 7 * 2 + 4 * UC
GT = UNIT // P
GROUPS = FF // UNIT
GROUP2_CHUNKS = 2 * (UC + D // UNIT * (GT // KC))

C_G, C_QG, C_KVG, C_SUB, C_LAM, C_INIT = 0, 16, 20, 24, 152, 408
C_N = 410
B_PRE, B_MLP, B_SSM, B_CW, B_CB, B_DTB, B_AL, B_DS = 0, 16, 32, 48, 176, 208, 240, 272
B_N = 304


class Mark:

    def __init__(self, sem, n, frames):
        self.sem, self.n, self.frames = sem, n, frames


class Marks:

    def __init__(self, nc, plan):
        self.nc, self.plan, self.stack = nc, plan, []
        self.count, self.named = {}, {}
        self.eng = {"pe": nc.tensor, "act": nc.scalar, "dve": nc.vector, "pool": nc.gpsimd,
                    "sp": nc.sync}
        self.handle = {}

    def add(self, name, handle, start=0):
        self.handle[name], self.count[name] = handle, start

    def stride(self, frame, sem):
        return self.plan.get((frame, sem), 0)

    @contextmanager
    def loop(self, name, n, carry=()):
        for eng, names in carry:
            for m in names:
                if m in self.named:
                    self.wait(eng, self.named[m])
        start = dict(self.count)
        with self.nc.Fori(0, n, engines=(ET.PE, ET.Activation, ET.DVE, ET.Pool)) as i:
            frame = {"name": name, "var": i, "n": n, "live": True, "marks": {}}
            self.stack.append(frame)
            yield i
            self.stack.pop()
            frame["live"] = False
        for s in self.count:
            self.plan[(name, s)] = self.count[s] - start[s]
            self.count[s] = start[s] + n * (self.count[s] - start[s])
        for k, m in frame["marks"].items():
            self.plan[(name, "last", k)] = (m.sem, m.n)

    def done(self, ins, sem, name=None, by=1):
        ins.then_inc(self.handle[sem], by)
        self.count[sem] += by
        return self.keep(name, Mark(sem, self.count[sem], list(self.stack)))

    def keep(self, name, m):
        if name:
            self.named[name] = m
            for f in self.stack:
                f["marks"][name] = m
        return m

    def value(self, sem, n, frames, back=None):
        v = n
        for f in frames:
            st = self.stride(f["name"], sem)
            if f["live"]:
                k = f["var"]
                v = v + (k * st if st else 0)
                if f is back:
                    assert not self.plan.get("real") or n - st > 0, (sem, n, st)
                    v = v - st
            else:
                v = v + (f["n"] - 1) * st
        return v

    def wait_value(self, eng, sem, v, alone=True):
        self.eng[eng].wait_ge(self.handle[sem], v)
        if alone and not isinstance(v, int):
            self.eng[eng].sem_inc(self.handle["holder_" + eng])

    def wait(self, eng, m):
        if m is not None:
            self.wait_value(eng, m.sem, self.value(m.sem, m.n, m.frames))

    def wait_last(self, eng, name):
        if not self.stack:
            return self.wait(eng, self.named.get(name))
        f = self.stack[-1]
        if name in f["marks"]:
            return self.wait(eng, f["marks"][name])
        last = self.plan.get((f["name"], "last", name))
        if last is None:
            return self.wait(eng, self.named.get(name))
        sem, n = last
        self.wait_value(eng, sem, self.value(sem, n, list(self.stack), back=f))


def build(nc, plan, x, layer_c, w_in, w_uq, w_ukv, w_out, rel_table, block_c, rows_c, w_in_2,
          w_out_2, w_up, w_down, c_ident, c_tri, c_mask, c_bucket, c_rope, out):
    with ExitStack() as ctx:
        def sb(name, shape, dt=F32):
            return ctx.enter_context(nc.sbuf_tensor(name, shape, dt))

        def sem(name):
            return ctx.enter_context(nc.semaphore(name))

        M = Marks(nc, plan)
        pe, act, dve, pool, sp = nc.tensor, nc.scalar, nc.vector, nc.gpsimd, nc.sync
        wait, done, last, keep = M.wait, M.done, M.wait_last, M.keep

        raw = sb("raw", [P, RING, CHUNK])
        w_hi = sb("w_hi", [P, RING, CHUNK], F32R)
        w_lo = sb("w_lo", [P, RING, CHUNK], F32R)
        a_hi = sb("a_hi", [P, KT, S], F32R)
        a_lo = sb("a_lo", [P, KT, S], F32R)
        b_hi = sb("b_hi", [P, 2 * GT, S], F32R)
        b_lo = sb("b_lo", [P, 2 * GT, S], F32R)
        xres = sb("xres", [P, T, D])
        ident = sb("ident", [P, P])
        tri = sb("tri", [P, P])
        ones = sb("ones", [P, P])
        masks = sb("masks", [P, 2, S])
        minus_half = sb("minus_half", [P, 1])
        lc = sb("lc", [P, C_N])
        bc = sb("bc", [P, B_N])
        ARENA = 21 * 1024
        arena = sb("arena", [P, ARENA])
        stat = sb("stat", [P, 128])

        def cut(at, *shape):
            n = 1
            for v in shape:
                n *= v
            assert at + n <= ARENA, (at, n)
            ap = arena[:, at:at + n]
            if len(shape) == 2:
                return ap.rearrange("p (a b) -> p a b", b=shape[1])
            if len(shape) == 3:
                return ap.rearrange("p (a b c) -> p a b c", b=shape[1], c=shape[2])
            return ap

        pg = ctx.enter_context(nc.psum_tensor("pg", [P, 2, 2, 512], F32))
        pa = ctx.enter_context(nc.psum_tensor("pa", [P, 4, 512], F32))
        bias_dram = nc.dram_tensor("bias_scratch", (P, DH, 512), F32, kind="Internal").ap()

        for e in ("pe", "act", "dve", "pool"):
            M.add(e, sem(f"progress_{e}"), CREDIT)
            M.eng[e].sem_inc(M.handle[e], CREDIT)
        for e in ("pe", "act", "dve", "pool", "sp"):
            M.handle["holder_" + e] = sem(f"holder_{e}")
        landed = [sem(f"landed{s}") for s in range(RING)]
        M.add("rounded", sem("rounded"))
        M.add("split", sem("split"), RING)
        dve.sem_inc(M.handle["split"], RING)
        M.add("used", sem("used"))
        M.count["unit"] = 0
        M.add("out_a", sem("out_a"), 2)
        M.add("out_v", sem("out_v"), 2)
        act.sem_inc(M.handle["out_a"], 2)
        dve.sem_inc(M.handle["out_v"], 2)
        for n in ("ld_x", "ld_table", "ld_const", "ld_layer", "ld_bias"):
            M.add(n, sem(n))
        vec_out = sem("vec_out")
        M.add("hidden", sem("hidden"), CREDIT)
        dve.sem_inc(M.handle["hidden"], CREDIT)
        stored = sem("stored")

        def here(name):
            return M.value(name, M.count[name], M.stack)

        def stream():
            c = [0]

            def load(src, n, k, base):
                s = c[0] % RING
                num = base + c[0]
                M.wait_value("sp", "split", num + 1)
                dst = raw[:, s, 0:k * n].rearrange("p (k n) -> p k n", k=k)
                sp.dma_start(dst, src.rearrange("(k p) n -> p k n", p=P)).then_inc(landed[s], 32)
                c[0] += 1

            def units(w, col, n, base, chunks=UC):
                c0 = c[0]
                with sp.Fori(0, n) as u:
                    for j in range(chunks):
                        load(w[j * KC * P:(j + 1) * KC * P, bass.ds(u * UNIT + col, UNIT)], UNIT, KC,
                             base + u * chunks)
                assert chunks % RING == 0
                c[0] = c0 + n * chunks

            with sp.Fori(0, DEPTH) as l:
                lb = l * LAYER_CHUNKS
                win = w_in[bass.ds(l * D, D), :]
                units(win, 0, 8, lb)
                for j in range(2):
                    load(win[j * D // 2:(j + 1) * D // 2, W_IN - MH * MV - ROPE:W_IN - MH * MV],
                         ROPE, KT // 2, lb)
                units(win, 8 * UNIT, 2, lb)
                units(win, W_IN - MH * MV, 2, lb)
                uq = w_uq[bass.ds(l * QR, QR), :].rearrange("k (h c) -> k h c", h=MH)
                ukv = w_ukv[bass.ds(l * KVR, KVR), :].rearrange("k (h c) -> k h c", h=MH)

                def low_rank(w, c0, cn, h0, hn):
                    for j in range(2):
                        s = c[0] % RING
                        M.wait_value("sp", "split", lb + c[0] + 1)
                        for k in range(KC):
                            dst = raw[:, s, k * UNIT:(k + 1) * UNIT].rearrange("p (h c) -> p h c", h=hn)
                            r0 = (j * KC + k) * P
                            sp.dma_start(dst, w[r0:r0 + P, h0:h0 + hn, c0:c0 + cn]).then_inc(
                                landed[s], 16)
                        c[0] += 1

                low_rank(uq, NOPE, ROPE, 0, 8)
                for h0 in (0, 4):
                    low_rank(uq, 0, NOPE, h0, 4)
                for h0 in (0, 4):
                    low_rank(ukv, 0, NOPE, h0, 4)
                for h0 in (0, 4):
                    low_rank(ukv, NOPE, MV, h0, 4)
                for half in range(2):
                    units(w_out[bass.ds(l * D + half * (D // 2), D // 2), :], 0, 4, lb, UC // 2)
                assert c[0] == LAYER_CHUNKS, c[0]
            c[0] = DEPTH * LAYER_CHUNKS
            units(w_in_2[:, :], D + XBC + SH, 12, 0)
            units(w_in_2[:, :], 0, 4, 0)
            load(w_in_2[:, D + XBC:D + XBC + SH], SH, KT, 0)
            units(w_in_2[:, :], D, 8, 0)
            units(w_out_2[D:2 * D, :], 0, 4, 0)
            units(w_out_2[0:D, :], 0, 4, 0)

            def up(g, base):
                for j in range(UC):
                    load(w_up[j * KC * P:(j + 1) * KC * P, bass.ds(g, UNIT)], UNIT, KC, base)

            def down(g, base):
                c0 = c[0]
                with sp.Fori(0, D // UNIT // 2) as u:
                    for j in range(RING):
                        e, k = j // (GT // KC), j % (GT // KC)
                        load(w_down[bass.ds(g + k * KC * P, KC * P),
                                    bass.ds(u * (2 * UNIT) + e * UNIT, UNIT)], UNIT, KC, base + u * RING)
                c[0] = c0 + D // UNIT * (GT // KC)

            up(0, 0)
            c0 = c[0]
            with sp.Fori(0, GROUPS // 2 - 1) as i:
                f = i * (2 * UNIT)
                for b in range(2):
                    up(f + (b + 1) * UNIT, i * GROUP2_CHUNKS)
                    down(f + b * UNIT, i * GROUP2_CHUNKS)
            assert c[0] - c0 == GROUP2_CHUNKS
            c[0] = c0 + (GROUPS // 2 - 1) * GROUP2_CHUNKS
            up(FF - UNIT, 0)
            down(FF - 2 * UNIT, 0)
            down(FF - UNIT, 0)
            for j in range(RING):
                s = (c[0] + j) % RING
                M.wait_value("sp", "split", c[0] + j + 1)
                sp.dma_start(raw[:, s, :].rearrange("p (k n) -> p k n", k=KC),
                             w_down[0:KC * P, 0:UNIT].rearrange("(k p) n -> p k n", p=P)).then_inc(
                    landed[s], 32)

        for s in range(RING):
            M.handle[f"landed{s}"], M.count[f"landed{s}"] = landed[s], 0

        started = []

        def split_next():
            s = M.count["rounded"] % RING
            M.count[f"landed{s}"] += 32
            M.wait_value("act", f"landed{s}", here(f"landed{s}"), alone=False)
            if started:
                M.wait_value("act", "used", here("used"), alone=False)
            done(act.copy(w_hi[:, s, :], raw[:, s, :]), "rounded")
            M.wait_value("dve", "rounded", here("rounded"), alone=False)
            done(dve.tensor_tensor(w_lo[:, s, :], raw[:, s, :], w_hi[:, s, :].bitcast(F32),
                                   ALU.subtract), "split")

        hosted = {"at": 0, "steps": {}}

        def host(steps):
            hosted["at"], hosted["steps"] = 0, steps
            for f in steps.get(-1, ()):
                f()

        def multiply(emit, split=True):
            s = M.count["used"] % RING
            M.wait_value("pe", "split", here("used") + RING + 1, alone=False)
            done(emit(s), "used")
            started.append(s)
            if split:
                split_next()
            for f in hosted["steps"].get(hosted["at"], ()):
                f()
            hosted["at"] += 1

        def column_chunk(s, k0, par, first, final, a0):
            ins = None
            for kk in range(KC):
                for f in range(4):
                    wh = w_hi[:, s, kk * UNIT + f * P:kk * UNIT + (f + 1) * P]
                    wl = w_lo[:, s, kk * UNIT + f * P:kk * UNIT + (f + 1) * P]
                    o = pg[:, par, f // 2, (f % 2) * S:(f % 2 + 1) * S]
                    ah, al = a_hi[:, a0 + k0 + kk, :], a_lo[:, a0 + k0 + kk, :]
                    for n, (l, r) in enumerate(((wh, ah), (wh, al), (wl, ah))):
                        ins = pe.matmul(o, l, r, start=(first and kk == 0 and f % 2 == 0 and n == 0),
                                        stop=(final and kk == KC - 1 and n == 2),
                                        skip_group_check=True)
            return ins

        def narrow_chunk(s, k0, par, first, final, n, kc):
            ins = None
            for kk in range(kc):
                wh, wl = w_hi[:, s, kk * n:(kk + 1) * n], w_lo[:, s, kk * n:(kk + 1) * n]
                ah, al = a_hi[:, k0 + kk, :], a_lo[:, k0 + kk, :]
                for m, (l, r) in enumerate(((wh, ah), (wh, al), (wl, ah))):
                    ins = pe.matmul(pg[0:n, par, 0, 0:S], l, r, start=(first and kk == 0 and m == 0),
                                    stop=(final and kk == kc - 1 and m == 2))
            return ins

        def row_chunk(s, k0, par, first, final, a0, act_hi=None, act_lo=None, n=UNIT, kc=KC):
            ins = None
            for kk in range(kc):
                wh, wl = w_hi[:, s, kk * n:(kk + 1) * n], w_lo[:, s, kk * n:(kk + 1) * n]
                for t in range(T):
                    ah = (act_hi or a_hi)[:, a0 + k0 + kk, t * P:(t + 1) * P]
                    al = (act_lo or a_lo)[:, a0 + k0 + kk, t * P:(t + 1) * P]
                    for m, (l, r) in enumerate(((ah, wh), (ah, wl), (al, wh))):
                        ins = pe.matmul(pg[:, par, t, 0:n], l, r,
                                        start=(first and kk == 0 and m == 0),
                                        stop=(final and kk == kc - 1 and m == 2))
            return ins

        def unit(kind, evac, chunks=UC, a0=0, n=UNIT, kc=KC, hi=None, lo=None, after=None,
                 eager=False):
            par = M.count["unit"] % 2
            M.wait_value("pe", "out_a", here("unit") + 1)
            M.wait_value("pe", "out_v", here("unit") + 1)
            for j in range(chunks):
                if kind == "col":
                    def emit(s):
                        return column_chunk(s, j * kc, par, j == 0, j == chunks - 1, a0)
                elif kind == "narrow":
                    def emit(s):
                        return narrow_chunk(s, j * kc, par, j == 0, j == chunks - 1, n, kc)
                else:
                    def emit(s):
                        return row_chunk(s, j * kc, par, j == 0, j == chunks - 1, a0, hi, lo, n, kc)
                multiply(emit, not (eager and j == chunks - 1))
            M.count["unit"] += 1
            complete = Mark("used", M.count["used"], list(M.stack))
            wait("act", complete)
            wait("dve", complete)
            a, v = evac(par)
            done(v, "out_v")
            done(a or after(), "out_a")

        def copy_rows(dst):
            def evac(par):
                return (act.copy(dst(0), pg[:, par, 0, :]), dve.tensor_copy(dst(1), pg[:, par, 1, :]))
            return evac

        def copy_cols(dst):
            def evac(par):
                return (act.copy(dst(0), pg[:, par, 0, :].rearrange("p (f s) -> p f s", f=2)),
                        dve.tensor_copy(dst(1), pg[:, par, 1, :].rearrange("p (f s) -> p f s", f=2)))
            return evac

        def fence(engines=("pe", "act", "dve", "pool"), on=("pe", "act", "dve", "pool"), gemm=True):
            for e in engines:
                for o in on + (("used", "out_a", "out_v") if gemm else ()):
                    M.wait_value(e, o, here(o))

        def rstd(ss, dst, width):
            n = ss.shape[1]
            m = done(dve.tensor_scalar(ss, ss, 1.0 / width, EPS, ALU.mult, ALU.add), "dve")
            wait("pool", m)
            return done(pool.tensor_tensor(dst, ss, minus_half[:, 0:1].to_broadcast([P, n]), ALU.pow), "pool")

        def transposer(src, a0, gain=None, diag=None, banks=(0, 1, 2, 3), free=None):
            def turn(kp):
                b = banks[kp % len(banks)]
                last("pe", f"bank{b}")
                for kk in range(2):
                    for t in range(T):
                        k = 2 * kp + kk
                        o = pa[:, b, kk * S + t * P:kk * S + (t + 1) * P]
                        if diag is None:
                            ins = pe.transpose(o, src(t)[:, k * P:(k + 1) * P], ident[:, :])
                        else:
                            ins = pe.matmul(o, src(t)[:, k * P:(k + 1) * P], diag(t), start=True,
                                            stop=True)
                m = done(ins, "pe")
                wait("act", m)
                wait("dve", m)
                if free:
                    free(kp)
                if gain is None:
                    dst_h = a_hi[:, a0 + 2 * kp:a0 + 2 * kp + 2, :]
                    dst_l = a_lo[:, a0 + 2 * kp:a0 + 2 * kp + 2, :]
                    ps = pa[:, b, :].rearrange("p (k s) -> p k s", k=2)
                    h = done(act.copy(dst_h, ps), "act")
                    wait("dve", h)
                    return done(dve.tensor_tensor(dst_l, ps, dst_h.bitcast(F32), ALU.subtract), "dve",
                                f"bank{b}")
                for kk in range(2):
                    k = 2 * kp + kk
                    h = done(act.activation(a_hi[:, a0 + k, :], pa[:, b, kk * S:(kk + 1) * S], ACT.Copy,
                                            scale=gain[:, k:k + 1]), "act")
                wait("dve", h)
                for kk in range(2):
                    k = 2 * kp + kk
                    m = done(dve.scalar_tensor_tensor(a_lo[:, a0 + k, :], pa[:, b, kk * S:(kk + 1) * S],
                                                      gain[:, k:k + 1], a_hi[:, a0 + k, :].bitcast(F32),
                                                      ALU.mult, ALU.subtract), "dve", f"bank{b}")
                return m
            return turn

        def feed(turn, n, ahead=3):
            marks = {}

            def bring(kp):
                marks[kp] = turn(kp)
            steps = {k: [] for k in range(-1, n)}
            for kp in range(n):
                steps[max(kp - ahead, -1)].append(lambda kp=kp: bring(kp))
            for kp in range(n):
                steps[kp - 1].append(lambda kp=kp: wait("pe", marks[kp]))
            return steps

        def square_sums(srcs, tmps, ss):
            for i, (src, tmp) in enumerate(zip(srcs, tmps)):
                if i % 2 == 0:
                    a = done(act.activation(tmp, src, ACT.Square, accum_out=ss[:, i:i + 1]), "act")
                else:
                    v = done(dve.tensor_tensor_reduce(tmp, src, src, 1.0, 0.0, ALU.mult, ALU.add,
                                                      ss[:, i:i + 1]), "dve")
            return a, v

        parts = stat[:, 0:2 * T * 2].rearrange("p (t i) -> p t i", t=T)

        gained_parts = stat[:, 16:16 + 4 * T].rearrange("p (t i) -> p t i", t=T)

        def square_part(srcs, tmps, i, parts=parts, name="parts"):
            M.wait_value("act", "out_v", here("out_v"))
            last("act", name)
            for t in range(T):
                m = done(act.activation(tmps[t], srcs[t], ACT.Square, accum_out=parts[:, t, i:i + 1]), "act",
                         name)
            return m

        def sum_parts(parts=parts, name="parts"):
            last("dve", name)
            two = stat[:, 12:16].rearrange("p (t i) -> p t i", t=T)
            ss = stat[:, 8:10].rearrange("p (t i) -> p t i", t=T)
            wait("dve", done(dve.tensor_tensor(two, parts[:, :, 0:2], parts[:, :, 2:4], ALU.add), "dve"))
            wait("dve", done(dve.tensor_tensor(ss, two[:, :, 0:1], two[:, :, 1:2], ALU.add), "dve"))
            return stat[:, 8:10]

        def diag_of(ready, n=T):
            wait("dve", ready)
            for i in range(n):
                m = done(dve.tensor_scalar(diags[:, i, :], ident[:, :], stat[:, 40 + i:41 + i], None,
                                           ALU.mult), "dve")
            return m

        def norm_diag(srcs, tmps, width):
            n = len(srcs)
            for m in square_sums(srcs, tmps, stat[:, 32:32 + n]):
                wait("dve", m)
            wait("pe", diag_of(rstd(stat[:, 32:32 + n], stat[:, 40:40 + n], width), n))

        def scaled_halves(ops, tmps):
            done(dve.memset(parts, 0.0), "dve", "parts")
            for t in range(T):
                for i in range(2):
                    cols = slice(i * (D // 2), (i + 1) * (D // 2))
                    m = done(ops(t, cols), "dve")
                    last("act", "parts")
                    wait("act", m)
                    done(act.activation(tmps[t][:, cols], xres[:, t, cols], ACT.Square,
                                        accum_out=parts[:, t, i:i + 1]), "act", "parts")
            wait("pe", diag_of(rstd(sum_parts(), stat[:, 40:42], D)))

        def move(turned, dest, ot):
            last("pe", "finished")
            last("pe", "moved")
            for t in range(T):
                ins = pe.transpose(ot[:, t * P:(t + 1) * P], turned[:, t, :], ident[:, :])
            m = done(ins, "pe", "out_turned")
            wait("act", m)
            m = done(act.copy(dest[0], ot), "act")
            wait("dve", m)
            return done(dve.tensor_tensor(dest[1], ot, dest[0].bitcast(F32), ALU.subtract), "dve", "moved")

        ROWS = ((0, P, P), (P, 3 * P, 0))

        def head(e, stage, score, maps, mask, scale, weights, pt, v, finish, turned=None, dest=None):
            base = 64 + 32 * e
            n = 2 * maps
            ot = pa[:, 1, 0:S] if maps == 1 else pa[:, 3, S:2 * S]
            mx, neg, den, rec = (stat[:, base + n * i:base + n * (i + 1)] for i in range(4))
            box = {}

            def stage_step():
                last("pool", "scored")
                last("pool", "maxed")
                box["staged"] = stage()

            def score_step():
                wait("pe", box["staged"])
                last("pe", "maxed")
                m = done(score(), "pe", "scored")
                wait("dve", m)
                last("dve", f"turned{e}")
                for mm in range(maps):
                    for i, (a, b, m0) in enumerate(ROWS):
                        k = 2 * mm + i
                        m = done(dve.tensor_tensor_reduce(
                            sc[e][:, mm, a:b], pa[:, mm, a:b], mask[:, m0:m0 + b - a], scale, 3.0 * NEG,
                            ALU.add, ALU.max, mx[:, k:k + 1]), "dve", "maxed")
                wait("dve", m)
                m = done(dve.tensor_scalar(neg, mx, -1.0, None, ALU.mult), "dve")
                wait("act", m)
                for mm in range(maps):
                    for i, (a, b, _) in enumerate(ROWS):
                        k = 2 * mm + i
                        m = done(act.activation(sc[e][:, mm, a:b], sc[e][:, mm, a:b], ACT.Exp,
                                                bias=neg[:, k:k + 1], accum_out=den[:, k:k + 1]), "act")
                wait("dve", m)
                box["rec"] = done(dve.reciprocal(rec, den), "dve")
                box["tile"], box["weighed"] = weights(e, m, rec, box["rec"])

            def turn_step():
                wait("pe", box["weighed"])
                last("pe", "pt_copied")
                for b in range(3):
                    ins = pe.transpose(pa[:, 2, b * P:(b + 1) * P], box["tile"][:, b * P:(b + 1) * P],
                                       ident[:, :])
                m = done(ins, "pe", f"turned{e}")
                wait("act", m)
                last("act", "applied")
                box["pt"] = done(act.copy(pt, pa[:, 2, 0:3 * P]), "act", "pt_copied")

            def apply_step():
                wait("pe", box["pt"])
                last("pe", "finished")
                if maps == 2:
                    last("pe", "moved")
                o = pa[:, 3, 0:2 * P].rearrange("p (t v) -> p t v", t=2)
                pe.matmul(o[:, 0, :], pt[:, 0:P], v(0), start=True, stop=True)
                pe.matmul(o[:, 1, :], pt[:, P:2 * P], v(0), start=True, stop=False)
                m = done(pe.matmul(o[:, 1, :], pt[:, 2 * P:3 * P], v(1), start=False, stop=True), "pe",
                         "applied")
                if turned is not None:
                    last("dve", "out_turned")
                box["finished"] = keep("finished", finish(e, o, rec, m, box["rec"]))

            def move_step():
                move(turned, dest, ot)

            return stage_step, score_step, turn_step, apply_step, move_step

        def schedule(heads, at, carried=None):
            steps = {-1: [heads[0][0]]}
            if carried:
                steps[carried[0]] = [carried[1]]
            for i, (h, when) in enumerate(zip(heads, at)):
                for rank, slot in enumerate(when, 1):
                    fs = steps.setdefault(slot, [])
                    fs.append(h[rank])
                    if rank == 1 and i + 1 < len(heads):
                        fs.append(heads[i + 1][0])
            return steps

        def flat(ap):
            return ap.rearrange("p a s -> p (a s)")

        bucket = cut(0, 512)
        table = cut(512, DH)
        bias = cut(19456, DH, S)
        vec = cut(1024, DH, 512)
        diags = cut(18176, 4, P)
        rope = sb("rope", [P, T, 2, ROPE])
        vecs = bias_dram.rearrange("p h j -> (p h j)")
        skew = bass.AP(tensor=vecs.tensor, offset=vecs.offset + P - 1,
                       ap=[[DH * 512 - 1, P], [512, DH], [1, S]])
        for dst, src in ((bucket[0:33, :], c_bucket), (table[0:32, :], rel_table)):
            act.dma_start(dst, src).then_inc(M.handle["ld_table"], 16)
        M.count["ld_table"] = 2 * 16
        sp.dma_start(ident[:, :], c_ident).then_inc(M.handle["ld_x"], 16)
        for t in range(T):
            sp.dma_start(xres[:, t, :], x[t * P:(t + 1) * P, :]).then_inc(M.handle["ld_x"], 16)
        M.count["ld_x"] = 3 * 16
        for dst, src in ((tri[:, :], c_tri), (masks[:, :, :], c_mask), (bc[:, :], block_c),
                         (rope[:, :, :, :], c_rope)):
            act.dma_start(dst, src).then_inc(M.handle["ld_const"], 16)
        M.count["ld_const"] = 4 * 16
        done(dve.memset(minus_half[:, 0:1], -0.5), "dve")
        m_tab = done(dve.memset(table[32:33, :], 1.0), "dve")
        done(dve.memset(ones[:, :], 1.0), "dve")
        done(dve.memset(cut(18944, S), 0.0), "dve")

        M.wait_value("pe", "ld_table", M.count["ld_table"])
        wait("pe", m_tab)
        vmarks = {}
        for h in range(DH):
            if h >= 4:
                wait("pe", vmarks[h - 4])
            m = done(pe.matmul(pa[:, h % 4, :], table[0:33, h:h + 1].to_broadcast([33, P]),
                               bucket[0:33, :], start=True, stop=True), "pe")
            e, fn = (("act", act.copy), ("dve", dve.tensor_copy))[h % 2]
            wait(e, m)
            vmarks[h] = done(fn(vec[:, h, :], pa[:, h % 4, :]), e)
        stream()
        for e in ("pe", "act", "dve"):
            M.wait_value(e, "ld_x", M.count["ld_x"])
        for e in ("act", "dve"):
            wait(e, m)

        tok = cut(0, T, 8 * UNIT)
        qkT = cut(8 * 1024, 16, S)
        qrT = cut(12 * 1024, 4, S)
        krT = cut(13 * 1024, S)
        kr = cut(13 * 1024 + 256, T, ROPE)
        kr_f = cut(13 * 1024 + 768, S)
        krd = cut(13 * 1024 + 512, T, 2 * ROPE)
        tmp = cut(8 * 1024, T, D)
        rt = cut(14 * 1024, T, 1152)
        q_s, k_s, b_st = (cut(16640 + S * i, S) for i in range(3))
        sc = [cut(17408, 2, 3 * P), cut(14 * 1024, 2, 3 * P)]
        w_s = cut(18176, 3 * P)
        pt_s = cut(18560, 3 * P)
        og = cut(18944, T, P)
        junk = cut(19200, P)
        lamt = cut(19200, 2, 64)
        gain_f = cut(14 * 1024, D)
        sq_tmp = cut(12 * 1024, 2 * T, UNIT)

        def load_layer(l):
            M.wait_value("pool", "dve", here("dve"))
            pool.dma_start(lc[:, :], layer_c[bass.ds(l * P, P), :]).then_inc(M.handle["ld_layer"], 16)
            M.count["ld_layer"] += 16

        load_layer(0)
        norm_diag([xres[:, t, :] for t in range(T)], [tmp[:, t, :] for t in range(T)], D)
        for h in (DH - 2, DH - 1):
            wait("act", vmarks[h])
        act.dma_start(bias_dram, vec[:, :, :]).then_inc(vec_out, 16)
        pool.wait_ge(vec_out, 16)
        pool.dma_start(bias[:, :, :], skew).then_inc(M.handle["ld_bias"], 16)
        M.count["ld_bias"] = 16
        for _ in range(RING):
            split_next()
        with M.loop("layer", DEPTH) as l:
            for e in ("act", "dve"):
                M.wait_value(e, "ld_layer", here("ld_layer"))
            for i in range(2):
                m = done(dve.tensor_tensor_reduce(lamt[:, i, :], lc[:, C_LAM + 128 * i:C_LAM + 128 * i + 64],
                                                  lc[:, C_LAM + 128 * i + 64:C_LAM + 128 * i + 128], 1.0,
                                                  0.0, ALU.mult, ALU.add, stat[:, 60 + i:61 + i]), "dve")
            wait("act", m)
            m = done(act.activation(stat[:, 60:62], stat[:, 60:62], ACT.Exp), "act")
            wait("dve", m)
            m = done(dve.tensor_tensor(stat[:, 62:63], stat[:, 61:62], stat[:, 60:61], ALU.subtract), "dve")
            wait("dve", m)
            done(dve.tensor_tensor(stat[:, 62:63], stat[:, 62:63], lc[:, C_INIT:C_INIT + 1],
                                   ALU.subtract), "dve", "neglam")

            turn = transposer(lambda t: xres[:, t, :], 0, lc[:, C_G:C_G + KT], lambda t: diags[:, t, :])
            host(feed(turn, UC))
            for i in range(4):
                unit("col", copy_cols(lambda half: qkT[:, 4 * i + 2 * half:4 * i + 2 * half + 2, :]))
            host({})
            for e in ("act", "dve", "pool"):
                M.wait_value(e, "ld_bias", M.count["ld_bias"])
                M.wait_value(e, "ld_const", M.count["ld_const"])
            with M.loop("v_za", 2) as u:
                for e in range(2):
                    unit("row", copy_rows(lambda t: tok[:, t, bass.ds(u * (2 * UNIT) + e * UNIT, UNIT)]))
            unit("narrow", lambda par: (act.nop(), dve.tensor_copy(kr_f[0:ROPE, :], pg[0:ROPE, par, 0, 0:S])),
                 chunks=2, n=ROPE, kc=KT // 2, eager=True)
            split_next()
            kr_there = Mark("out_v", M.count["out_v"], list(M.stack))
            fence(("act", "pool"), on=())
            for t in range(T):
                m = done(act.activation(tok[:, t, 1024:2048], tok[:, t, 1024:2048], ACT.Silu), "act")
            fence(("dve",))
            for t in range(T):
                za = tok[:, t, 1024:2048].rearrange("p (h v) -> p h v", h=DH)
                g = lc[:, C_SUB:C_SUB + DV].unsqueeze(1).to_broadcast([P, DH, DV])
                m = done(dve.scalar_tensor_tensor(za, za, lc[:, C_INIT + 1:C_INIT + 2], g,
                                                  ALU.mult, ALU.mult), "dve")
            wait("dve", m)

            def diff_head(h, e):
                def stage():
                    done(pool.tensor_copy(q_s, flat(qkT[:, bass.ds(h, 1), :])), "pool")
                    done(pool.tensor_copy(k_s, flat(qkT[:, bass.ds(h + DH, 1), :])), "pool")
                    return done(pool.tensor_copy(b_st, flat(bias[:, bass.ds(h, 1), :])), "pool")

                def score():
                    for mm in range(2):
                        r = slice(mm * DQK, (mm + 1) * DQK)
                        pe.matmul(pa[:, mm, 0:P], q_s[r, 0:P], k_s[r, 0:P], start=True, stop=True)
                        ins = pe.matmul(pa[:, mm, P:3 * P], q_s[r, P:S], k_s[r, 0:S], start=True,
                                        stop=True)
                    return ins

                def weights(_, m, rec, rm):
                    wait("dve", rm)
                    m = done(dve.tensor_scalar(rec[:, 2:4], rec[:, 2:4], stat[:, 62:63], None, ALU.mult),
                             "dve")
                    for t, (a, b, _) in enumerate(ROWS):
                        m2 = done(dve.tensor_scalar(sc[0][:, 0, a:b], sc[0][:, 0, a:b], rec[:, t:t + 1],
                                                    None, ALU.mult), "dve")
                    wait("dve", m2)
                    last("dve", "turned0")
                    for t, (a, b, _) in enumerate(ROWS):
                        m = done(dve.scalar_tensor_tensor(w_s[:, a:b], sc[0][:, 1, a:b],
                                                          rec[:, 2 + t:3 + t], sc[0][:, 0, a:b],
                                                          ALU.mult, ALU.add), "dve")
                    return w_s, m

                def finish(_, o, rec, m, rm):
                    ss, rs = stat[:, 80:82], stat[:, 82:84]
                    wait("act", m)
                    for t in range(T):
                        last("act", "junk")
                        m = done(act.activation(junk, o[:, t, :], ACT.Square, accum_out=ss[:, t:t + 1]),
                                 "act", "junk")
                    wait("dve", m)
                    m = rstd(ss, rs, DV)
                    wait("dve", m)
                    for t in range(T):
                        m = done(dve.scalar_tensor_tensor(og[:, t, :], o[:, t, :], rs[:, t:t + 1],
                                                          tok[:, t, bass.ds(h * DV + 1024, DV)],
                                                          ALU.mult, ALU.mult), "dve")
                    return m

                return head(0, stage, score, 2, b_st, DQK ** -0.5, weights, pt_s,
                            lambda t: tok[:, t, bass.ds(h * DV, DV)], finish, og,
                            (flat(b_hi[:, bass.ds(h, 1), :]), flat(b_lo[:, bass.ds(h, 1), :])))

            for b in range(4):
                last("pe", f"bank{b}")
            for e in ("out_a", "out_v"):
                M.wait_value("pe", e, here(e))
            with M.loop("c_zb", 2) as u:
                host(schedule([diff_head(u * 4 + e, e) for e in range(4)],
                              [(0, 3, 4, 7), (3, 7, 8, 11), (7, 11, 12, 14), (11, 14, 15)],
                              (1, lambda: move(og, (flat(b_hi[:, bass.ds(DH - 1 - u * 4, 1), :]),
                                                    flat(b_lo[:, bass.ds(DH - 1 - u * 4, 1), :])),
                                               pa[:, 3, S:2 * S]))))
                for e in range(2):
                    unit("row", copy_rows(lambda t: tok[:, t, bass.ds(u * (2 * UNIT) + (2048 + e * UNIT),
                                                                      UNIT)]))
            host({})
            fence()

            norm_diag([tok[:, t, 2048 + UNIT * i:2048 + UNIT * (i + 1)] for i in range(2) for t in range(T)],
                      [tmp[:, t, UNIT * i:UNIT * (i + 1)] for i in range(2) for t in range(T)], QR)
            turn_c = [transposer(lambda t, i=i: tok[:, t, 2048 + UNIT * i:2048 + UNIT * (i + 1)], 4 * i,
                                 lc[:, gc:gc + 4], lambda t, i=i: diags[:, 2 * i + t, :],
                                 banks=(2 * i, 2 * i + 1)) for i, gc in ((0, C_QG), (1, C_KVG))]

            def turn_kr():
                wait("pe", kr_there)
                for t in range(T):
                    ins = pe.transpose(pa[:, 3, t * ROPE:(t + 1) * ROPE], kr_f[0:ROPE, t * P:(t + 1) * P],
                                       ident[0:ROPE, 0:ROPE])
                wait("act", done(ins, "pe"))
                done(act.copy(kr, pa[:, 3, 0:T * ROPE].rearrange("p (t c) -> p t c", t=T)), "act", "bank3")

            steps = feed(turn_c[0], 2)
            steps[0].insert(0, turn_kr)
            steps[-1].insert(2, lambda: keep("bank2", move(
                og, (flat(b_hi[:, DH - 1:DH, :]), flat(b_lo[:, DH - 1:DH, :])), pa[:, 2, 0:S])))
            latent_kv = []
            steps[0].append(lambda: latent_kv.append(turn_c[1](0)))
            steps[1].append(lambda: latent_kv.append(turn_c[1](1)))
            host(steps)
            unit("row", copy_rows(lambda t: tok[:, t, 2048:2048 + UNIT]), chunks=2, a0=0)
            host({})
            fence(("dve",), on=())
            for t in range(T):
                cs = rope[:, t, 0, :]
                sn = rope[:, t, 1, :]
                half = ROPE // 2
                for src, dst, heads in ((tok[:, t, 2048:2560], rt[:, t, 0:512], MH),
                                        (kr[:, t, :], rt[:, t, 512:576], 1)):
                    s3 = src.rearrange("p (h c) -> p h c", h=heads)
                    d3 = dst.rearrange("p (h c) -> p h c", h=heads)
                    rot = rt[:, t, 576:576 + ROPE * heads].rearrange("p (h c) -> p h c", h=heads)

                    def bcast(v):
                        return v.unsqueeze(1).to_broadcast([P, heads, v.shape[-1]])
                    last("dve", "rope_add")
                    done(dve.tensor_tensor(rot[:, :, 0:half], s3[:, :, half:ROPE], bcast(sn[:, 0:half]),
                                           ALU.mult), "dve")
                    done(dve.tensor_tensor(rot[:, :, half:ROPE], s3[:, :, 0:half], bcast(sn[:, half:ROPE]),
                                           ALU.mult), "dve")
                    m = done(dve.tensor_tensor(d3, s3, bcast(cs), ALU.mult), "dve")
                    wait("dve", m)
                    m = done(dve.tensor_tensor(d3, d3, rot, ALU.add), "dve", "rope_add")
                wait("dve", m)
                for i in range(2):
                    m = done(dve.tensor_copy(krd[:, t, i * ROPE:(i + 1) * ROPE], rt[:, t, 512:576]), "dve")
            roped = m

            def turn_roped():
                wait("pe", roped)
                for b in range(3):
                    last("pe", f"bank{b}")
                for i in range(4):
                    for t in range(T):
                        pe.transpose(pa[:, i // 2, (i % 2) * S + t * P:(i % 2) * S + (t + 1) * P],
                                     rt[:, t, i * P:(i + 1) * P], ident[:, :])
                for t in range(T):
                    ins = pe.transpose(pa[:, 2, t * P:(t + 1) * P], krd[:, t, :], ident[:, :])
                m = done(ins, "pe")
                wait("act", m)
                wait("dve", m)
                done(act.copy(qrT[:, 0:2, :], pa[:, 0, :].rearrange("p (a s) -> p a s", a=2)), "act")
                done(dve.tensor_copy(qrT[:, 2:4, :], pa[:, 1, :].rearrange("p (a s) -> p a s", a=2)), "dve")
                done(act.copy(krT, pa[:, 2, 0:S]), "act")

            host({3: [lambda: [wait("pe", m) for m in latent_kv]], 7: [turn_roped]})
            for i in range(4):
                unit("col", copy_cols(lambda half: qkT[:, 4 * i + 2 * half:4 * i + 2 * half + 2, :]),
                     chunks=2, a0=4 * (i // 2))
            host({})
            fence(("act",), on=())
            for t in range(T):
                done(act.activation(tok[:, t, 3072:4096], tok[:, t, 3072:4096], ACT.Silu), "act")
            unit("row", copy_rows(lambda t: tok[:, t, 0:UNIT]), chunks=2, a0=4)
            fence(("pool",))
            unit("row", copy_rows(lambda t: tok[:, t, UNIT:2 * UNIT]), chunks=2, a0=4)

            def latent_head(hp, e):
                r = slice((e % 2) * ROPE, (e % 2 + 1) * ROPE)

                def stage():
                    if e % 2 == 0:
                        done(pool.tensor_copy(b_st, flat(qrT[:, bass.ds(hp * 2 + e // 2, 1), :])), "pool")
                    return done(pool.tensor_copy(q_s, flat(qkT[:, bass.ds(hp * 4 + e, 1), :])), "pool")

                def score():
                    k_h = flat(qkT[:, bass.ds(hp * 4 + (MH + e), 1), :])
                    for (a, b, _), qc, nk in zip(ROWS, (slice(0, P), slice(P, S)), (P, S)):
                        pe.matmul(pa[:, 0, a:b], q_s[:, qc], k_h[:, 0:nk], start=True, stop=False)
                        ins = pe.matmul(pa[:, 0, a:b], b_st[r, qc], krT[r, 0:nk], start=False, stop=True)
                    return ins

                def finish(_, o, rec, m, rm):
                    wait("dve", m)
                    for t in range(T):
                        m = done(dve.scalar_tensor_tensor(
                            og[:, t, :], o[:, t, :], rec[:, t:t + 1],
                            tok[:, t, bass.ds(hp * (4 * MV) + (e * MV + 3072), MV)], ALU.mult, ALU.mult),
                            "dve")
                    return m

                return head(e % 2, stage, score, 1, masks[:, 0, :], (NOPE + ROPE) ** -0.5,
                            lambda _, m, rec, rm: (sc[e % 2][:, 0, :], m), pt_s,
                            lambda t: tok[:, t, bass.ds(hp * (4 * MV) + e * MV, MV)], finish, og,
                            (flat(a_hi[:, bass.ds(hp * 4 + (8 + e), 1), :]),
                             flat(a_lo[:, bass.ds(hp * 4 + (8 + e), 1), :])))

            def add_x(u, e):
                def evac(par):
                    xs = [xres[:, t, bass.ds(u * (2 * UNIT) + e * UNIT, UNIT)] for t in range(T)]
                    done(dve.tensor_tensor(xs[0], xs[0], pg[:, par, 0, :], ALU.add), "dve")
                    return act.nop(), dve.tensor_tensor(xs[1], xs[1], pg[:, par, 1, :], ALU.add)
                return evac

            fence(("pe",), gemm=False)
            with M.loop("out_diff", 2) as u:
                host(schedule([latent_head(u, e) for e in range(4)],
                              [(0, 2, 3, 4), (1, 3, 4, 5), (3, 5, 6, 7), (4, 6, 7)],
                              (0, lambda: move(og, (flat(a_hi[:, bass.ds(u * 4 + (DH - 1), 1), :]),
                                                    flat(a_lo[:, bass.ds(u * 4 + (DH - 1), 1), :])),
                                               pa[:, 1, 0:S]))))
                for e in range(2):
                    unit("row", add_x(u, e), chunks=UC // 2, hi=b_hi, lo=b_lo)
            tail = {}

            def move_tail():
                tail["m"] = move(og, (flat(a_hi[:, KT - 1:KT, :]), flat(a_lo[:, KT - 1:KT, :])), pa[:, 1, 0:S])
            host({-1: [lambda: last("pe", "moved")], 0: [move_tail], 2: [lambda: wait("pe", tail["m"])]})
            last("pool", "applied")
            last("pool", "finished")
            pool.dma_start(gain_f, rows_c[0:P, :]).then_inc(M.handle["ld_layer"], 16)
            M.count["ld_layer"] += 16
            for u in range(2):
                for e in range(2):
                    i = 2 * u + e
                    unit("row", add_x(u, e), chunks=UC // 2, a0=8, eager=(i == 3))
                    c = slice(i * UNIT, (i + 1) * UNIT)
                    square_part([xres[:, t, c] for t in range(T)], [sq_tmp[:, t, :] for t in range(T)], i)
                    if i == 0:
                        M.wait_value("dve", "ld_layer", here("ld_layer"))
                    wait("dve", Mark("out_v", M.count["out_v"], list(M.stack)))
                    for t in range(T):
                        m = done(dve.tensor_tensor(tmp[:, t, c], xres[:, t, c], gain_f[:, c], ALU.mult), "dve")
                    wait("act", m)
                    square_part([tmp[:, t, c] for t in range(T)], [sq_tmp[:, T + t, :] for t in range(T)], i,
                                gained_parts, "gained_parts")

            fence()
            load_layer(l + 1)
            wait("pe", diag_of(rstd(sum_parts(), stat[:, 40:42], D)))
            split_next()

        rows = cut(18 * 1024, D)

        def load_row(i):
            M.wait_value("pool", "dve", here("dve"))
            pool.dma_start(rows, rows_c[i * P:(i + 1) * P, :]).then_inc(M.handle["ld_layer"], 16)
            M.count["ld_layer"] += 16

        tmp2 = cut(8 * 1024, T, D)
        xt, st = [xres[:, t, :] for t in range(T)], [tmp2[:, t, :] for t in range(T)]

        z = cut(0, T, D)
        qkT2 = cut(4 * 1024, 32, S)
        v2t = cut(12 * 1024, T, D)
        r1, r2, ss2 = stat[:, 40:42], stat[:, 44:46], stat[:, 8:10]
        r_keep = stat[:, 42:44]
        wait("dve", done(dve.tensor_copy(r_keep, r1), "dve"))
        sum_parts(gained_parts, "gained_parts")
        for _ in range(2):
            wait("dve", done(dve.tensor_tensor(ss2, ss2, r_keep, ALU.mult), "dve"))
        wait("dve", rstd(ss2, r2, D))
        wait("pe", diag_of(done(dve.tensor_tensor(r1, r_keep, r2, ALU.mult), "dve")))
        steps = feed(transposer(lambda t: tmp2[:, t, :], 0, bc[:, B_PRE:B_PRE + KT],
                                lambda t: diags[:, t, :], banks=(0, 1)), UC, 2)

        def new_x():
            for t in range(T):
                m = done(dve.tensor_scalar(xres[:, t, :], tmp2[:, t, :], r_keep[:, t:t + 1], None, ALU.mult),
                         "dve")
            return m
        steps[UC - 1] = steps.get(UC - 1, []) + [new_x]
        host(steps)
        for e in range(2):
            unit("col", copy_cols(lambda half: qkT2[:, 4 * e + 2 * half:4 * e + 2 * half + 2, :]))
        host({})
        with M.loop("qk2", 3) as u:
            for e in range(2):
                unit("col", copy_cols(lambda half: qkT2[:, bass.ds(u * 8 + (8 + 4 * e + 2 * half), 2), :]))
        with M.loop("v2", 2) as u:
            for e in range(2):
                unit("row", copy_rows(lambda t: v2t[:, t, bass.ds(u * (2 * UNIT) + e * UNIT, UNIT)]))
        sc[0], sc[1] = cut(17408, 1, 3 * P), cut(17408 + 384, 1, 3 * P)

        def dilated_head(hp, e):
            def stage():
                return done(pool.tensor_copy(q_s, flat(qkT2[:, bass.ds(hp * 8 + e, 1), :])), "pool")

            def score():
                k_h = flat(qkT2[:, bass.ds(hp * 8 + (AH + e), 1), :])
                pe.matmul(pa[:, 0, 0:P], q_s[:, 0:P], k_h[:, 0:P], start=True, stop=True)
                return pe.matmul(pa[:, 0, P:3 * P], q_s[:, P:S], k_h[:, 0:S], start=True, stop=True)

            def finish(_, o, rec, m, rm):
                wait("dve", m)
                for t in range(T):
                    m = done(dve.tensor_scalar(v2t[:, t, bass.ds(hp * (8 * AD) + e * AD, AD)], o[:, t, :],
                                               rec[:, t:t + 1], None, ALU.mult), "dve")
                return m

            return head(e % 2, stage, score, 1, masks[:, 1, :], AD ** -0.5,
                        lambda _, m, rec, rm: (sc[e % 2][:, 0, :], m), pt_s,
                        lambda t: v2t[:, t, bass.ds(hp * (8 * AD) + e * AD, AD)], finish)

        fence(("act", "dve", "pool"))
        fence(("pe",), gemm=False)
        with M.loop("z", 2) as u:
            host(schedule([dilated_head(u, e) for e in range(8)],
                          [(k, min(k + 2, 15), min(k + 3, 15)) for k in (0, 2, 4, 6, 8, 10, 11, 13)]))
            for e in range(2):
                unit("row", copy_rows(lambda t: z[:, t, bass.ds(u * (2 * UNIT) + e * UNIT, UNIT)]))
        host({})
        fence(("act", "dve", "pool"))

        dt = cut(16 * 1024, T, SH)
        dt_f = cut(16896, S)
        unit("narrow", lambda par: (act.nop(), dve.tensor_copy(dt_f[0:SH, :], pg[0:SH, par, 0, 0:S])),
             chunks=1, n=SH, kc=KT, eager=True)
        split_next()
        M.wait_value("pe", "out_v", here("out_v"))
        last("pe", "bank3")
        for t in range(T):
            ins = pe.transpose(pa[:, 3, t * SH:(t + 1) * SH], dt_f[0:SH, t * P:(t + 1) * P],
                               ident[0:SH, 0:SH])
        m = done(ins, "pe")
        wait("dve", m)
        m = done(dve.tensor_copy(dt, pa[:, 3, 0:T * SH].rearrange("p (t c) -> p t c", t=T)), "dve", "bank3")
        wait("dve", m)

        A = 16 * 1024 + 64
        n2 = T * SH
        v1, v2, s1, s2 = (cut(A + n2 * i, n2) for i in range(4))
        dtf = dt.rearrange("p t h -> p (t h)")
        dA = cut(A + 4 * n2, T, SH)
        acs = cut(A + 5 * n2, 3, SH)
        aneg = cut(A + 7 * n2, SH)

        def chain(ins):
            m = done(ins, "dve")
            wait("dve", m)
            return m

        chain(dve.tensor_tensor(dt, dt, bc[:, B_DTB:B_DTB + SH].unsqueeze(1).to_broadcast([P, T, SH]),
                                ALU.add))
        chain(dve.tensor_scalar(v1, dtf, -1.0, None, ALU.mult))
        m = chain(dve.tensor_tensor(v1, v1, dtf, ALU.min))
        wait("act", m)
        done(act.activation(aneg, bc[:, B_AL:B_AL + SH], ACT.Exp), "act")
        m = done(act.activation(v1, v1, ACT.Exp), "act")
        wait("dve", m)
        chain(dve.tensor_scalar(v2, v1, 2.0, None, ALU.add))
        chain(dve.reciprocal(v2, v2))
        chain(dve.tensor_tensor(s1, v1, v2, ALU.mult))
        chain(dve.tensor_tensor(s2, s1, s1, ALU.mult))
        chain(dve.tensor_scalar(v1, s2, 1.0 / 17, 1.0 / 15, ALU.mult, ALU.add))
        for k in (13, 11, 9, 7, 5, 3, 1):
            chain(dve.tensor_tensor(v1, v1, s2, ALU.mult))
            chain(dve.tensor_scalar(v1, v1, 1.0 / k, None, ALU.add))
        chain(dve.tensor_tensor(v1, v1, s1, ALU.mult))
        chain(dve.tensor_scalar(dtf, dtf, 0.0, None, ALU.max))
        chain(dve.scalar_tensor_tensor(dtf, v1, 2.0, dtf, ALU.mult, ALU.add))
        m = chain(dve.scalar_tensor_tensor(dA, dt, -1.0, aneg.unsqueeze(1).to_broadcast([P, T, SH]),
                                           ALU.mult, ALU.mult))
        summed_dt = m

        def dt_sums():
            wait("pe", summed_dt)
            last("pe", "bank3")
            pe.matmul(pa[:, 3, 0:SH], tri[:, :], dA[:, 0, :], start=True, stop=True)
            pe.matmul(pa[:, 3, SH:2 * SH], tri[:, :], dA[:, 1, :], start=True, stop=True)
            m = done(pe.matmul(pa[:, 3, 2 * SH:3 * SH], ones[:, :], dA[:, 0, :], start=True, stop=True),
                     "pe")
            wait("dve", m)
            done(dve.tensor_copy(acs[:, 0, :], pa[:, 3, 0:SH]), "dve")
            chain(dve.tensor_copy(acs[:, 2, :], pa[:, 3, SH:2 * SH]))
            done(dve.tensor_tensor(acs[:, 1, :], acs[:, 0, :], pa[:, 3, 2 * SH:3 * SH], ALU.subtract),
                 "dve", "bank3")

        for t in range(T):
            done(act.activation(z[:, t, :], z[:, t, :], ACT.Silu), "act")

        xbc = cut(4 * 1024, 32, S)

        def conv(u, e):
            def evac(par):
                def tap(f, j):
                    return bc[:, bass.ds(u * 32 + (B_CW + (4 * e + f) * 4 + j), 1)]

                def dst(f, a=0, b=S):
                    return flat(xbc[:, bass.ds(u * 8 + (4 * e + f), 1), a:b])
                ps = [pg[:, par, f // 2, (f % 2) * S:(f % 2 + 1) * S] for f in range(4)]
                for f in range(4):
                    cb = bc[:, bass.ds(u * 8 + (B_CB + 4 * e + f), 1)]
                    m = done(dve.tensor_scalar(dst(f), ps[f], tap(f, 3), cb, ALU.mult, ALU.add), "dve")
                for j in (1, 2, 3):
                    wait("dve", m)
                    for f in range(4):
                        v = dve.scalar_tensor_tensor(dst(f, j), ps[f][:, 0:S - j], tap(f, 3 - j),
                                                     dst(f, j), ALU.mult, ALU.add)
                        if not (j == 3 and f == 3):
                            m = done(v, "dve")
                return None, v
            return evac

        def silu_tiles(u, e):
            wait("act", Mark("out_v", M.count["out_v"], list(M.stack)))
            t4 = xbc[:, bass.ds(u * 8 + 4 * e, 4), :]
            return act.activation(t4, t4, ACT.Silu)

        with M.loop("conv_x", 2) as u:
            for e in range(2):
                unit("col", conv(u, e), after=lambda: silu_tiles(u, e))

        xs = cut(17 * 1024, T, D)

        def turn_x(i):
            def step():
                b = i % 2
                if i == 0:
                    fence(("pe",), on=())
                    last("pe", "bank1")
                last("pe", f"bank{b}")
                for kk in range(2):
                    for t in range(T):
                        ins = pe.transpose(pa[:, b, (t * 2 + kk) * P:(t * 2 + kk + 1) * P],
                                           xbc[:, 2 * i + kk, t * P:(t + 1) * P], ident[:, :])
                wait("act", done(ins, "pe"))
                done(act.copy(xs[:, :, 2 * P * i:2 * P * (i + 1)],
                              pa[:, b, :].rearrange("p (t c) -> p t c", t=T)), "act", f"bank{b}")
            return step

        steps = {2 + 2 * i: [turn_x(i)] for i in range(8)}
        steps[19] = [dt_sums]
        last_unit = 3 * UC

        def tile_free(kp):
            M.wait_value("act", "used", M.count["used"])

        turn_y = transposer(lambda t: v2t[:, t, :], 0, banks=(2, 3), free=tile_free)
        for kp in range(UC):
            steps.setdefault(last_unit + kp, []).append(lambda kp=kp: turn_y(kp))
        host(steps)
        for u in (2, 3):
            for e in range(2):
                if (u, e) == (3, 1):
                    fence(("pool",), on=("pe", "act", "dve"))
                unit("col", conv(u, e), after=lambda: silu_tiles(u, e))
        host({})
        for b in range(4):
            last("pe", f"bank{b}")
        last("pool", "bank3")

        G = 12 * 1024
        b_s = cut(G, S)
        c_m = cut(G + 256, 3 * P)
        da_s = cut(G + 640, T, HPG)
        ac_s = cut(G + 656, 3, HPG)
        dec = cut(G + 1024, HPG, 3 * P)
        xdt = cut(G + 2560, T, HPG, HD)
        yb = cut(G + 3072, T, HPG * HD)
        ysq = cut(G + 3584, HPG * HD)
        mix = cut(4 * 1024, T, D)

        def scan_group(g, e):
            x_g = xs[:, :, bass.ds(g * (HPG * HD), HPG * HD)].rearrange("p t (r c) -> p t r c", r=HPG)
            box = {}

            def stage():
                last("pool", "scored")
                last("pool", "decayed")
                done(pool.tensor_copy(b_s, flat(xbc[:, bass.ds(g + 16, 1), :])), "pool")
                done(pool.tensor_copy(da_s, dA[:, :, bass.ds(g * HPG, HPG)]), "pool")
                box["staged"] = done(pool.tensor_copy(ac_s, acs[:, :, bass.ds(g * HPG, HPG)]), "pool")

            def score():
                wait("pe", box["staged"])
                last("pe", "decayed")
                c_g = flat(xbc[:, bass.ds(g + 24, 1), :])
                pe.matmul(pa[:, 0, 0:S], b_s[:, 0:P], c_g[:, 0:S], start=True, stop=True)
                m = done(pe.matmul(pa[:, 0, S:S + P], b_s[:, P:S], c_g[:, P:S], start=True, stop=True),
                         "pe")
                wait("dve", m)
                last("dve", "multiplied")
                done(dve.tensor_tensor(c_m[:, 0:P], pa[:, 0, 0:P], tri[:, :], ALU.mult), "dve")
                done(dve.tensor_copy(c_m[:, P:S], pa[:, 0, P:S]), "dve")
                done(dve.tensor_tensor(c_m[:, S:S + P], pa[:, 0, S:S + P], tri[:, :], ALU.mult), "dve")
                for r in range(HPG):
                    for t in range(T):
                        ins = pe.matmul(pa[:, 1 + r // 2, (r % 2) * S + t * P:(r % 2) * S + (t + 1) * P],
                                        da_s[:, t, r:r + 1].to_broadcast([P, P]), tri[:, :],
                                        start=True, stop=True)
                m = done(ins, "pe", "scored")
                wait("dve", m)
                last("dve", "applied")
                for r in range(HPG):
                    for blk, t in ((0, 0), (1, 1), (2, 1)):
                        m = done(dve.tensor_scalar(
                            dec[:, r, blk * P:(blk + 1) * P],
                            pa[:, 1 + r // 2, (r % 2) * S + t * P:(r % 2) * S + (t + 1) * P],
                            ac_s[:, blk, r:r + 1], 0.0, ALU.subtract, ALU.min), "dve", "decayed")
                wait("act", m)
                m = done(act.activation(dec, dec, ACT.Exp), "act")
                wait("dve", m)
                box["m"] = done(dve.tensor_tensor(dec, dec, c_m.unsqueeze(1).to_broadcast([P, HPG, 3 * P]),
                                                  ALU.mult), "dve", "multiplied")
                last("pool", "applied")
                last("pool", "gated")
                for t in range(T):
                    dt_g = dt[:, t, bass.ds(g * HPG, HPG)].unsqueeze(2).to_broadcast([P, HPG, HD])
                    done(pool.tensor_tensor(xdt[:, t, :, :], x_g[:, t, :, :], dt_g, ALU.mult), "pool")
                for t in range(T):
                    ds_g = bc[:, bass.ds(g * HPG + B_DS, HPG)].unsqueeze(2).to_broadcast([P, HPG, HD])
                    yt = yb[:, t, :].rearrange("p (r c) -> p r c", r=HPG)
                    box["x"] = done(pool.tensor_tensor(yt, x_g[:, t, :, :], ds_g, ALU.mult), "pool")

            def apply():
                wait("pe", box["m"])
                wait("pe", box["x"])
                last("pe", "summed")
                for r in range(HPG):
                    o = [pa[:, 3, t * S + r * HD:t * S + (r + 1) * HD] for t in range(T)]
                    pe.matmul(o[0], dec[:, r, 0:P], xdt[:, 0, r, :], start=True, stop=True)
                    pe.matmul(o[1], dec[:, r, P:2 * P], xdt[:, 0, r, :], start=True, stop=False)
                    ins = pe.matmul(o[1], dec[:, r, 2 * P:3 * P], xdt[:, 1, r, :], start=False, stop=True)
                m = done(ins, "pe", "applied")
                wait("dve", m)
                m = done(dve.tensor_tensor(yb, yb, pa[:, 3, :].rearrange("p (t c) -> p t c", t=T),
                                           ALU.add), "dve", "summed")
                wait("dve", m)
                zg = z[:, :, bass.ds(g * (HPG * HD), HPG * HD)]
                m = done(dve.tensor_tensor(yb, yb, zg, ALU.mult), "dve")
                wait("act", m)
                for t in range(T):
                    last("act", "junk")
                    m = done(act.activation(ysq, yb[:, t, :], ACT.Square, accum_out=stat[:, 28 + t:29 + t]),
                             "act", "junk")
                wait("dve", m)
                m = rstd(stat[:, 28:30], stat[:, 30:32], HPG * HD)
                wait("dve", m)
                for t in range(T):
                    m = done(dve.tensor_scalar(zg[:, t, :], yb[:, t, :], stat[:, 30 + t:31 + t], None,
                                               ALU.mult), "dve", "gated")
                keep(f"gated{e}", m)

            return stage, score, apply

        def put(dst, u, e, add):
            def evac(par):
                d = [dst[:, t, bass.ds(u * (2 * UNIT) + e * UNIT, UNIT)] for t in range(T)]
                if not add:
                    return act.copy(d[0], pg[:, par, 0, :]), dve.tensor_copy(d[1], pg[:, par, 1, :])
                done(dve.tensor_tensor(d[0], d[0], pg[:, par, 0, :], ALU.add), "dve")
                return act.nop(), dve.tensor_tensor(d[1], d[1], pg[:, par, 1, :], ALU.add)
            return evac

        with M.loop("out_att", 2) as u:
            g4 = [scan_group(u * 4 + e, e) for e in range(4)]
            host({-1: [g4[0][0]], 1: [g4[0][1], g4[1][0]], 5: [g4[0][2], g4[1][1], g4[2][0]],
                  8: [g4[1][2]], 9: [g4[2][1], g4[3][0]], 12: [g4[2][2], g4[3][1]], 15: [g4[3][2]]})
            for e in range(2):
                unit("row", put(mix, u, e, False))
        host({})
        fence(("pool",))
        load_row(1)
        turn_z = transposer(lambda t: z[:, t, :], 0, bc[:, B_SSM:B_SSM + KT], banks=(0, 1, 2))
        last("pe", "decayed")

        def turn_group(kp):
            last("pe", f"gated{max(kp - 4, 0)}")
            return turn_z(kp)

        host(feed(turn_group, UC))
        tmp3 = cut(12 * 1024, T, D)

        def gained(i):
            c = slice(i * UNIT, (i + 1) * UNIT)
            square_part([mix[:, t, c] for t in range(T)], [tmp3[:, t, c] for t in range(T)], i)
            wait("dve", Mark("out_v", M.count["out_v"], []))
            for t in range(T):
                done(dve.tensor_tensor(tmp2[:, t, c], mix[:, t, c], rows[:, c], ALU.mult), "dve")

        M.wait_value("dve", "ld_layer", here("ld_layer"))
        for i in range(D // UNIT):
            unit("row", put(mix, i // 2, i % 2, True), eager=(i == 3))
            gained(i)
        host({})
        m = rstd(sum_parts(), stat[:, 42:44], D)
        wait("dve", m)
        scaled_halves(lambda t, c: dve.scalar_tensor_tensor(xres[:, t, c], tmp2[:, t, c],
                                                            stat[:, 42 + t:43 + t], xres[:, t, c],
                                                            ALU.mult, ALU.add), st)
        split_next()

        steps = feed(transposer(lambda t: xres[:, t, :], 0, bc[:, B_MLP:B_MLP + KT],
                                lambda t: diags[:, t, :]), UC)

        def clear_mix():
            done(dve.memset(mix, 0.0), "dve")
            load_row(2)
        steps[UC - 2].append(clear_mix)
        host(steps)
        h_t = cut(0, 2, 2, UNIT)

        def up(b):
            def evac(par):
                for i in range(2):
                    r = h_t[:, b, i, :]
                    last("act", f"hidden{b}")
                    m = done(act.activation(r, pg[:, par, i, :], ACT.Relu), "act")
                    wait("act", m)
                    m = done(act.activation(r, r, ACT.Square), "act")
                    wait("act", m)
                    r3 = r.rearrange("p (f s) -> p f s", f=2)
                    hh = b_hi[:, 4 * b + 2 * i:4 * b + 2 * i + 2, :]
                    hl = b_lo[:, 4 * b + 2 * i:4 * b + 2 * i + 2, :]
                    a = act.copy(hh, r3)
                    m = done(a, "act")
                    wait("dve", m)
                    m = done(dve.tensor_tensor(hl, r3, hh.bitcast(F32), ALU.subtract),
                             "hidden" if i else "dve")
                keep(f"hidden{b}", m)
                return act.nop(), dve.nop()
            unit("col", evac)

        def down(b, name, later=0):
            M.wait_value("pe", "hidden", here("hidden") - later)
            with M.loop(name, 2) as u:
                for e in range(2):
                    unit("row", put(mix, u, e, True), chunks=GT // KC, hi=b_hi[:, 4 * b:4 * b + 4, :],
                         lo=b_lo[:, 4 * b:4 * b + 4, :])

        up(0)
        host({})
        with M.loop("groups", GROUPS // 2 - 1):
            for b in range(2):
                up(1 - b)
                down(b, f"down{b}", 1)
        up(1)
        down(0, "down_last0", 1)
        down(1, "down_last1")
        fence()

        M.wait_value("dve", "ld_layer", here("ld_layer"))
        for t in range(T):
            done(dve.tensor_tensor(tmp2[:, t, :], mix[:, t, :], rows, ALU.mult), "dve")
            m = done(act.activation(tmp3[:, t, :], mix[:, t, :], ACT.Square, accum_out=stat[:, t:t + 1]),
                     "act")
        wait("dve", m)
        wait("dve", rstd(stat[:, 0:2], stat[:, 2:4], D))
        for t in range(T):
            m = done(dve.scalar_tensor_tensor(xres[:, t, :], tmp2[:, t, :], stat[:, 2 + t:3 + t],
                                              xres[:, t, :], ALU.mult, ALU.add), "dve")
            wait("act", m)
            act.dma_start(out[t * P:(t + 1) * P, :], xres[:, t, :]).then_inc(stored, 16)
        act.wait_ge(stored, T * 16)
    return M.plan


def _rope_consts(np):
    pos = np.arange(S, dtype=np.float32)
    inv = (1.0 / (10000.0 ** (np.arange(0, ROPE, 2, dtype=np.float32) / ROPE))).astype(np.float32)
    ang = (pos[:, None] * inv[None, :]).astype(np.float32)
    ang = np.concatenate([ang, ang], axis=-1)
    sin = np.sin(ang)
    sin[:, :ROPE // 2] *= -1
    t = np.stack([np.cos(ang), sin], axis=1).astype(np.float32)
    return np.ascontiguousarray(t.reshape(T, P, 2, ROPE).transpose(1, 0, 2, 3))


def _bucket_const(np):
    dist = 255 - np.arange(512)
    n = np.maximum(dist, 0)
    nf = np.maximum(n, 1).astype(np.float32)
    large = 16 + (np.log(nf / np.float32(16)) / np.float32(math.log(128 / 16)) * 16).astype(np.int32)
    b = np.where(n < 16, n, np.minimum(large, 31))
    c = np.zeros((33, 512), np.float32)
    c[b, np.arange(512)] = 8.0
    c[:32, dist < 0] = 0.0
    c[32, dist < 0] = NEG
    return c


def _mask_const(np):
    dist = 128 + np.arange(P)[:, None] - np.arange(S)[None, :]
    causal = np.where(dist >= 0, 0.0, NEG)
    n = sum(((dist >= 0) & (dist % d == 0) & (dist <= w)).astype(np.int64)
            for w, d in ((128, 1), (512, 4), (2048, 16)))
    dil = np.where(n > 0, np.log(np.maximum(n, 1)) * AD ** 0.5, NEG)
    return np.stack([causal, dil], axis=1).astype(np.float32)


def kernel(**inputs):
    import numpy as np
    import concourse.bacc as bacc
    from concourse.bass_utils import run_bass_kernel_spmd as run

    g = {k: np.ascontiguousarray(v) for k, v in inputs.items()}

    def cols(v):
        return v.reshape(-1, P).T

    def rows(v):
        return np.broadcast_to(v.reshape(1, -1), (P, v.size))

    layer_c = []
    for l in (*range(DEPTH), DEPTH - 1):
        li = 0.8 - 0.6 * math.exp(-0.3 * l)
        layer_c.append(np.concatenate([
            cols(g["norm_g"][l]), cols(g["mla_q_norm_g"][l]), cols(g["mla_kv_norm_g"][l]),
            rows(g["diff_subln_g"][l]), rows(g["diff_lambda"][l]),
            rows(np.array([li, 1.0 - li], np.float32))], axis=1))
    conv = g["conv_w_2"][0].reshape(4, 32, P).transpose(2, 1, 0).reshape(P, 128)
    block_c = np.concatenate([
        cols(g["norm_mix_pre_2"][0]), cols(g["norm_mlp_pre_2"][0]), cols(g["ssm_norm_w_2"][0]), conv,
        cols(g["conv_b_2"][0]), rows(g["dt_bias_2"][0]), rows(g["a_log_2"][0]), rows(g["d_skip_2"][0])],
        axis=1)
    arrays = {
        "x": g["x"][0], "layer_c": np.concatenate(layer_c, axis=0),
        "w_in": g["w_in"].reshape(DEPTH * D, W_IN), "w_uq": g["w_uq"].reshape(DEPTH * QR, -1),
        "w_ukv": g["w_ukv"].reshape(DEPTH * KVR, -1), "w_out": g["w_out"].reshape(DEPTH * D, D),
        "rel_table": g["rel_bias_table"], "block_c": block_c,
        "rows_c": np.concatenate([rows(g["final_norm_g"]), rows(g["norm_mix_post_2"][0]),
                                  rows(g["norm_mlp_post_2"][0])], axis=0),
        "w_in_2": g["w_in_2"][0], "w_out_2": g["w_out_2"][0], "w_up": g["w_up_2"][0],
        "w_down": g["w_down_2"][0], "c_ident": np.eye(P, dtype=np.float32),
        "c_tri": np.triu(np.ones((P, P), np.float32)), "c_mask": _mask_const(np),
        "c_bucket": _bucket_const(np), "c_rope": _rope_consts(np),
    }
    arrays = {k: np.ascontiguousarray(v) for k, v in arrays.items()}
    plan = {}
    for real in (False, True):
        plan["real"] = real
        nc = bacc.Bacc("TRN2", target_bir_lowering=False, num_devices=1)
        args = {k: nc.dram_tensor(f"in_{k}", v.shape, mybir.dt.from_np(v.dtype),
                                  kind="ExternalInput").ap() for k, v in arrays.items()}
        out = nc.dram_tensor("out_x", (S, D), F32, kind="ExternalOutput").ap()
        build(nc, plan, out=out, **args)
    r = run(nc, [{f"in_{k}": v for k, v in arrays.items()}], core_ids=[0])
    return r.results[0]["out_x"].reshape(1, S, D)
```
